# Optimizing a Trainium2 kernel written in Bass

```python
import math
import jax, jax.numpy as jnp
from jax import lax
import numpy as np

D_MODEL = 1024
BATCH = 1
SEQ = 1024
DEPTH = 2

GLA_HEADS = 4
GLA_DK = 32
GLA_DV = 64
GLA_RANK = 16
GLA_GATE_TEMP = 16.0
DIFF_HEADS = 4
DIFF_HD = 64
DIFF_DV = 2 * DIFF_HD
HGRN_HEADS = 4
HGRN_DK = 64
HGRN_DV = 64
CHUNK = 16
Q_BLOCK = 128
ROPE_THETA = 10000.0
EPS = 1e-6
F_FLOOR = 1e-30

GLA_W = GLA_HEADS * GLA_DV
DIFF_W = DIFF_HEADS * DIFF_DV
HGRN_W = HGRN_HEADS * HGRN_DV
MIX_W = GLA_W + DIFF_W + HGRN_W

IN_SIZES = (
    GLA_HEADS * GLA_DK, GLA_HEADS * GLA_DK, GLA_W, GLA_W, GLA_RANK, GLA_RANK,
    DIFF_HEADS * 2 * DIFF_HD, DIFF_HEADS * 2 * DIFF_HD, DIFF_W, DIFF_W,
    HGRN_HEADS * HGRN_DK, HGRN_HEADS * HGRN_DK, HGRN_HEADS * HGRN_DK, HGRN_W, HGRN_W,
)
IN_W = sum(IN_SIZES)


def _offsets():
    offs, run = [], 0
    for s in IN_SIZES[:-1]:
        run += s
        offs.append(run)
    return offs

def rms_norm(x, w):
    xf = x.astype(jnp.float32)
    xf = xf * lax.rsqrt(jnp.mean(xf * xf, axis=-1, keepdims=True) + EPS)
    return xf.astype(x.dtype) * w

def split_heads(t, n_heads):
    b, l, _ = t.shape
    return t.reshape(b, l, n_heads, -1).transpose(0, 2, 1, 3)

def merge_heads(t):
    b, h, l, d = t.shape
    return t.transpose(0, 2, 1, 3).reshape(b, l, h * d)

def rope(x, pos):
    d = x.shape[-1]
    inv_freq = ROPE_THETA ** (-jnp.arange(0, d, 2, dtype=jnp.float32) / d)
    ang = pos.astype(jnp.float32)[:, None] * inv_freq[None, :]
    cos, sin = jnp.cos(ang).astype(x.dtype), jnp.sin(ang).astype(x.dtype)
    x1, x2 = x[..., : d // 2], x[..., d // 2:]
    return jnp.concatenate([x1 * cos - x2 * sin, x2 * cos + x1 * sin], axis=-1)

def chunked_gated_scan(q, k, v, log_g):
    b_, h_, l_, dk = q.shape
    dv = v.shape[-1]
    n = l_ // CHUNK
    r = lambda t: t.reshape(b_, h_, n, CHUNK, t.shape[-1])
    q, k, v, lg = r(q), r(k), r(v), r(log_g)
    bcum = jnp.cumsum(lg.astype(jnp.float32), axis=3)
    mask = jnp.tril(jnp.ones((CHUNK, CHUNK), dtype=bool))[:, :, None]
    diff = bcum[:, :, :, :, None, :] - bcum[:, :, :, None, :, :]
    decay = jnp.where(mask, jnp.exp(jnp.where(mask, diff, 0.0)), 0.0)
    attn = jnp.einsum('bhntk,bhnsk,bhntsk->bhnts', q, k, decay.astype(q.dtype))
    o_intra = jnp.einsum('bhnts,bhnsv->bhntv', attn, v)
    b_last = bcum[:, :, :, -1:, :]
    u = jnp.einsum('bhnsk,bhnsv->bhnkv', k * jnp.exp(b_last - bcum).astype(k.dtype), v)
    g_chunk = jnp.exp(b_last[:, :, :, 0, :]).astype(u.dtype)

    def step(state, inp):
        g_n, u_n = inp
        return g_n[..., None] * state + u_n, state

    s0 = jnp.zeros((b_, h_, dk, dv), u.dtype)
    _, s_prev = lax.scan(step, s0, (jnp.moveaxis(g_chunk, 2, 0), jnp.moveaxis(u, 2, 0)))
    s_prev = jnp.moveaxis(s_prev, 0, 2)
    o_inter = jnp.einsum('bhntk,bhnkv->bhntv', q * jnp.exp(bcum).astype(q.dtype), s_prev)
    return (o_intra + o_inter).reshape(b_, h_, l_, dv).astype(v.dtype)

def bidir_scan(q, k_f, k_b, v, lg_f, lg_b):
    flip = lambda t: jnp.flip(t, axis=2)
    o_f = chunked_gated_scan(q, k_f, v, lg_f)
    o_b = flip(chunked_gated_scan(flip(q), flip(k_b), flip(v), flip(lg_b)))
    return o_f + o_b

def gla_branch(q, k, v, g, a_f, a_b, wa2_f, ba_f, wa2_b, ba_b, norm_w):
    q = split_heads(q, GLA_HEADS) * (GLA_DK ** -0.5)
    k = split_heads(k, GLA_HEADS)
    v = split_heads(v, GLA_HEADS)
    lg_f = split_heads(jax.nn.log_sigmoid((a_f @ wa2_f + ba_f).astype(jnp.float32)) / GLA_GATE_TEMP, GLA_HEADS)
    lg_b = split_heads(jax.nn.log_sigmoid((a_b @ wa2_b + ba_b).astype(jnp.float32)) / GLA_GATE_TEMP, GLA_HEADS)
    o = bidir_scan(q, k, k, v, lg_f, lg_b)
    o = rms_norm(o, norm_w)
    return merge_heads(o) * jax.nn.silu(g)

def diff_branch(q, k, v, g, lq1, lk1, lq2, lk2, norm_w, lambda_init, pos):
    b_, l_, _ = q.shape
    q = q.reshape(b_, l_, DIFF_HEADS, 2, DIFF_HD).transpose(3, 0, 2, 1, 4)
    k = k.reshape(b_, l_, DIFF_HEADS, 2, DIFF_HD).transpose(3, 0, 2, 1, 4)
    q = rope(q, pos) * (DIFF_HD ** -0.5)
    k = rope(k, pos)
    v = split_heads(v, DIFF_HEADS)
    lam = (jnp.exp(jnp.sum(lq1 * lk1).astype(jnp.float32))
           - jnp.exp(jnp.sum(lq2 * lk2).astype(jnp.float32)) + lambda_init)
    nb = l_ // Q_BLOCK
    qb = jnp.moveaxis(q.reshape(2, b_, DIFF_HEADS, nb, Q_BLOCK, DIFF_HD), 3, 0)

    def block(qblk):
        s = jnp.einsum('cbhqd,cbhkd->cbhqk', qblk, k).astype(jnp.float32)
        p = jax.nn.softmax(s, axis=-1)
        w = p[0] - lam * p[1]
        return jnp.einsum('bhqk,bhkv->bhqv', w.astype(v.dtype), v)

    o = lax.map(block, qb)
    o = jnp.moveaxis(o, 0, 2).reshape(b_, DIFF_HEADS, l_, DIFF_DV)
    o = rms_norm(o, norm_w) * (1.0 - lambda_init)
    return merge_heads(o) * jax.nn.silu(g)

def hgrn_branch(q, z_f, z_b, i, g, lb, norm_w):
    lb32 = lb.astype(jnp.float32)

    def gates(z):
        z32 = z.astype(jnp.float32)
        one_minus_f = (1.0 - lb32) * jax.nn.sigmoid(-z32)
        f = lb32 + (1.0 - lb32) * jax.nn.sigmoid(z32)
        log_f = jnp.log(jnp.maximum(f, F_FLOOR))
        return split_heads(log_f, HGRN_HEADS), split_heads(one_minus_f.astype(z.dtype), HGRN_HEADS)

    lg_f, k_f = gates(z_f)
    lg_b, k_b = gates(z_b)
    o = bidir_scan(split_heads(q, HGRN_HEADS), k_f, k_b, split_heads(i, HGRN_HEADS), lg_f, lg_b)
    o = rms_norm(o, norm_w)
    return merge_heads(o) * jax.nn.silu(g)

def first_inputs(seed: int = 0) -> dict:
    key = jax.random.key(seed)
    ks = jax.random.split(key, 20)
    nrm = lambda k, shape, s: jax.random.normal(k, shape, jnp.float32) * s
    return {
        "x": nrm(ks[0], (BATCH, SEQ, D_MODEL), 1.0),
        "norm_pre": 1.0 + nrm(ks[1], (DEPTH, D_MODEL), 0.05),
        "norm_post": 1.0 + nrm(ks[2], (DEPTH, D_MODEL), 0.05),
        "w_in": nrm(ks[3], (DEPTH, D_MODEL, IN_W), D_MODEL ** -0.5),
        "w_out": nrm(ks[4], (DEPTH, MIX_W, D_MODEL), MIX_W ** -0.5),
        "gla_wa2_fwd": nrm(ks[5], (DEPTH, GLA_RANK, GLA_HEADS * GLA_DK), GLA_RANK ** -0.5),
        "gla_ba_fwd": nrm(ks[6], (DEPTH, GLA_HEADS * GLA_DK), 0.1),
        "gla_wa2_bwd": nrm(ks[7], (DEPTH, GLA_RANK, GLA_HEADS * GLA_DK), GLA_RANK ** -0.5),
        "gla_ba_bwd": nrm(ks[8], (DEPTH, GLA_HEADS * GLA_DK), 0.1),
        "gla_norm": 1.0 + nrm(ks[9], (DEPTH, GLA_DV), 0.05),
        "diff_lq1": nrm(ks[10], (DEPTH, DIFF_HD), 0.1),
        "diff_lk1": nrm(ks[11], (DEPTH, DIFF_HD), 0.1),
        "diff_lq2": nrm(ks[12], (DEPTH, DIFF_HD), 0.1),
        "diff_lk2": nrm(ks[13], (DEPTH, DIFF_HD), 0.1),
        "diff_norm": 1.0 + nrm(ks[14], (DEPTH, DIFF_DV), 0.05),
        "hgrn_lb_logits": nrm(ks[15], (DEPTH, HGRN_HEADS * HGRN_DK), 0.1),
        "hgrn_norm": 1.0 + nrm(ks[16], (DEPTH, HGRN_DV), 0.05),
    }

def first_block(x, norm_pre, norm_post, w_in, w_out, gla_wa2_fwd, gla_ba_fwd, gla_wa2_bwd, gla_ba_bwd,
              gla_norm, diff_lq1, diff_lk1, diff_lq2, diff_lk2, diff_norm, hgrn_lb_logits, hgrn_norm):
    pos = jnp.arange(x.shape[1], dtype=jnp.int32)
    p_lb = jax.nn.softmax(hgrn_lb_logits.astype(jnp.float32), axis=0)
    lb_all = jnp.cumsum(p_lb, axis=0) - p_lb[0:1]
    offs = _offsets()
    for layer in range(DEPTH):
        lambda_init = 0.8 - 0.6 * math.exp(-0.3 * layer)
        h = rms_norm(x, norm_pre[layer])
        proj = h @ w_in[layer]
        (gq, gk, gv, gg, gaf, gab, dq, dk, dv, dg, hq, hzf, hzb, hi, hg) = jnp.split(proj, offs, axis=-1)
        y_a = gla_branch(gq, gk, gv, gg, gaf, gab, gla_wa2_fwd[layer], gla_ba_fwd[layer],
                         gla_wa2_bwd[layer], gla_ba_bwd[layer], gla_norm[layer])
        y_b = diff_branch(dq, dk, dv, dg, diff_lq1[layer], diff_lk1[layer], diff_lq2[layer], diff_lk2[layer],
                          diff_norm[layer], lambda_init, pos)
        y_c = hgrn_branch(hq, hzf, hzb, hi, hg, lb_all[layer], hgrn_norm[layer])
        y = jnp.concatenate([y_a, y_b, y_c], axis=-1) @ w_out[layer]
        x = x + rms_norm(y, norm_post[layer])
    return x


DEPTH_2 = 1

CHUNK_2 = 64
PLE_DIM = 256
D_MIX = D_MODEL
D_CONV = D_MIX // 2
D_LRU = D_MIX - D_CONV
CONV_HEADS = 8
LRU_HEADS = 8
LRU_HEAD_DIM = D_LRU // LRU_HEADS
CONV_WIDTH = 31
LRU_CONV_WIDTH = 4
LRU_C = 8.0
N_GROUPS = 4
EXPERTS_PER_GROUP = 8
N_EXPERTS = N_GROUPS * EXPERTS_PER_GROUP
TOP_K = 2
D_EXPERT = D_MODEL // 2
ROUTE_BLOCK = 128


def _rmsnorm(x, g):
    xf = x.astype(jnp.float32)
    y = xf * lax.rsqrt(jnp.mean(xf * xf, axis=-1, keepdims=True) + EPS)
    return (y * g.astype(jnp.float32)).astype(x.dtype)

def _layernorm(x, g, b):
    xf = x.astype(jnp.float32)
    mu = jnp.mean(xf, axis=-1, keepdims=True)
    var = jnp.mean(jnp.square(xf - mu), axis=-1, keepdims=True)
    y = (xf - mu) * lax.rsqrt(var + EPS)
    return (y * g.astype(jnp.float32) + b.astype(jnp.float32)).astype(x.dtype)

def _causal_depthwise_conv(x, w, b):
    width = w.shape[0]
    y = lax.conv_general_dilated(
        x, w[:, None, :], window_strides=(1,), padding=((width - 1, 0),),
        dimension_numbers=('NWC', 'WIO', 'NWC'), feature_group_count=x.shape[-1])
    return y + b

def _conformer_conv(v, g, w_dw, b_dw, ln_g, ln_b):
    u = v * jax.nn.sigmoid(g)
    u = _causal_depthwise_conv(u, w_dw, b_dw)
    return jax.nn.silu(_layernorm(u, ln_g, ln_b))

def _rglru(x, w_r, b_r, w_i, b_i, lam):
    B, S, C = x.shape
    xh = x.reshape(B, S, LRU_HEADS, LRU_HEAD_DIM)
    r = jax.nn.sigmoid(jnp.einsum('bshi,hij->bshj', xh, w_r).reshape(B, S, C) + b_r)
    i_g = jax.nn.sigmoid(jnp.einsum('bshi,hij->bshj', xh, w_i).reshape(B, S, C) + b_i)
    log_a = -LRU_C * r.astype(jnp.float32) * jax.nn.softplus(-lam.astype(jnp.float32))
    a = jnp.exp(log_a)
    u = jnp.sqrt(-jnp.expm1(2.0 * log_a)) * (i_g * x).astype(jnp.float32)
    nc = S // CHUNK_2
    a_c = a.reshape(B, nc, CHUNK_2, C)
    u_c = u.reshape(B, nc, CHUNK_2, C)

    def combine(left, right):
        a_l, h_l = left
        a_r, h_r = right
        return a_l * a_r, a_r * h_l + h_r

    a_cum, h_loc = lax.associative_scan(combine, (a_c, u_c), axis=2)

    def step(h_prev, xs):
        ac, hl = xs
        h = hl + ac * h_prev[:, None, :]
        return h[:, -1, :], h

    _, h = lax.scan(step, jnp.zeros((B, C), jnp.float32),
                    (jnp.moveaxis(a_cum, 1, 0), jnp.moveaxis(h_loc, 1, 0)))
    return jnp.moveaxis(h, 0, 1).reshape(B, S, C).astype(x.dtype)

def _hier_route(h, w_group, b_group, w_expert, b_expert):
    T = h.shape[0]
    g_logits = (h @ w_group).astype(jnp.float32) + b_group.astype(jnp.float32)
    g_prob, g_idx = lax.top_k(jax.nn.softmax(g_logits, axis=-1), 1)
    e_logits = ((h @ w_expert).astype(jnp.float32) + b_expert.astype(jnp.float32))
    e_logits = e_logits.reshape(T, N_GROUPS, EXPERTS_PER_GROUP)
    e_sel = jnp.take_along_axis(e_logits, g_idx[:, :, None], axis=1)[:, 0]
    e_prob, e_loc = lax.top_k(jax.nn.softmax(e_sel, axis=-1), TOP_K)
    e_prob = e_prob / jnp.sum(e_prob, axis=-1, keepdims=True)
    gate = g_prob * e_prob
    expert_id = g_idx * EXPERTS_PER_GROUP + e_loc
    return expert_id, gate

def _routed_experts(h, expert_id, gate, w1, w3, w2):
    T, D = h.shape
    A = T * TOP_K
    flat_e = expert_id.reshape(A)
    flat_tok = jnp.repeat(jnp.arange(T, dtype=jnp.int32), TOP_K, total_repeat_length=A)
    flat_gate = gate.reshape(A)
    order = jnp.argsort(flat_e)
    se, st, sg = flat_e[order], flat_tok[order], flat_gate[order]
    counts = jnp.zeros((N_EXPERTS,), jnp.int32).at[flat_e].add(1)
    padded = (counts + ROUTE_BLOCK - 1) // ROUTE_BLOCK * ROUTE_BLOCK
    start = jnp.cumsum(counts) - counts
    pad_end = jnp.cumsum(padded)
    pad_start = pad_end - padded
    dest = pad_start[se] + (jnp.arange(A, dtype=jnp.int32) - start[se])
    n_blocks = -(-A // ROUTE_BLOCK) + N_EXPERTS
    P = n_blocks * ROUTE_BLOCK
    buf_tok = jnp.zeros((P,), jnp.int32).at[dest].set(st)
    buf_gate = jnp.zeros((P,), jnp.float32).at[dest].set(sg)
    block_start = jnp.arange(n_blocks, dtype=jnp.int32) * ROUTE_BLOCK
    block_e = jnp.minimum(jnp.searchsorted(pad_end, block_start, side='right'), N_EXPERTS - 1)

    def expert_block(args):
        tok, e, g = args
        xb = h[tok]
        y = (jax.nn.silu(xb @ w1[e]) * (xb @ w3[e])) @ w2[e]
        return (y * g[:, None]).astype(h.dtype)

    y = lax.map(expert_block, (buf_tok.reshape(n_blocks, ROUTE_BLOCK), block_e,
                               buf_gate.reshape(n_blocks, ROUTE_BLOCK)))
    return jnp.zeros_like(h).at[buf_tok].add(y.reshape(P, D))

def second_inputs(seed: int = 0) -> dict:
    key = jax.random.key(seed)
    ks = jax.random.split(key, 32)
    f32 = jnp.float32
    L = DEPTH_2

    def nrm(k, shape, scale):
        return jax.random.normal(k, shape, f32) * scale

    def gain(k, shape):
        return 1.0 + 0.05 * jax.random.normal(k, shape, f32)

    u = jax.random.uniform(ks[14], (L, D_LRU), f32, 0.9, 0.999)
    s = u ** (1.0 / LRU_C)
    lru_lambda = jnp.log(s) - jnp.log1p(-s)
    return {
        'x': nrm(ks[0], (BATCH, SEQ, D_MODEL), 1.0),
        'p': nrm(ks[1], (L, BATCH, SEQ, PLE_DIM), 1.0),
        'g_mix': gain(ks[2], (L, D_MODEL)),
        'w_in': nrm(ks[3], (L, D_MODEL, 2 * D_CONV + 2 * D_LRU), D_MODEL ** -0.5),
        'conv_dw_w': nrm(ks[4], (L, CONV_WIDTH, D_CONV), CONV_WIDTH ** -0.5),
        'conv_dw_b': nrm(ks[5], (L, D_CONV), 0.02),
        'conv_ln_g': gain(ks[6], (L, D_CONV)),
        'conv_ln_b': nrm(ks[7], (L, D_CONV), 0.02),
        'lru_conv_w': nrm(ks[8], (L, LRU_CONV_WIDTH, D_LRU), LRU_CONV_WIDTH ** -0.5),
        'lru_conv_b': nrm(ks[9], (L, D_LRU), 0.02),
        'lru_w_r': nrm(ks[10], (L, LRU_HEADS, LRU_HEAD_DIM, LRU_HEAD_DIM), LRU_HEAD_DIM ** -0.5),
        'lru_b_r': nrm(ks[11], (L, D_LRU), 0.02),
        'lru_w_i': nrm(ks[12], (L, LRU_HEADS, LRU_HEAD_DIM, LRU_HEAD_DIM), LRU_HEAD_DIM ** -0.5),
        'lru_b_i': nrm(ks[13], (L, D_LRU), 0.02),
        'lru_lambda': lru_lambda,
        'w_out': nrm(ks[15], (L, D_MIX, D_MODEL), D_MIX ** -0.5),
        'g_ffn': gain(ks[16], (L, D_MODEL)),
        'w_group': nrm(ks[17], (L, D_MODEL, N_GROUPS), D_MODEL ** -0.5),
        'b_group': nrm(ks[18], (L, N_GROUPS), 0.01),
        'w_expert': nrm(ks[19], (L, D_MODEL, N_EXPERTS), D_MODEL ** -0.5),
        'b_expert': nrm(ks[20], (L, N_EXPERTS), 0.01),
        'w1': nrm(ks[21], (L, N_EXPERTS, D_MODEL, D_EXPERT), D_MODEL ** -0.5),
        'w3': nrm(ks[22], (L, N_EXPERTS, D_MODEL, D_EXPERT), D_MODEL ** -0.5),
        'w2': nrm(ks[23], (L, N_EXPERTS, D_EXPERT, D_MODEL), D_EXPERT ** -0.5),
        'g_ple': gain(ks[24], (L, D_MODEL)),
        'w_ple': nrm(ks[25], (L, PLE_DIM, D_MODEL), PLE_DIM ** -0.5),
        'g_ple_proj': gain(ks[26], (L, D_MODEL)),
        'w_ple_gate': nrm(ks[27], (L, D_MODEL, D_MODEL), D_MODEL ** -0.5),
        'g_final': gain(ks[28], (D_MODEL,)),
    }

def second_block(x, p, g_mix, w_in, conv_dw_w, conv_dw_b, conv_ln_g, conv_ln_b,
              lru_conv_w, lru_conv_b, lru_w_r, lru_b_r, lru_w_i, lru_b_i, lru_lambda,
              w_out, g_ffn, w_group, b_group, w_expert, b_expert, w1, w3, w2,
              g_ple, w_ple, g_ple_proj, w_ple_gate, g_final):
    B, S, D = x.shape
    for i in range(DEPTH_2):
        h = _rmsnorm(x, g_mix[i])
        z = h @ w_in[i]
        conv_v, conv_g, lru_x, lru_g = jnp.split(
            z, [D_CONV, 2 * D_CONV, 2 * D_CONV + D_LRU], axis=-1)
        y_conv = _conformer_conv(conv_v, conv_g, conv_dw_w[i], conv_dw_b[i],
                                 conv_ln_g[i], conv_ln_b[i])
        xr = _causal_depthwise_conv(lru_x, lru_conv_w[i], lru_conv_b[i])
        y_lru = _rglru(xr, lru_w_r[i], lru_b_r[i], lru_w_i[i], lru_b_i[i],
                       lru_lambda[i]) * jax.nn.gelu(lru_g)
        x = x + jnp.concatenate([y_conv, y_lru], axis=-1) @ w_out[i]
        hf = _rmsnorm(x, g_ffn[i]).reshape(B * S, D)
        eid, gate = _hier_route(hf, w_group[i], b_group[i], w_expert[i], b_expert[i])
        x = x + _routed_experts(hf, eid, gate, w1[i], w3[i], w2[i]).reshape(B, S, D)
        e = _rmsnorm(p[i] @ w_ple[i], g_ple_proj[i])
        pg = jax.nn.sigmoid(_rmsnorm(x, g_ple[i]) @ w_ple_gate[i])
        x = x + pg * e
    return _rmsnorm(x, g_final)


def setup_inputs(seed=0):
    out = dict(first_inputs(seed))
    for name, value in second_inputs(seed + 1).items():
        if name != "x":
            out[name + "_2"] = value
    return out


def reference(
    x, norm_pre, norm_post, w_in, w_out, gla_wa2_fwd, gla_ba_fwd, gla_wa2_bwd, gla_ba_bwd,
    gla_norm, diff_lq1, diff_lk1, diff_lq2, diff_lk2, diff_norm, hgrn_lb_logits, hgrn_norm, p_2,
    g_mix_2, w_in_2, conv_dw_w_2, conv_dw_b_2, conv_ln_g_2, conv_ln_b_2, lru_conv_w_2,
    lru_conv_b_2, lru_w_r_2, lru_b_r_2, lru_w_i_2, lru_b_i_2, lru_lambda_2, w_out_2, g_ffn_2,
    w_group_2, b_group_2, w_expert_2, b_expert_2, w1_2, w3_2, w2_2, g_ple_2, w_ple_2,
    g_ple_proj_2, w_ple_gate_2, g_final_2,
):
    x = first_block(
        x, norm_pre, norm_post, w_in, w_out, gla_wa2_fwd, gla_ba_fwd, gla_wa2_bwd, gla_ba_bwd,
        gla_norm, diff_lq1, diff_lk1, diff_lq2, diff_lk2, diff_norm, hgrn_lb_logits, hgrn_norm,
    )
    return second_block(
        x, p_2, g_mix_2, w_in_2, conv_dw_w_2, conv_dw_b_2, conv_ln_g_2, conv_ln_b_2,
        lru_conv_w_2, lru_conv_b_2, lru_w_r_2, lru_b_r_2, lru_w_i_2, lru_b_i_2, lru_lambda_2,
        w_out_2, g_ffn_2, w_group_2, b_group_2, w_expert_2, b_expert_2, w1_2, w3_2, w2_2,
        g_ple_2, w_ple_2, g_ple_proj_2, w_ple_gate_2, g_final_2,
    )


_drawn_inputs = setup_inputs


def setup_inputs(seed=0):
    import zlib

    import numpy as np

    out = dict(_drawn_inputs(seed))
    spreads = {}
    factors = {'conv_dw_b_2': 3.787,
     'conv_ln_g_2': 3.069,
     'conv_ln_b_2': 5.168,
     'lru_b_r_2': 46.23,
     'lru_b_i_2': 29.845,
     'b_group_2': 5.073,
     'b_expert_2': 5.536,
     'g_ple_2': 8.0,
     'g_ple_proj_2': 3.886}
    for name, (base, spread) in spreads.items():
        noise = np.random.default_rng([zlib.crc32(name.encode()), seed]).standard_normal(out[name].shape)
        drawn = base * np.exp(spread * noise) if base else spread * noise
        out[name] = __import__('jax').numpy.asarray(drawn.astype(out[name].dtype))
    for name, factor in factors.items():
        out[name] = (out[name] * factor).astype(out[name].dtype)
    return out
```

```python
from contextlib import ExitStack
import math

import numpy as np

import concourse.bass as bass
from concourse import mybir

F32 = mybir.dt.float32
I32 = mybir.dt.int32
U32 = mybir.dt.uint32
ALU = mybir.AluOpType
ACT = mybir.ActivationFunctionType
AX = mybir.AxisListType

P = 128
D = 1024
SEQ = 1024
DEPTH = 2
KT = D // P
TT = SEQ // P
HALF = 512
EPS = 1e-6
F_FLOOR = 1e-30

GLA_HEADS, GLA_DK, GLA_DV, GLA_RANK, GATE_TEMP = 4, 32, 64, 16, 16.0
DIFF_HEADS, DIFF_HD = 4, 64
HGRN_HEADS, HGRN_DK = 4, 64
CHUNK = 16
NCH = SEQ // CHUNK
CPT = P // CHUNK
IN_SIZES = (128, 128, 256, 256, 16, 16, 512, 512, 512, 512, 256, 256, 256, 256, 256)
IN_OFF = [sum(IN_SIZES[:i]) for i in range(len(IN_SIZES) + 1)]
IN_W = IN_OFF[-1]
(GQ, GK, GV, GG, GAF, GAB, DQ, DK, DV, DG, HQ, HZF, HZB, HI, HG) = IN_OFF[:-1]
ROPE_THETA = 10000.0

C_PRE, C_BA, C_GLAN, C_HGRNN, C_LB, C_FLAG, C_N = 0, 8, 10, 11, 12, 16, 17
R_POST, R_DN, R_LQ, R_LINIT, R_N = 0, 1024, 1152, 1408, 1410
K_ID, K_ROT, K_G0, K_G1, K_H, K_MASK, K_COS, K_SIN = 0, 128, 256, 384, 512, 640, 648, 1672
K_NH = 2696
K_N = 2697


class Signal:

    def __init__(self, sem, keys):
        self.sem = sem
        self.order = {k: n + 1 for n, k in enumerate(keys)}

    def wait(self, eng, key):
        eng.wait_ge(self.sem, self.order[key])

    def all(self, eng):
        eng.wait_ge(self.sem, len(self.order))


class Chain:

    def __init__(self, eng, sem):
        self.eng, self.sem, self.n = eng, sem, 0

    def did(self, ins):
        self.n += 1
        ins.then_inc(self.sem, 1)
        return self.n

    def wait(self, n=None):
        self.eng.wait_ge(self.sem, self.n if n is None else n)

    def link(self, ins):
        self.did(ins)
        self.wait()


def rsqrt_of_mean(nc, chain, out, total, n, minus_half):
    chain.link(nc.gpsimd.tensor_scalar(out, total, 1.0 / n, EPS, ALU.mult, ALU.add))
    return nc.gpsimd.tensor_tensor(out, out, minus_half, ALU.pow)


def norm_transpose(nc, S, x_tile, col, hT, ident, minus_half, tag):
    with ExitStack() as ctx:
        sb = lambda name, shape, dt=F32: ctx.enter_context(nc.sbuf_tensor(name, shape, dt))
        xt = sb(tag + "nt_x", [P, 2, D])
        sq = sb(tag + "nt_sq", [P, D])
        xn = sb(tag + "nt_n", [P, 2, D])
        ss = sb(tag + "nt_ss", [P, TT])
        rstd = sb(tag + "nt_r", [P, TT])
        ps = ctx.enter_context(nc.psum_tensor(tag + "nt_ps", [P, 2, KT, P], F32))
        s_x = [S(tag + "nt_x0"), S(tag + "nt_x1")]
        s_sq, s_n, s_t, s_h, s_c, s_rs = S(tag + "nt_sq"), S(tag + "nt_n"), S(tag + "nt_t"), S(tag + "nt_h"), S(tag + "nt_chain"), S(tag + "nt_rs")
        with nc.Block() as block:
            @block.sync
            def _(sp):
                for t in range(TT):
                    if t >= 2:
                        sp.wait_ge(s_sq, t - 1)
                        sp.wait_ge(s_n, t - 1)
                    sp.dma_start(xt[:, t % 2, :], x_tile(t)).then_inc(s_x[t % 2], 16)

            @block.gpsimd
            def _(pool):
                c = Chain(pool, s_c)
                for t in range(TT):
                    pool.wait_ge(s_sq, t + 1)
                    rsqrt_of_mean(nc, c, rstd[:, t:t + 1], ss[:, t:t + 1], D, minus_half).then_inc(s_rs, 1)

            @block.scalar
            def _(act):
                for t in range(TT):
                    act.wait_ge(s_x[t % 2], 16 * (t // 2 + 1))
                    if t:
                        act.wait_ge(s_sq, t)
                    nc.scalar.activation(sq[:], xt[:, t % 2, :], ACT.Square,
                                         accum_out=ss[:, t:t + 1]).then_inc(s_sq, 1)

            def evacuate(dve, t):
                dve.wait_ge(s_t, t + 1)
                nc.vector.tensor_tensor(hT[:, :, t * P:(t + 1) * P], ps[:, t % 2],
                                        col.unsqueeze(2).broadcast_to([P, KT, P]),
                                        ALU.mult).then_inc(s_h, 1)

            @block.vector
            def _(dve):
                for t in range(TT):
                    dve.wait_ge(s_rs, t + 1)
                    dve.wait_ge(s_x[t % 2], 16 * (t // 2 + 1))
                    if t >= 2:
                        dve.wait_ge(s_t, t - 1)
                    nc.vector.tensor_scalar(xn[:, t % 2, :], xt[:, t % 2, :], rstd[:, t:t + 1], None,
                                            ALU.mult).then_inc(s_n, 1)
                    if t:
                        evacuate(dve, t - 1)
                evacuate(dve, TT - 1)

            @block.tensor
            def _(pe):
                for t in range(TT):
                    pe.wait_ge(s_n, t + 1)
                    if t >= 2:
                        pe.wait_ge(s_h, t - 1)
                    for k in range(KT):
                        last = nc.tensor.transpose(ps[:, t % 2, k, :], xn[:, t % 2, k * P:(k + 1) * P],
                                                   ident)
                    last.then_inc(s_t, 1)


def rope_units():
    return [(h, w, f) for h in range(DIFF_HEADS) for w in range(2) for f in range(2)]


def diff_attention(nc, S, l, w_in, hT, y_dram, K, rows):
    NQ = TT
    STEPS = DIFF_HEADS * NQ
    with ExitStack() as ctx:
        sb = lambda name, shape, dt=F32: ctx.enter_context(nc.sbuf_tensor(name, shape, dt))
        wqk = sb("da_wqk", [P, 2, KT, 512])
        vt = sb("da_v", [P, TT, 512])
        gt = sb("da_g", [P, TT, 512])
        qk = sb("da_qk", [P, 2, 2, SEQ])
        raw = sb("da_raw", [P, 2, HALF])
        rs_ = sb("da_rs", [P, HALF])
        small = sb("da_small", [P, 16])
        st = sb("da_st", [P, STEPS, 10])
        with ExitStack() as ctx2:
            pr = [ctx2.enter_context(nc.psum_tensor(f"da_p{i}", [P, HALF], F32)) for i in range(4)]
            wvg = ctx2.enter_context(nc.sbuf_tensor("da_wvg", [P, 2, KT, 512], F32))
            sig = ctx2.enter_context(nc.sbuf_tensor("da_sig", [P, 2, 512], F32))
            s_w, s_p, s_v, s_sg, s_g, s_g1, s_lam, s_lr, s_le = (S("da_w"), S("da_p"), S("da_v"), S("da_sg"), S("da_g"),
                                                 S("da_g1"), S("da_lam"), S("da_lr"), S("da_le"))
            with nc.Block() as block:
                @block.sync
                def _(sp):
                    for j, off in enumerate((DV, DG)):
                        sp.dma_start(wvg[:, j], w_in(l, off, 512)).then_inc(s_w, 16)
                        sp.wait_ge(s_w, 16 * (j + 1))
                    for j, off in enumerate((DQ, DK)):
                        sp.dma_start(wqk[:, j], w_in(l, off, 512)).then_inc(s_w, 16)
                    sp.wait_ge(s_w, 64)

                @block.tensor
                def _(pe):
                    for n in range(2 * TT):
                        j, t = divmod(n, TT)
                        if t == 0:
                            pe.wait_ge(s_w, 16 * (j + 1))
                        if n >= 4:
                            m = n - 4
                            if m < TT:
                                pe.wait_ge(s_v, m + 1)
                            else:
                                pe.wait_ge(s_g1, m - TT + 1)
                        for k in range(KT):
                            last = nc.tensor.matmul(pr[n % 4][:], hT[:, k, t * P:(t + 1) * P],
                                                    wvg[:, j, k, :], start=(k == 0), stop=(k == KT - 1))
                        last.then_inc(s_p, 1)

                @block.scalar
                def _(act):
                    act.wait_ge(s_lr, 2)
                    nc.scalar.activation(small[:, 2:4], small[:, 0:2], ACT.Exp).then_inc(s_le, 1)
                    for t in range(TT):
                        act.wait_ge(s_p, t + 1)
                        nc.scalar.activation(vt[:, t, :], pr[t % 4][:], ACT.Copy).then_inc(s_v, 1)
                    for t in range(TT):
                        act.wait_ge(s_p, TT + t + 1)
                        if t >= 2:
                            act.wait_ge(s_g1, t - 1)
                        nc.scalar.activation(sig[:, t % 2, :], pr[(TT + t) % 4][:], ACT.Sigmoid).then_inc(s_sg, 1)

                @block.vector
                def _(dve):
                    for j in range(2):
                        a = rows[:, R_LQ + 128 * j:R_LQ + 128 * j + 64]
                        b = rows[:, R_LQ + 128 * j + 64:R_LQ + 128 * j + 128]
                        nc.vector.tensor_tensor_reduce(sig[:, j, 0:64], a, b, 1.0, 0.0, ALU.mult, ALU.add,
                                                       small[:, j:j + 1]).then_inc(s_lr, 1)
                    dve.wait_ge(s_le, 1)
                    nc.vector.tensor_tensor(small[:, 4:5], small[:, 3:4], small[:, 2:3], ALU.subtract).then_inc(s_lam, 1)
                    dve.wait_ge(s_lam, 1)
                    nc.vector.tensor_tensor(small[:, 5:6], small[:, 4:5], rows[:, R_LINIT:R_LINIT + 1],
                                            ALU.subtract).then_inc(s_lam, 1)
                    nc.vector.tensor_scalar(rs_[:, 0:128], rows[:, R_DN:R_DN + 128],
                                            rows[:, R_LINIT + 1:R_LINIT + 2], None, ALU.mult).then_inc(s_lam, 1)
                    dve.wait_ge(s_lam, 3)
                    for t in range(TT):
                        dve.wait_ge(s_sg, t + 1)
                        nc.vector.tensor_tensor(gt[:, t, :], pr[(TT + t) % 4][:], sig[:, t % 2, :],
                                                ALU.mult).then_inc(s_g1, 1)
                        dve.wait_ge(s_g1, t + 1)
                        g4 = gt[:, t, :].rearrange("p (h v) -> p h v", h=DIFF_HEADS)
                        nc.vector.tensor_tensor(g4, g4, rs_[:, 0:128].unsqueeze(1).broadcast_to([P, DIFF_HEADS, 128]),
                                                ALU.mult).then_inc(s_g, 1)

        e = sb("da_e", [P, 2, 2, SEQ])
        w = sb("da_wt", [P, 2, SEQ])
        wT = sb("da_wT", [P, 2, TT, P])
        y = sb("da_y", [P, 2, P])
        osb = sb("da_o", [P, 4, P])
        junk = sb("da_j", [P, P])
        yst = sb("da_yst", [P, 2, SEQ])
        s_st = [S("da_st0"), S("da_st1")]
        ps_s = ctx.enter_context(nc.psum_tensor("da_ps", [P, 2, SEQ], F32))
        ps_t = ctx.enter_context(nc.psum_tensor("da_pt", [P, TT, P], F32))
        ps_o = ctx.enter_context(nc.psum_tensor("da_po", [P, HALF], F32))
        ps_r = ctx.enter_context(nc.psum_tensor("da_pr", [P, HALF], F32))
        s_s, s_m, s_e, s_w2, s_t2, s_wT, s_pv, s_y, s_yt, s_ye, s_c = (
            S("da_s"), S("da_m"), S("da_e"), S("da_w2"), S("da_t2"), S("da_wT"), S("da_pv"), S("da_y"),
            S("da_yt"), S("da_ye"), S("da_chain"))
        s_pj, s_rw, s_rt, s_rc, s_rd = S("da_pj"), S("da_rw"), S("da_rt"), S("da_rc"), S("da_rd")
        s_pv_read, s_oss, s_ors, s_pc = S("da_pvr"), S("da_oss"), S("da_ors"), S("da_pool")
        units = rope_units()

        def unit_at(g, odd):
            n = 4 + (g // 2)
            return n if g % 2 == odd and g >= 0 and n < len(units) else None

        with nc.Block() as block:
            @block.sync
            def _(sp):
                for h in range(DIFF_HEADS):
                    sp.wait_ge(s_ye, NQ * (h + 1))
                    sp.dma_start(y_dram[2 + h], yst[:, h % 2, :]).then_inc(s_st[h % 2], 16)
                for j in range(2):
                    sp.wait_ge(s_st[j], 16 * DIFF_HEADS // 2)

            @block.gpsimd
            def _(pool):
                c = Chain(pool, s_pc)
                for a in range(STEPS):
                    pool.wait_ge(s_oss, a + 1)
                    rsqrt_of_mean(nc, c, st[:, a, 7:8], st[:, a, 6:7], 2 * DIFF_HD, K[:, K_NH:K_NH + 1]).then_inc(s_ors, 1)

            @block.tensor
            def _(pe):
                def project(n):
                    h, wh, f = units[n]
                    if n >= 1:
                        pe.wait_ge(s_rd, n)
                    for k in range(KT):
                        last = nc.tensor.matmul(ps_r[:], wqk[:, wh, k, h * P:(h + 1) * P],
                                                hT[:, k, f * HALF:(f + 1) * HALF], start=(k == 0), stop=(k == KT - 1))
                    last.then_inc(s_pj, 1)

                def turn(n):
                    pe.wait_ge(s_rw, n + 1)
                    nc.tensor.matmul(ps_r[:], K[:, K_ROT:K_ROT + P], raw[:, n % 2, :], start=True,
                                     stop=True).then_inc(s_rt, 1)

                for n in range(4):
                    project(n)
                    turn(n)
                for g in range(STEPS + 4):
                    if 4 <= g:
                        a = g - 4
                        pe.wait_ge(s_y, a + 1)
                        if a:
                            pe.wait_ge(s_ye, a)
                        done = [n for n in range(4, len(units)) if 2 * (n - 4) + 1 < g]
                        pe.wait_ge(s_rd, 4 + len(done))
                        raws = [n for n in range(4, len(units)) if 2 * (n - 4) < g]
                        pe.wait_ge(s_rw, 4 + len(raws))
                        nc.tensor.transpose(ps_r[:, 0:P], y[:, a % 2, :], K[:, K_ID:K_ID + P]).then_inc(s_yt, 1)
                    if g < STEPS:
                        h, i = divmod(g, NQ)
                        if i == 0:
                            pe.wait_ge(s_rc, 4 * (h + 1))
                        if g:
                            pe.wait_ge(s_e, 2 * g)
                        for c in range(2):
                            rows_ = slice(64 * c, 64 * c + 64)
                            for f in range(2):
                                last = nc.tensor.matmul(
                                    ps_s[:, c, f * HALF:(f + 1) * HALF], qk[rows_, h % 2, 0, i * P:(i + 1) * P],
                                    qk[rows_, h % 2, 1, f * HALF:(f + 1) * HALF], start=True, stop=True)
                            last.then_inc(s_s, 1)
                    if g >= 4 and (unit_at(g, 0) is not None or unit_at(g, 1) is not None):
                        pe.wait_ge(s_ye, g - 3)
                    if unit_at(g, 0) is not None:
                        project(unit_at(g, 0))
                    if unit_at(g, 1) is not None:
                        turn(unit_at(g, 1))
                    if 1 <= g <= STEPS:
                        a = g - 1
                        pe.wait_ge(s_w2, a + 1)
                        if a >= 1:
                            pe.wait_ge(s_wT, a)
                        for k in range(TT):
                            last = nc.tensor.transpose(ps_t[:, k, :], w[:, a % 2, k * P:(k + 1) * P], K[:, K_ID:K_ID + P])
                        last.then_inc(s_t2, 1)
                    if 2 <= g <= STEPS + 1:
                        a = g - 2
                        ha = a // NQ
                        pe.wait_ge(s_wT, a + 1)
                        if a:
                            pe.wait_ge(s_pv_read, a)
                        for k in range(TT):
                            last = nc.tensor.matmul(ps_o[:, 0:P], wT[:, a % 2, k, :], vt[:, k, ha * P:(ha + 1) * P],
                                                    start=(k == 0), stop=(k == TT - 1))
                        last.then_inc(s_pv, 1)

            @block.scalar
            def _(act):
                def raw_copy(n):
                    act.wait_ge(s_pj, n + 1)
                    if n >= 2:
                        act.wait_ge(s_rc, n - 1)
                    nc.scalar.activation(raw[:, n % 2, :], ps_r[:], ACT.Copy).then_inc(s_rw, 1)

                for n in range(4):
                    raw_copy(n)
                for g in range(STEPS + 4):
                    if 4 <= g:
                        a = g - 4
                        ha, ia = divmod(a, NQ)
                        act.wait_ge(s_yt, a + 1)
                        if ia == 0 and ha >= 2:
                            act.wait_ge(s_st[ha % 2], 16 * (ha // 2))
                        nc.scalar.activation(yst[:, ha % 2, ia * P:(ia + 1) * P], ps_r[:, 0:P],
                                             ACT.Copy).then_inc(s_ye, 1)
                    if g < STEPS:
                        for c in range(2):
                            act.wait_ge(s_m, 2 * g + c + 1)
                            if g >= 2 and c == 0:
                                act.wait_ge(s_w2, g - 1)
                            nc.scalar.activation(e[:, g % 2, c, :], ps_s[:, c, :], ACT.Exp,
                                                 bias=st[:, g, c:c + 1], scale=DIFF_HD ** -0.5,
                                                 accum_out=st[:, g, 2 + c:3 + c]).then_inc(s_e, 1)
                    if unit_at(g, 0) is not None:
                        raw_copy(unit_at(g, 0))
                    if 1 <= g <= STEPS:
                        a = g - 1
                        act.wait_ge(s_t2, a + 1)
                        if a >= 2:
                            act.wait_ge(s_pv, a - 1)
                        nc.scalar.activation(wT[:, a % 2], ps_t[:], ACT.Copy).then_inc(s_wT, 1)

            @block.vector
            def _(dve):
                c_ = Chain(dve, s_c)

                def turned(n):
                    h, wh, f = units[n]
                    cols = slice(f * HALF, (f + 1) * HALF)
                    dve.wait_ge(s_rt, n + 1)
                    if n:
                        dve.wait_ge(s_rc, n)
                    if units[n][0] >= 2:
                        dve.wait_ge(s_s, 2 * NQ * (h - 1))
                    nc.vector.tensor_tensor(rs_[:], ps_r[:], K[:, K_SIN + f * HALF:K_SIN + (f + 1) * HALF],
                                            ALU.mult).then_inc(s_rd, 1)
                    c_.did(nc.vector.tensor_tensor(qk[:, h % 2, wh, cols], raw[:, n % 2, :],
                                                   K[:, K_COS + f * HALF:K_COS + (f + 1) * HALF], ALU.mult))
                    c_.wait()
                    dve.wait_ge(s_rd, n + 1)
                    nc.vector.tensor_tensor(qk[:, h % 2, wh, cols], qk[:, h % 2, wh, cols], rs_[:],
                                            ALU.add).then_inc(s_rc, 1)

                for n in range(4):
                    turned(n)
                for g in range(STEPS + 3):
                    if 1 <= g <= STEPS:
                        a = g - 1
                        dve.wait_ge(s_e, 2 * a + 2)
                        c_.link(nc.vector.reciprocal(st[:, a, 4:6], st[:, a, 2:4]))
                        c_.link(nc.vector.scalar_tensor_tensor(st[:, a, 6:7], st[:, a, 2:3], st[:, a, 5:6],
                                                               small[:, 5:6], ALU.mult, ALU.mult))
                        if a >= 2:
                            dve.wait_ge(s_t2, a - 1)
                        nc.vector.scalar_tensor_tensor(w[:, a % 2, :], e[:, a % 2, 1, :], st[:, a, 6:7],
                                                       e[:, a % 2, 0, :], ALU.mult, ALU.add).then_inc(s_w2, 1)
                    if g < STEPS:
                        for c in range(2):
                            dve.wait_ge(s_s, 2 * g + c + 1)
                            c_.link(nc.vector.tensor_reduce(st[:, g, 8 + c:9 + c], ps_s[:, c, :], AX.X, ALU.max))
                            nc.vector.tensor_scalar(st[:, g, c:c + 1], st[:, g, 8 + c:9 + c], -DIFF_HD ** -0.5, None,
                                                    ALU.mult).then_inc(s_m, 1)
                    if unit_at(g, 1) is not None:
                        turned(unit_at(g, 1))
                    if 2 <= g <= STEPS + 1:
                        a = g - 2
                        ha, ia = divmod(a, NQ)
                        dve.wait_ge(s_pv, a + 1)
                        nc.vector.tensor_scalar(osb[:, a % 4, :], ps_o[:, 0:P], st[:, a, 4:5], None,
                                                ALU.mult).then_inc(s_pv_read, 1)
                        dve.wait_ge(s_pv_read, a + 1)
                        if a >= 1:
                            dve.wait_ge(s_oss, a)
                        nc.vector.tensor_tensor_reduce(junk[:], osb[:, a % 4, :], osb[:, a % 4, :], 1.0, 0.0,
                                                       ALU.mult, ALU.add, st[:, a, 6:7]).then_inc(s_oss, 1)
                    if 3 <= g <= STEPS + 2:
                        a = g - 3
                        ha, ia = divmod(a, NQ)
                        dve.wait_ge(s_ors, a + 1)
                        if a >= 2:
                            dve.wait_ge(s_yt, a - 1)
                        nc.vector.scalar_tensor_tensor(y[:, a % 2, :], osb[:, a % 4, :], st[:, a, 7:8],
                                                       gt[:, ia, ha * P:(ha + 1) * P], ALU.mult, ALU.mult).then_inc(s_y, 1)


def out_project(nc, S, y_dram, w_dram, x_tile, x_out, post, minus_half, tag):
    with ExitStack() as ctx:
        sb = lambda name, shape, dt=F32: ctx.enter_context(nc.sbuf_tensor(name, shape, dt))
        w = sb(tag + "op_w", [P, KT, D])
        yT = sb(tag + "op_y", [P, KT, SEQ])
        xt = sb(tag + "op_x", [P, 2, D])
        xo = sb(tag + "op_o", [P, 2, D])
        sq = sb(tag + "op_sq", [P, D])
        ss = sb(tag + "op_ss", [P, TT])
        rstd = sb(tag + "op_r", [P, TT])
        s_pc = S(tag + "op_pool")
        ps = [ctx.enter_context(nc.psum_tensor(f"{tag}op_ps{i}", [P, D], F32)) for i in range(2)]
        s_w = [S(tag + "op_w0"), S(tag + "op_w1")]
        s_x = [S(tag + "op_x0"), S(tag + "op_x1")]
        s_o = [S(tag + "op_o0"), S(tag + "op_o1")]
        s_p, s_sq, s_s, s_y, s_c = S(tag + "op_p"), S(tag + "op_sq"), S(tag + "op_s"), S(tag + "op_y"), S(tag + "op_chain")
        with nc.Block() as block:
            @block.sync
            def _(sp):
                for j in range(2):
                    sp.dma_start(w[:, 4 * j:4 * j + 4, :], w_dram[:, 4 * j:4 * j + 4, :]).then_inc(s_w[j], 16)
                    sp.dma_start(yT[:, 4 * j:4 * j + 4, :],
                                 y_dram[4 * j:4 * j + 4].rearrange("k p s -> p k s")).then_inc(s_w[j], 16)
                for t in range(TT):
                    if t >= 2:
                        sp.wait_ge(s_y, t - 1)
                    sp.dma_start(xt[:, t % 2, :], x_tile(t)).then_inc(s_x[t % 2], 16)

            @block.tensor
            def _(pe):
                for t in range(TT):
                    if t >= 2:
                        pe.wait_ge(s_y, t - 1)
                    for k in range(KT):
                        if t == 0 and k % 4 == 0:
                            pe.wait_ge(s_w[k // 4], 32)
                        for f in range(2):
                            last = nc.tensor.matmul(ps[t % 2][:, f * HALF:(f + 1) * HALF], yT[:, k, t * P:(t + 1) * P],
                                                    w[:, k, f * HALF:(f + 1) * HALF], start=(k == 0), stop=(k == KT - 1))
                    last.then_inc(s_p, 1)

            @block.gpsimd
            def _(pool):
                c = Chain(pool, s_pc)
                for t in range(TT if post is not None else 0):
                    pool.wait_ge(s_sq, t + 1)
                    rsqrt_of_mean(nc, c, rstd[:, t:t + 1], ss[:, t:t + 1], D, minus_half).then_inc(s_s, 1)

            @block.scalar
            def _(act):
                for t in range(TT):
                    if post is not None:
                        act.wait_ge(s_p, t + 1)
                        if t:
                            act.wait_ge(s_sq, t)
                        nc.scalar.activation(sq[:], ps[t % 2][:], ACT.Square, accum_out=ss[:, t:t + 1]).then_inc(s_sq, 1)
                    act.wait_ge(s_y, t + 1)
                    act.dma_start(x_out(t), xo[:, t % 2, :]).then_inc(s_o[t % 2], 16)
                for j in range(2):
                    act.wait_ge(s_o[j], 16 * TT // 2)

            @block.vector
            def _(dve):
                c = Chain(dve, s_c)
                for t in range(TT):
                    if t >= 2:
                        dve.wait_ge(s_o[t % 2], 16 * (t // 2))
                    if post is not None:
                        dve.wait_ge(s_s, t + 1)
                        c.link(nc.vector.scalar_tensor_tensor(xo[:, t % 2, :], ps[t % 2][:], rstd[:, t:t + 1], post,
                                                              ALU.mult, ALU.mult))
                        dve.wait_ge(s_x[t % 2], 16 * (t // 2 + 1))
                        nc.vector.tensor_tensor(xo[:, t % 2, :], xo[:, t % 2, :], xt[:, t % 2, :], ALU.add).then_inc(s_y, 1)
                    else:
                        dve.wait_ge(s_p, t + 1)
                        dve.wait_ge(s_x[t % 2], 16 * (t // 2 + 1))
                        nc.vector.tensor_tensor(xo[:, t % 2, :], ps[t % 2][:], xt[:, t % 2, :], ALU.add).then_inc(s_y, 1)


def by_chunk(ap):
    return ap.rearrange("p (n i) -> p n i", i=CHUNK)


def gated_scans(nc, S, l, w_in, wa2, hT, y_dram, K, cols):
    LAGS = CHUNK
    units = (dict(nv=2, heads=4, dk=32, yt=(0, 1)), dict(nv=1, heads=2, dk=64, yt=(6,)),
             dict(nv=1, heads=2, dk=64, yt=(7,)))
    NU = len(units)
    proj = [
        [("q", GQ, P), ("k", GK, P), ("v0", GV, P), ("v1", GV + P, P), ("g0", GG, P), ("g1", GG + P, P), ("a", GAF, 32)],
    ] + [[("q", HQ + P * j, P), ("zf", HZF + P * j, P), ("zb", HZB + P * j, P), ("v0", HI + P * j, P),
          ("g0", HG + P * j, P)] for j in range(2)]
    banks = [(u, name, f) for u in range(NU) for name, _, _ in proj[u] for f in range(2)]
    bank_no = {b: i for i, b in enumerate(banks)}

    with ExitStack() as ctx:
        sb = lambda name, shape, dt=F32: ctx.enter_context(nc.sbuf_tensor(name, shape, dt))
        wt = sb("gs_w", [P, 4, KT, P])
        wa = sb("gs_wa", [32, 2 * P])
        q = sb("gs_q", [P, SEQ])
        kd = sb("gs_k", [P, 2, SEQ])
        fd = sb("gs_f", [P, 2, SEQ])
        v = sb("gs_v", [P, 2, SEQ])
        gate = sb("gs_g", [P, 2, SEQ])
        vtok = sb("gs_vt", [P, TT, 2 * P])
        sig = sb("gs_sig", [P, 2, HALF])
        ats = sb("gs_a", [32, SEQ])
        pre = sb("gs_pre", [P, 2, SEQ])
        suf = sb("gs_suf", [P, 2, SEQ])
        R = sb("gs_R", [P, 2, SEQ])
        ys = sb("gs_y", [P, 2, HALF])
        Pq = sb("gs_P", [P, 2, SEQ])
        oacc = sb("gs_o", [P, 2, SEQ])
        tmp = sb("gs_tmp", [P, 2, HALF])
        qx = sb("gs_qx", [P, 2, SEQ])
        ktok = sb("gs_kt", [P, TT, P])
        U = sb("gs_U", [P, NCH, GLA_DV])
        Vx = sb("gs_Vx", [P, 4, CPT, GLA_DV])
        lb = sb("gs_lb", [P, 8])
        pb = [ctx.enter_context(nc.psum_tensor(f"gs_b{i}", [P, HALF], F32)) for i in range(2)]
        plag = [ctx.enter_context(nc.psum_tensor(f"gs_l{i}", [P, HALF], F32)) for i in range(4)]
        pu = ctx.enter_context(nc.psum_tensor("gs_u", [P, 2, HALF], F32))

        s_w = [S(f"gs_w{i}") for i in range(4)]
        items = [(u, name) for u in range(NU) for name, _, _ in proj[u]]
        s_sg, s_done = S("gs_sg"), S("gs_done")
        s_wa = S("gs_wa")
        s_fm, s_fr = S("gs_fm"), S("gs_fr")
        s_yo = [S("gs_yo0"), S("gs_yo1")]
        s_lbe, s_lbd = S("gs_lbe"), S("gs_lbd")
        proj_done = Signal(S("gs_proj"), banks)
        read_out = Signal(S("gs_read"), banks)
        gate_ready = Signal(S("gs_gate"), [b for b in banks if b[1][0] == "g"])
        gla_log = [(d, f) for d in range(2) for f in range(2)]
        s_gx, s_gl1, s_gl2, s_gl3, s_gmin, s_gf, s_gz = (S("gs_gx"), S("gs_gl1"), S("gs_gl2"), S("gs_gl3"), S("gs_gmin"),
                                                   S("gs_gf"), S("gs_gz"))
        unit_dir = [(u, d) for u in range(NU) for d in range(2)]
        ready = Signal(S("gs_ready"), range(NU))
        s_chain = S("gs_chain")
        lag_keys = [(u, d, j) for u, d in unit_dir for j in range(LAGS)]
        P_ready = Signal(S("gs_P"), lag_keys)
        pieces = []
        for u, d, j in lag_keys:
            for vt_ in range(units[u]["nv"]):
                for hf in (range(2) if j < 8 else range(1)):
                    pieces.append((u, d, j, vt_, hf))
        piece_no = {p: i for i, p in enumerate(pieces)}
        lag_sum = Signal(S("gs_lag"), pieces)
        lag_read = Signal(S("gs_lagr"), pieces)
        suf_ready = Signal(S("gs_suf"), unit_dir)
        qx_keys = [(u, d, vt_) for u, d in unit_dir for vt_ in range(units[u]["nv"])]
        qx_ready = Signal(S("gs_qx"), qx_keys)
        vtr = [(u, t) for u in range(NU) for t in range(TT)]
        v_turned, v_tok = Signal(S("gs_vtr"), vtr), Signal(S("gs_vtk"), vtr)
        kt_keys = [(u, d, f) for u, d in unit_dir for f in range(2)]
        k_turned, k_tok = Signal(S("gs_ktr"), kt_keys), Signal(S("gs_ktk"), kt_keys)
        ut = [(u, d, t) for u, d in unit_dir for t in range(TT)]
        Vx_ready, U_sum, U_ready = Signal(S("gs_vx"), ut), Signal(S("gs_us"), ut), Signal(S("gs_ur"), ut)
        state_ready = Signal(S("gs_st"), unit_dir)
        inter_keys = [(u, d, vt_, f) for u, d in unit_dir for vt_ in range(units[u]["nv"]) for f in range(2)]
        inter_sum, inter_read = Signal(S("gs_is"), inter_keys), Signal(S("gs_ir"), inter_keys)
        fin_keys = [(u, vt_, f) for u in range(NU) for vt_ in range(units[u]["nv"]) for f in range(2)]
        fin_sq, fin_sum, fin_y = (Signal(S("gs_fq"), fin_keys), Signal(S("gs_fs"), fin_keys),
                                  Signal(S("gs_fy"), fin_keys))

        def half(ap, f):
            return ap[:, f * HALF:(f + 1) * HALF]

        with nc.Block() as block:
            @block.sync
            def _(sp):
                sp.dma_start(wa[:], wa2(l)).then_inc(s_wa, 16)
                for i, (u, name) in enumerate(items):
                    if i >= 4:
                        proj_done.wait(sp, (*items[i - 4], 1))
                    off, width = [(o, w) for n, o, w in proj[u] if n == name][0]
                    sp.dma_start(wt[:, i % 4, :, 0:width], w_in(l, off, width)).then_inc(s_w[i % 4], 16)

            def lag_window(ap3, d, j, hf):
                n0, n1 = (32 * hf, 32 * hf + 32) if j < 8 else (0, NCH)
                lo, hi = (j, CHUNK) if d == 0 else (0, CHUNK - j)
                return ap3[:, n0:n1, lo:hi], (n1 - n0) * (CHUNK - j)

            def partner(ap3, d, j, hf):
                n0, n1 = (32 * hf, 32 * hf + 32) if j < 8 else (0, NCH)
                lo, hi = (0, CHUNK - j) if d == 0 else (j, CHUNK)
                return ap3[:, n0:n1, lo:hi]

            def spread_query(dve, c, u, d, vt_):
                i = qx_keys.index((u, d, vt_))
                if i:
                    inter_sum.wait(dve, (*qx_keys[i - 1], 1))
                if u < 2:
                    c.link(nc.vector.memset(qx[:], 0.0))
                dk = units[u]["dk"]
                for h in range(2):
                    rr = slice((2 * vt_ + h) * dk, (2 * vt_ + h + 1) * dk)
                    last = nc.vector.tensor_tensor(qx[rr, h, :], q[rr, :], pre[rr, d, :], ALU.mult)
                last.then_inc(qx_ready.sem, 1)

            def lags(dve, c, u, d):
                un = units[u]
                f3, q3 = by_chunk(fd[:, d]), by_chunk(q[:])
                k3 = by_chunk(kd[:, d if u else 0])
                R3 = [by_chunk(R[:, i]) for i in range(2)]
                P3 = [by_chunk(Pq[:, i]) for i in range(2)]
                v3 = [by_chunk(v[:, i]) for i in range(2)]
                o3 = [by_chunk(oacc[:, i]) for i in range(2)]
                first = lambda ap, j: ap[:, :, j:] if d == 0 else ap[:, :, :CHUNK - j]
                second = lambda ap, j: ap[:, :, :CHUNK - j] if d == 0 else ap[:, :, j:]

                def decayed(j):
                    if j:
                        before = k3 if j == 1 else R3[(j - 1) % 2]
                        b = before[:, :, j - 1:CHUNK - 1] if d == 0 else before[:, :, 1:CHUNK - j + 1]
                        c.link(nc.vector.tensor_tensor(first(R3[j % 2], j), b, first(f3, j), ALU.mult))
                    if j >= 2:
                        lag_sum.wait(dve, [p for p in pieces if p[:3] == (u, d, j - 2)][-1])
                    elif (u, d) != (0, 0):
                        up, dp = (u, 0) if d else (u - 1, 1)
                        lag_sum.wait(dve, [p for p in pieces if p[:3] == (up, dp, LAGS - 1)][-1])
                    r = k3 if j == 0 else R3[j % 2]
                    nc.vector.tensor_tensor(first(P3[j % 2], j), first(q3, j), first(r, j), ALU.mult).then_inc(P_ready.sem, 1)

                decayed(0)
                for j in range(LAGS):
                    if j + 1 < LAGS:
                        decayed(j + 1)
                    for vt_ in range(un["nv"]):
                        for hf in (range(2) if j < 8 else range(1)):
                            piece = (u, d, j, vt_, hf)
                            n = piece_no[piece]
                            lag_sum.wait(dve, piece)
                            n0, n1 = (32 * hf, 32 * hf + 32) if j < 8 else (0, NCH)
                            cnt = (n1 - n0) * (CHUNK - j)
                            ps3 = plag[n % 4][:, 0:cnt].rearrange("p (n i) -> p n i", i=CHUNK - j)
                            vv = second(v3[vt_], j)[:, n0:n1]
                            oo = first(o3[vt_], j)[:, n0:n1]
                            if d == 0 and j == 0:
                                c.did(nc.vector.tensor_tensor(oo, ps3, vv, ALU.mult))
                                dve.wait_ge(c.sem, c.n)
                                dve.sem_inc(lag_read.sem, 1)
                            else:
                                tt = tmp[:, n % 2, 0:cnt].rearrange("p (n i) -> p n i", i=CHUNK - j)
                                nc.vector.tensor_tensor(tt, ps3, vv, ALU.mult).then_inc(lag_read.sem, 1)
                                lag_read.wait(dve, piece)
                                c.wait()
                                c.did(nc.vector.tensor_tensor(oo, oo, tt, ALU.add))

            @block.tensor
            def _(pe):
                ident = K[:, K_ID:K_ID + P]
                for u in range(NU):
                    un = units[u]
                    for n, (name, _, width) in enumerate(proj[u]):
                        it = items.index((u, name))
                        pe.wait_ge(s_w[it % 4], 16 * (it // 4 + 1))
                        for f in range(2):
                            i = bank_no[(u, name, f)]
                            if i >= 2:
                                read_out.wait(pe, banks[i - 2])
                            if u and f == 0 and n == 0:
                                fin_y.wait(pe, (u - 1, units[u - 1]["nv"] - 1, 1))
                            for k in range(KT):
                                last = nc.tensor.matmul(pb[i % 2][0:width, :], wt[:, it % 4, k, 0:width], half(hT[:, k], f),
                                                        start=(k == 0), stop=(k == KT - 1))
                            last.then_inc(proj_done.sem, 1)
                    if u == 0:
                        pe.wait_ge(s_wa, 16)
                        for m, (d, f) in enumerate(gla_log):
                            read_out.wait(pe, (0, "a", 1))
                            if m >= 2:
                                pe.wait_ge(s_gx, m - 1)
                            nc.tensor.matmul(pb[m % 2][:], wa[:, d * P:(d + 1) * P], half(ats, f), start=True,
                                             stop=True).then_inc(s_gz, 1)
                        pe.wait_ge(s_gx, 4)
                    for t in range(TT):
                        for vt_ in range(un["nv"]):
                            if t >= 2:
                                v_tok.wait(pe, (u, t - 2))
                            read_out.wait(pe, (u, f"v{vt_}", 1))
                            read_out.wait(pe, banks[bank_no[(u, proj[u][-1][0], 1)]])
                            last = nc.tensor.transpose(pb[t % 2][:, vt_ * P:(vt_ + 1) * P], v[:, vt_, t * P:(t + 1) * P], ident)
                        last.then_inc(v_turned.sem, 1)
                    for d in range(2):
                        suf_ready.wait(pe, (u, d))
                        v_tok.wait(pe, (u, TT - 1))
                        for f in range(2):
                            if d or f:
                                pass
                            for t in range(4 * f, 4 * f + 4):
                                last = nc.tensor.transpose(pb[f][:, (t % 4) * P:(t % 4 + 1) * P],
                                                           suf[:, d, t * P:(t + 1) * P], ident)
                            last.then_inc(k_turned.sem, 1)
                        for t in range(TT):
                            Vx_ready.wait(pe, (u, d, t))
                            if t == 0:
                                k_tok.wait(pe, (u, d, 1))
                                if (u, d) != (0, 0):
                                    before = unit_dir[unit_dir.index((u, d)) - 1]
                                    inter_read.wait(pe, (*before, units[before[0]]["nv"] - 1, 1))
                            if t >= 2:
                                U_ready.wait(pe, (u, d, t - 2))
                            dk = un["dk"]
                            for h in range(un["heads"]):
                                last = nc.tensor.matmul(pu[h * dk:(h + 1) * dk, t % 2, :],
                                                        ktok[:, t, h * dk:(h + 1) * dk],
                                                        Vx[:, h].rearrange("p j v -> p (j v)"), start=True, stop=True)
                            last.then_inc(U_sum.sem, 1)
                        for j in range(LAGS):
                            P_ready.wait(pe, (u, d, j))
                            src = by_chunk(Pq[:, j % 2, :])
                            for vt_ in range(un["nv"]):
                                kcol = (K_G0, K_G1)[vt_] if u == 0 else K_H
                                for hf in (range(2) if j < 8 else range(1)):
                                    n = piece_no[(u, d, j, vt_, hf)]
                                    if n >= 4:
                                        lag_read.wait(pe, pieces[n - 4])
                                    rhs, cnt = lag_window(src, d, j, hf)
                                    nc.tensor.matmul(plag[n % 4][:, 0:cnt], K[:, kcol:kcol + P], rhs, start=True,
                                                     stop=True).then_inc(lag_sum.sem, 1)
                        state_ready.wait(pe, (u, d))
                        for vt_ in range(un["nv"]):
                            qx_ready.wait(pe, (u, d, vt_))
                            for f in range(2):
                                m = inter_keys.index((u, d, vt_, f))
                                if m >= 2:
                                    inter_read.wait(pe, inter_keys[m - 2])
                                for n in range(32 * f, 32 * f + 32):
                                    prev = n - 1 if d == 0 else n + 1
                                    if not 0 <= prev < NCH:
                                        continue
                                    for h in range(2):
                                        last = nc.tensor.matmul(
                                            pu[64 * h:64 * h + 64, m % 2, (n % 32) * CHUNK:(n % 32 + 1) * CHUNK],
                                            U[:, prev, :], qx[:, h, n * CHUNK:(n + 1) * CHUNK],
                                            start=True, stop=True)
                                last.then_inc(inter_sum.sem, 1)
                    for vt_ in range(un["nv"]):
                        for f in range(2):
                            fin_sq.wait(pe, (u, vt_, f))
                            m = fin_keys.index((u, vt_, f))
                            if m >= 2:
                                pe.wait_ge(s_fm, m - 1)
                            nc.tensor.matmul(pb[m % 2][:], K[:, K_H:K_H + P], half(Pq[:, m % 2], f), start=True,
                                             stop=True).then_inc(fin_sum.sem, 1)

            @block.scalar
            def _(act):
                act.wait_ge(s_lbd, 1)
                nc.scalar.activation(lb[:, 0:2], lb[:, 4:6], ACT.Sigmoid).then_inc(s_lbe, 1)
                for u in range(NU):
                    un = units[u]
                    if u:
                        fin_y.wait(act, (u - 1, units[u - 1]["nv"] - 1, 1))
                    for name, _, width in proj[u]:
                        for f in range(2):
                            proj_done.wait(act, (u, name, f))
                            src = pb[bank_no[(u, name, f)] % 2]
                            if name == "q":
                                ins = nc.scalar.activation(half(q, f), src[:], ACT.Copy, scale=GLA_DK ** -0.5 if u == 0 else 1.0)
                            elif name == "k":
                                ins = nc.scalar.activation(half(kd[:, 0], f), src[:], ACT.Copy)
                            elif name[0] == "v":
                                ins = nc.scalar.activation(half(v[:, int(name[1])], f), src[:], ACT.Copy)
                            elif name == "a":
                                ins = nc.scalar.activation(half(ats, f), src[0:32, :], ACT.Copy)
                            elif name[0] == "z":
                                d = name[1] == "b"
                                nc.scalar.activation(half(fd[:, int(d)], f), src[:], ACT.Sigmoid)
                                ins = nc.scalar.activation(half(kd[:, int(d)], f), src[:], ACT.Sigmoid, scale=-1.0)
                            else:
                                ins = nc.scalar.activation(half(gate[:, int(name[1])], f), src[:], ACT.Copy)
                            ins.then_inc(read_out.sem, 1)
                    for vt_ in range(un["nv"]):
                        for f in range(2):
                            n = list(gate_ready.order).index((u, f"g{vt_}", f))
                            if n >= 2:
                                gate_ready.wait(act, list(gate_ready.order)[n - 2])
                            if n < 2 or True:
                                read_out.wait(act, (u, f"g{vt_}", f))
                            nc.scalar.activation(sig[:, n % 2, :], half(gate[:, vt_], f), ACT.Sigmoid).then_inc(s_sg, 1)
                    if u == 0:
                        for m, (d, f) in enumerate(gla_log):
                            act.wait_ge(s_gz, m + 1)
                            nc.scalar.activation(half(fd[:, d], f), pb[m % 2][:], ACT.Identity,
                                                 bias=cols[:, C_BA + d:C_BA + d + 1]).then_inc(s_gx, 1)
                            act.wait_ge(s_gx, m + 1)
                            nc.scalar.activation(half(pre[:, d], f), half(fd[:, d], f), ACT.Abs).then_inc(s_gl1, 1)
                            act.wait_ge(s_gl1, m + 1)
                            nc.scalar.activation(half(pre[:, d], f), half(pre[:, d], f), ACT.Exp, scale=-1.0).then_inc(s_gl2, 1)
                            act.wait_ge(s_gl2, m + 1)
                            nc.scalar.activation(half(pre[:, d], f), half(pre[:, d], f), ACT.Ln, bias=1.0).then_inc(s_gl3, 1)
                        for m, (d, f) in enumerate(gla_log):
                            act.wait_ge(s_gmin, m + 1)
                            nc.scalar.activation(half(fd[:, d], f), half(fd[:, d], f), ACT.Exp,
                                                 scale=1.0 / GATE_TEMP).then_inc(s_gf, 1)
                    for t in range(TT):
                        v_turned.wait(act, (u, t))
                        w = un["nv"] * P
                        nc.scalar.activation(vtok[:, t, 0:w], pb[t % 2][:, 0:w], ACT.Copy).then_inc(v_tok.sem, 1)
                    for d in range(2):
                        for f in range(2):
                            k_turned.wait(act, (u, d, f))
                            if d:
                                U_sum.wait(act, (u, 0, TT - 1))
                            nc.scalar.activation(ktok[:, 4 * f:4 * f + 4, :].rearrange("p t c -> p (t c)"), pb[f][:],
                                                 ACT.Copy).then_inc(k_tok.sem, 1)
                        if d:
                            inter_sum.wait(act, (u, 0, un["nv"] - 1, 1))
                        for t in range(TT):
                            U_sum.wait(act, (u, d, t))
                            nc.scalar.activation(U[:, t * CPT:(t + 1) * CPT, :].rearrange("p n v -> p (n v)"), pu[:, t % 2, :],
                                                 ACT.Copy).then_inc(U_ready.sem, 1)
                    for vt_ in range(un["nv"]):
                        for f in range(2):
                            m = fin_keys.index((u, vt_, f))
                            if vt_ == 0 and f == 0:
                                act.wait_ge(s_done, u + 1)
                            if vt_ or f:
                                fin_sum.wait(act, fin_keys[m - 1])
                            nc.scalar.activation(half(Pq[:, m % 2], f), half(oacc[:, vt_], f), ACT.Square).then_inc(fin_sq.sem, 1)
                    for m, (_, vt_, f) in enumerate(fin_keys):
                        if fin_keys[m][0] == u:
                            fin_y.wait(act, fin_keys[m])
                            act.dma_start(half(y_dram[un["yt"][vt_]], f), ys[:, m % 2, :]).then_inc(s_yo[m % 2], 16)
                for j in range(2):
                    act.wait_ge(s_yo[j], 16 * len(fin_keys) // 2)

            def norms(pool, u):
                for m, key in enumerate(fin_keys):
                    if key[0] == u:
                        pool.wait_ge(s_fm, m + 1)
                        nc.gpsimd.tensor_tensor(tmp[:, m % 2, :], tmp[:, m % 2, :],
                                                K[:, K_NH:K_NH + 1].broadcast_to([P, HALF]), ALU.pow).then_inc(s_fr, 1)

            @block.gpsimd
            def _(pool):
                for u in range(NU):
                    un = units[u]
                    if u:
                        norms(pool, u - 1)
                        inter_sum.wait(pool, inter_keys[[k[0] for k in inter_keys].index(u) - 1])
                        state_ready.wait(pool, (u - 1, 1))
                    for d in range(2):
                        for t in range(TT):
                            v_tok.wait(pool, (u, t))
                            i = list(Vx_ready.order).index((u, d, t))
                            if i:
                                U_sum.wait(pool, ut[i - 1])
                            for h in range(un["heads"]):
                                last = nc.gpsimd.tensor_tensor(
                                    Vx[:, h], vtok[:, t, h * 64:(h + 1) * 64].unsqueeze(1).broadcast_to([P, CPT, 64]),
                                    K[:, K_MASK:K_MASK + CPT].unsqueeze(2).broadcast_to([P, CPT, 64]), ALU.mult)
                            last.then_inc(Vx_ready.sem, 1)
                norms(pool, NU - 1)

            @block.vector
            def _(dve):
                c = Chain(dve, s_chain)
                c.link(nc.vector.tensor_tensor(lb[:, 6:8], cols[:, C_LB + 2:C_LB + 4], cols[:, C_LB:C_LB + 2], ALU.subtract))
                nc.vector.tensor_copy(lb[:, 4:6], lb[:, 6:8]).then_inc(s_lbd, 1)
                dve.wait_ge(s_lbe, 1)
                c.link(nc.vector.tensor_scalar(lb[:, 0:2], lb[:, 0:2], cols[:, C_FLAG:C_FLAG + 1], None, ALU.mult))
                c.link(nc.vector.tensor_scalar(lb[:, 2:4], lb[:, 0:2], -1.0, 1.0, ALU.mult, ALU.add))
                for u in range(NU):
                    un = units[u]
                    for vt_ in range(un["nv"]):
                        for f in range(2):
                            n = list(gate_ready.order).index((u, f"g{vt_}", f))
                            dve.wait_ge(s_sg, n + 1)
                            nc.vector.tensor_tensor(half(gate[:, vt_], f), half(gate[:, vt_], f), sig[:, n % 2, :],
                                                    ALU.mult).then_inc(gate_ready.sem, 1)
                    if u == 0:
                        for m, (d, f) in enumerate(gla_log):
                            dve.wait_ge(s_gl3, m + 1)
                            nc.vector.scalar_tensor_tensor(half(fd[:, d], f), half(fd[:, d], f), 0.0, half(pre[:, d], f),
                                                           ALU.min, ALU.subtract).then_inc(s_gmin, 1)
                        dve.wait_ge(s_gf, 4)
                    else:
                        read_out.wait(dve, (u, "zb", 1))
                        for d in range(2):
                            c.did(nc.vector.tensor_scalar(kd[:, d], kd[:, d], lb[:, 2 + u - 1:3 + u - 1], None, ALU.mult))
                            c.did(nc.vector.tensor_scalar(fd[:, d], fd[:, d], lb[:, 2 + u - 1:3 + u - 1], lb[:, u - 1:u],
                                                          ALU.mult, ALU.add))
                            c.wait()
                            c.link(nc.vector.tensor_scalar(fd[:, d], fd[:, d], F_FLOOR, None, ALU.max))
                    f3 = [by_chunk(fd[:, d]) for d in range(2)]
                    p3 = [by_chunk(pre[:, d]) for d in range(2)]
                    s3 = [by_chunk(suf[:, d]) for d in range(2)]
                    at = lambda d, i: i if d == 0 else CHUNK - 1 - i
                    key = lambda d: kd[:, d if u else 0]
                    for d in range(2):
                        c.did(nc.vector.tensor_copy(p3[d][:, :, at(d, 0)], f3[d][:, :, at(d, 0)]))
                        c.did(nc.vector.memset(s3[d][:, :, at(d, CHUNK - 1)], 1.0))
                    for i in range(1, CHUNK):
                        c.wait()
                        for d in range(2):
                            c.did(nc.vector.tensor_tensor(p3[d][:, :, at(d, i)], p3[d][:, :, at(d, i - 1)],
                                                          f3[d][:, :, at(d, i)], ALU.mult))
                            j = CHUNK - 1 - i
                            c.did(nc.vector.tensor_tensor(s3[d][:, :, at(d, j)], s3[d][:, :, at(d, j + 1)],
                                                          f3[d][:, :, at(d, j + 1)], ALU.mult))
                    c.wait()
                    for d in range(2):
                        nc.vector.tensor_tensor(suf[:, d], suf[:, d], key(d), ALU.mult).then_inc(suf_ready.sem, 1)
                    for d in range(2):
                        spread_query(dve, c, u, d, 0)
                        lags(dve, c, u, d)
                        U_ready.wait(dve, (u, d, TT - 1))
                        for n in range(1, NCH - 1):
                            m, prev = (n, n - 1) if d == 0 else (NCH - 1 - n, NCH - n)
                            g = p3[d][:, m, at(d, CHUNK - 1):at(d, CHUNK - 1) + 1]
                            ins = nc.vector.scalar_tensor_tensor(U[:, m, :], U[:, prev, :], g, U[:, m, :], ALU.mult, ALU.add)
                            if n < NCH - 2:
                                c.link(ins)
                        ins.then_inc(state_ready.sem, 1)
                        for vt_ in range(un["nv"]):
                            if vt_:
                                spread_query(dve, c, u, d, vt_)
                            for f in range(2):
                                m = inter_keys.index((u, d, vt_, f))
                                inter_sum.wait(dve, (u, d, vt_, f))
                                lo, hi = f * HALF, (f + 1) * HALF
                                if d == 0 and f == 0:
                                    lo += CHUNK
                                if d == 1 and f == 1:
                                    hi -= CHUNK
                                c.wait()
                                c.did(nc.vector.tensor_tensor(oacc[:, vt_, lo:hi], oacc[:, vt_, lo:hi],
                                                              pu[:, m % 2, lo - f * HALF:hi - f * HALF], ALU.add))
                                c.wait()
                                dve.sem_inc(inter_read.sem, 1)
                    dve.sem_inc(s_done, 1)
                    for vt_ in range(un["nv"]):
                        gain = cols[:, C_GLAN:C_GLAN + 1] if u == 0 else cols[:, C_HGRNN:C_HGRNN + 1]
                        for f in range(2):
                            m = fin_keys.index((u, vt_, f))
                            fin_sum.wait(dve, (u, vt_, f))
                            t0 = tmp[:, m % 2, :]
                            nc.vector.tensor_scalar(t0, pb[m % 2][:], 1.0 / GLA_DV, EPS, ALU.mult,
                                                    ALU.add).then_inc(s_fm, 1)
                            dve.wait_ge(s_fr, m + 1)
                            c.link(nc.vector.tensor_tensor(t0, t0, half(oacc[:, vt_], f), ALU.mult))
                            if m >= 2:
                                dve.wait_ge(s_yo[m % 2], 16 * (m // 2))
                            nc.vector.scalar_tensor_tensor(ys[:, m % 2, :], t0, gain, half(gate[:, vt_], f),
                                                           ALU.mult, ALU.mult).then_inc(fin_y.sem, 1)


def bass_stack(nc, d, out):
    x_all = nc.dram_tensor("x_layers", [DEPTH + 1, SEQ, D], F32, kind="Internal").ap()
    y_dram = nc.dram_tensor("mixed", [KT, P, SEQ], F32, kind="Internal").ap()
    with ExitStack() as ctx:
        sems = []

        def S(name):
            s = ctx.enter_context(nc.semaphore(name))
            sems.append(s)
            return s

        sb = lambda name, shape, dt=F32: ctx.enter_context(nc.sbuf_tensor(name, shape, dt))
        K = sb("consts", [P, K_N])
        s_k = ctx.enter_context(nc.semaphore("consts_in"))
        s_x0 = ctx.enter_context(nc.semaphore("x_copied"))
        with nc.Block() as block:
            @block.sync
            def _(sp):
                sp.dma_start(x_all[0], d["x"].rearrange("b s d -> (b s) d")).then_inc(s_x0, 16)
                sp.dma_start(K[:], d["consts"]).then_inc(s_k, 16)
                sp.wait_ge(s_k, 16)
                sp.wait_ge(s_x0, 16)

        def w_in(l, off, width):
            return d["w_in"][bass.ds(l, 1), :, off:off + width].rearrange("o (k p) n -> p (o k) n", p=P)

        with nc.Fori(0, DEPTH) as l:
            with ExitStack() as lctx:
                hT = lctx.enter_context(nc.sbuf_tensor("hT", [P, KT, SEQ], F32))
                cols = lctx.enter_context(nc.sbuf_tensor("cols", [P, C_N], F32))
                rows = lctx.enter_context(nc.sbuf_tensor("rows", [P, R_N], F32))
                s_par = S("params")
                start = nc.gpsimd
                mark = len(sems)
                clear_at = nc
                with nc.Block() as block:
                    @block.sync
                    def _(sp):
                        sp.dma_start(cols[:], d["cols"][bass.ds(l, 1)].rearrange("o p n -> p (o n)")).then_inc(s_par, 16)
                        sp.dma_start(rows[:], d["rows"][bass.ds(l, 1)].broadcast_to([P, R_N])).then_inc(s_par, 16)
                        sp.wait_ge(s_par, 32)
                norm_transpose(nc, S, lambda t: x_all[bass.ds(l, 1), t * P:(t + 1) * P, :].rearrange("o p n -> p (o n)"),
                               cols[:, C_PRE:C_PRE + 8], hT, K[:, K_ID:K_ID + P], K[:, K_NH:K_NH + 1], "a_")
                diff_attention(nc, S, l, w_in, hT, y_dram, K, rows)
                gated_scans(nc, S, l, w_in, lambda l: d["wa2"][bass.ds(l, 1)].rearrange("o r n -> r (o n)"), hT, y_dram, K, cols)
                out_project(nc, S, y_dram, d["w_out"][bass.ds(l, 1)].rearrange("o (k p) n -> p (o k) n", p=P),
                            lambda t: x_all[bass.ds(l, 1), t * P:(t + 1) * P, :].rearrange("o p n -> p (o n)"),
                            lambda t: x_all[bass.ds(l + 1, 1), t * P:(t + 1) * P, :].rearrange("o p n -> p (o n)"),
                            rows[:, R_POST:R_POST + D], K[:, K_NH:K_NH + 1], "a_")
                nc.all_engine_barrier()
                for s in sems:
                    nc.gpsimd.sem_clear(s)
                nc.all_engine_barrier()
        return x_all




D_CONV = 512
CT = D_CONV // P
CONV_W, LRU_W, LRU_C = 31, 4, 8.0
N_GROUPS, PER_GROUP = 4, 8
N_EXP = N_GROUPS * PER_GROUP
D_EXP = 512
FT = D_EXP // P
PLE = 256
N_OVER = 2 * SEQ // P
N_SLOTS = (N_EXP + N_OVER) * P
BIG = 1e30

(C2_MIX, C2_CW, C2_CB, C2_LG, C2_LB, C2_LW, C2_LCB, C2_BR, C2_BI, C2_LAM, C2_N) = (
    0, 8, 132, 136, 140, 144, 160, 164, 168, 172, 176)
R2_FFN, R2_B, R2_PLE, R2_PROJ, R2_FIN, R2_N = 0, 1024, 1060, 2084, 3108, 4132
K2_ONE, K2_MEAN, K2_TRI, K2_REV, K2_REVG, K2_E, K2_O, K2_TOK, K2_EPS, K2_N = 0, 128, 256, 384, 416, 420, 452, 468, 476, 477


def mixer(nc, S, w_dram, wr_dram, hT, y_dram, K2, cols, clear_extra):
    order = [(a + str(j), off + P * j) for j in range(CT) for a, off in (("g", D_CONV), ("v", 0))]
    order += [(a + str(j), off + P * j) for j in range(CT) for a, off in (("x", 2 * D_CONV), ("l", 3 * D_CONV))]
    items = [n for n, _ in order]
    banks = [(n, f) for n in items for f in range(2)]
    PAD = CONV_W - 1
    with ExitStack() as ctx:
        sb = lambda name, shape, dt=F32: ctx.enter_context(nc.sbuf_tensor(name, shape, dt))
        wt = sb("mx_w", [P, 4, KT, P])
        wri = sb("mx_wri", [P, 2, CT, P])
        ub = sb("mx_u", [P, CT, PAD + SEQ])
        sg = sb("mx_sg", [P, 2, HALF])
        cb = sb("mx_c", [P, CT, SEQ])
        yo = sb("mx_y", [P, 2, SEQ])
        xb = sb("mx_x", [P, CT, LRU_W - 1 + SEQ])
        gl = sb("mx_gl", [P, CT, SEQ])
        xr = sb("mx_xr", [P, 2, SEQ])
        mu = sb("mx_mu", [P, SEQ])
        ra = sb("mx_r", [P, 2, SEQ])
        th = sb("mx_t", [P, 2, SEQ])
        ia = sb("mx_i", [P, 2, SEQ])
        sp_ = sb("mx_sp", [P, 6, CT])
        pp = [ctx.enter_context(nc.psum_tensor(f"mx_p{i}", [P, HALF], F32)) for i in range(4)]
        pc = ctx.enter_context(nc.psum_tensor("mx_pc", [P, 2, SEQ], F32))
        s_w = [S(f"mx_w{i}") for i in range(4)]
        s_wri, s_clear, s_c = S("mx_wri"), S("mx_clear"), S("mx_chain")
        proj_done = Signal(S("mx_proj"), banks)
        act_read = Signal(S("mx_ar"), [b for b in banks if b[0][0] != "v"])
        u_ready = Signal(S("mx_ur"), [b for b in banks if b[0][0] == "v"])
        tiles = list(range(CT))
        conv_done = Signal(S("mx_cv"), tiles)
        c_ready = Signal(S("mx_cr"), tiles)
        s_mu, s_cen, s_sq, s_var, s_sd, s_rs, s_nrm = (S("mx_mu"), S("mx_cen"), S("mx_sq"), S("mx_var"), S("mx_sd"),
                                                    S("mx_rs"), S("mx_nrm"))
        s_y = [S("mx_y0"), S("mx_y1")]
        y_ready = Signal(S("mx_yr"), [("c", j) for j in tiles] + [("l", j) for j in tiles])
        lconv, xr_ready = Signal(S("mx_lc"), tiles), Signal(S("mx_xr"), tiles)
        gk = [(j, w, f) for j in tiles for w in range(2) for f in range(2)]
        gate_sum, gate_read = Signal(S("mx_gs"), gk), Signal(S("mx_gr"), gk)
        s_sp, s_nl, s_at, s_m, s_rt, s_ly = S("mx_sp"), S("mx_nl"), S("mx_at"), S("mx_m"), S("mx_rt"), S("mx_ly")
        half = lambda ap, f: ap[:, f * HALF:(f + 1) * HALF]

        def read_bank(eng, b):
            (u_ready if b[0][0] == "v" else act_read).wait(eng, b)

        with nc.Block() as block:
            @block.sync
            def _(sp):
                for i, (name, off) in enumerate(order):
                    if i >= 4:
                        proj_done.wait(sp, (items[i - 4], 1))
                    sp.dma_start(wt[:, i % 4], w_dram(off)).then_inc(s_w[i % 4], 16)
                    if i == 3:
                        sp.dma_start(wri[:], wr_dram).then_inc(s_wri, 16)
                clear_extra(sp, s_clear)
                for n, key in enumerate(y_ready.order):
                    y_ready.wait(sp, key)
                    sp.dma_start(y_dram[n], yo[:, n % 2, :]).then_inc(s_y[n % 2], 16)
                for j in range(2):
                    sp.wait_ge(s_y[j], 16 * CT)
                sp.wait_ge(s_clear, 16)

            @block.tensor
            def _(pe):
                for i, (name, _) in enumerate(order):
                    pe.wait_ge(s_w[i % 4], 16 * (i // 4 + 1))
                    for f in range(2):
                        n = 2 * i + f
                        if n >= 4:
                            read_bank(pe, banks[n - 4])
                        for k in range(KT):
                            last = nc.tensor.matmul(pp[n % 4][:], wt[:, i % 4, k, :], half(hT[:, k], f),
                                                    start=(k == 0), stop=(k == KT - 1))
                        last.then_inc(proj_done.sem, 1)
                act_read.all(pe)
                c_ready.all(pe)
                for f in range(2):
                    for j in range(CT):
                        last = nc.tensor.matmul(pp[f][:], K2[:, K2_MEAN:K2_MEAN + P], half(cb[:, j], f),
                                                start=(j == 0), stop=(j == CT - 1))
                    last.then_inc(s_mu, 1)
                for j in range(CT):
                    for f in range(2):
                        pe.wait_ge(s_sq, 2 * j + f + 1)
                        last = nc.tensor.matmul(pp[2 + f][:], K2[:, K2_MEAN:K2_MEAN + P],
                                                half(th[:, j % 2], f), start=(j == 0), stop=(j == CT - 1))
                    last.then_inc(s_var, 1)
                pe.wait_ge(s_sd, 2)
                pe.wait_ge(s_cen, 1)
                pe.wait_ge(s_wri, 16)
                for n, (j, w, f) in enumerate(gk):
                    xr_ready.wait(pe, j)
                    if n >= 4:
                        gate_read.wait(pe, gk[n - 4])
                    nc.tensor.matmul(pp[n % 4][:], wri[:, w, j, :], half(xr[:, j % 2], f), start=True,
                                     stop=True).then_inc(gate_sum.sem, 1)

            @block.scalar
            def _(act):
                for name, _ in order:
                    for f in range(2):
                        n = banks.index((name, f))
                        src = pp[n % 4][:]
                        j = int(name[1])
                        if name[0] == "v":
                            continue
                        proj_done.wait(act, (name, f))
                        if name[0] == "g":
                            if j:
                                u_ready.wait(act, ("v" + str(j - 1), f))
                            ins = nc.scalar.activation(sg[:, f, :], src, ACT.Sigmoid)
                        elif name[0] == "x":
                            ins = nc.scalar.activation(xb[:, j, LRU_W - 1 + f * HALF:LRU_W - 1 + (f + 1) * HALF], src, ACT.Copy)
                        else:
                            ins = nc.scalar.activation(half(gl[:, j], f), src, ACT.Copy)
                        ins.then_inc(act_read.sem, 1)
                for j in tiles:
                    conv_done.wait(act, j)
                    nc.scalar.activation(cb[:, j], pc[:, j % 2], ACT.Identity,
                                         bias=cols[:, C2_CB + j:C2_CB + j + 1]).then_inc(c_ready.sem, 1)
                for j in tiles:
                    act.wait_ge(s_cen, j + 1)
                    if j >= 2:
                        act.wait_ge(s_var, j - 1)
                    for f in range(2):
                        nc.scalar.activation(half(th[:, j % 2], f), half(cb[:, j], f), ACT.Square).then_inc(s_sq, 1)
                act.wait_ge(s_var, CT)
                for f in range(2):
                    nc.scalar.activation(half(mu, f), pp[2 + f][:], ACT.Sqrt, bias=K2[:, K2_EPS:K2_EPS + 1]).then_inc(s_sd, 1)
                for j in tiles:
                    act.wait_ge(s_nrm, j + 1)
                    if j >= 2:
                        act.wait_ge(s_y[j % 2], 16 * (j // 2))
                    nc.scalar.activation(yo[:, j % 2], cb[:, j], ACT.Silu, scale=cols[:, C2_LG + j:C2_LG + j + 1],
                                         bias=cols[:, C2_LB + j:C2_LB + j + 1]).then_inc(y_ready.sem, 1)
                for j in tiles:
                    nc.scalar.activation(gl[:, j], gl[:, j], ACT.Gelu_apprx_tanh).then_inc(s_ly, 1)
                act.wait_ge(s_sp, 1)
                nc.scalar.activation(sp_[:, 1, :], sp_[:, 0, :], ACT.Exp, scale=-1.0).then_inc(s_sp, 1)
                for j in tiles:
                    lconv.wait(act, j)
                    if j >= 2:
                        gate_sum.wait(act, (j - 2, 1, 1))
                        y_ready.wait(act, ("l", j - 2))
                    nc.scalar.activation(xr[:, j % 2], pc[:, j % 2], ACT.Identity,
                                         bias=cols[:, C2_LCB + j:C2_LCB + j + 1]).then_inc(xr_ready.sem, 1)
                    for w in range(2):
                        for f in range(2):
                            n = gk.index((j, w, f))
                            gate_sum.wait(act, (j, w, f))
                            col = (C2_BR, C2_BI)[w] + j
                            nc.scalar.activation(half((ra, ia)[w][:, j % 2], f), pp[n % 4][:], ACT.Sigmoid,
                                                 bias=cols[:, col:col + 1]).then_inc(gate_read.sem, 1)
                    act.wait_ge(s_nl, 1)
                    gate_read.wait(act, (j, 0, 1))
                    nc.scalar.activation(th[:, j % 2], ra[:, j % 2], ACT.Tanh, scale=sp_[:, 5, j:j + 1]).then_inc(s_at, 1)
                    nc.scalar.activation(ra[:, j % 2], ra[:, j % 2], ACT.Exp, scale=sp_[:, 5, j:j + 1]).then_inc(s_at, 1)
                    act.wait_ge(s_m, j + 1)
                    nc.scalar.activation(th[:, j % 2], th[:, j % 2], ACT.Sqrt).then_inc(s_rt, 1)

            @block.vector
            def _(dve):
                c = Chain(dve, s_c)
                c.did(nc.vector.memset(ub[:, :, 0:PAD], 0.0))
                c.did(nc.vector.memset(xb[:, :, 0:LRU_W - 1], 0.0))
                for j in tiles:
                    for f in range(2):
                        b = ("v" + str(j), f)
                        proj_done.wait(dve, b)
                        act_read.wait(dve, ("g" + str(j), f))
                        nc.vector.tensor_tensor(ub[:, j, PAD + f * HALF:PAD + (f + 1) * HALF], pp[banks.index(b) % 4][:],
                                                sg[:, f, :], ALU.mult).then_inc(u_ready.sem, 1)
                    if j % 2 == 0:
                        continue
                    u_ready.wait(dve, b)
                    c.wait()
                    if j > 1:
                        c_ready.wait(dve, j - 2)
                    for tap in range(CONV_W):
                        for jj in (j - 1, j):
                            acc = pc[:, jj % 2]
                            wcol = cols[:, C2_CW + tap * CT + jj:C2_CW + tap * CT + jj + 1]
                            src = ub[:, jj, tap:tap + SEQ]
                            if tap:
                                c.wait(c.n if tap == CONV_W - 1 and jj == j else c.n - 1)
                                ins = nc.vector.scalar_tensor_tensor(acc, src, wcol, acc, ALU.mult, ALU.add)
                            else:
                                ins = nc.vector.tensor_scalar(acc, src, wcol, None, ALU.mult)
                            if tap < CONV_W - 1:
                                c.did(ins)
                            else:
                                ins.then_inc(conv_done.sem, 1)
                lam = cols[:, C2_LAM:C2_LAM + CT]
                c.link(nc.vector.tensor_scalar(sp_[:, 4, :], lam, -1.0, None, ALU.mult))
                nc.vector.tensor_tensor(sp_[:, 0, :], lam, sp_[:, 4, :], ALU.max).then_inc(s_sp, 1)
                c.link(nc.vector.tensor_scalar(sp_[:, 4, :], sp_[:, 4, :], 0.0, None, ALU.max))
                dve.wait_ge(s_mu, 2)
                for j in tiles:
                    c.did(nc.vector.tensor_tensor(half(cb[:, j], 0), half(cb[:, j], 0), pp[0][:], ALU.subtract))
                    c.did(nc.vector.tensor_tensor(half(cb[:, j], 1), half(cb[:, j], 1), pp[1][:], ALU.subtract))
                    c.wait()
                    dve.sem_inc(s_cen, 1)
                dve.wait_ge(s_sd, 2)
                c.link(nc.vector.reciprocal(mu[:], mu[:]))
                for j in tiles:
                    nc.vector.tensor_tensor(cb[:, j], cb[:, j], mu[:], ALU.mult).then_inc(s_nrm, 1)
                dve.wait_ge(s_sp, 2)
                y1, z, z2, s1 = sp_[:, 1, :], sp_[:, 2, :], sp_[:, 3, :], sp_[:, 5, :]
                c.link(nc.vector.tensor_scalar(z2, y1, 2.0, None, ALU.add))
                c.link(nc.vector.reciprocal(z2, z2))
                c.link(nc.vector.tensor_tensor(z, y1, z2, ALU.mult))
                c.link(nc.vector.tensor_tensor(z2, z, z, ALU.mult))
                c.link(nc.vector.memset(s1, 1.0 / 17))
                for n in range(15, 0, -2):
                    c.link(nc.vector.tensor_tensor(s1, s1, z2, ALU.mult))
                    c.link(nc.vector.tensor_scalar(s1, s1, 1.0 / n, None, ALU.add))
                c.link(nc.vector.tensor_tensor(s1, s1, z, ALU.mult))
                c.link(nc.vector.tensor_scalar(s1, s1, 2.0, None, ALU.mult))
                c.link(nc.vector.tensor_tensor(s1, s1, sp_[:, 4, :], ALU.add))
                nc.vector.tensor_scalar(s1, s1, -LRU_C, None, ALU.mult).then_inc(s_nl, 1)

                def short_conv(j):
                    if j >= 2:
                        xr_ready.wait(dve, j - 2)
                    acc = pc[:, j % 2]
                    for tap in range(LRU_W):
                        wcol = cols[:, C2_LW + tap * CT + j:C2_LW + tap * CT + j + 1]
                        src = xb[:, j, tap:tap + SEQ]
                        if tap:
                            c.wait()
                            ins = nc.vector.scalar_tensor_tensor(acc, src, wcol, acc, ALU.mult, ALU.add)
                        else:
                            ins = nc.vector.tensor_scalar(acc, src, wcol, None, ALU.mult)
                        if tap < LRU_W - 1:
                            c.did(ins)
                        else:
                            ins.then_inc(lconv.sem, 1)

                act_read.all(dve)
                short_conv(0)
                for j in tiles:
                    if j + 1 < CT:
                        short_conv(j + 1)
                    dve.wait_ge(s_at, 2 * j + 2)
                    t, i_ = th[:, j % 2], ia[:, j % 2]
                    if j:
                        y_ready.wait(dve, ("l", j - 1))
                    c.link(nc.vector.tensor_scalar(mu[:], t, -1.0, 1.0, ALU.mult, ALU.add))
                    c.link(nc.vector.reciprocal(mu[:], mu[:]))
                    nc.vector.scalar_tensor_tensor(t, t, -2.0, mu[:], ALU.mult, ALU.mult).then_inc(s_m, 1)
                    gate_read.wait(dve, (j, 1, 1))
                    c.link(nc.vector.tensor_tensor(i_, i_, xr[:, j % 2], ALU.mult))
                    dve.wait_ge(s_rt, j + 1)
                    c.link(nc.vector.tensor_tensor(i_, i_, t, ALU.mult))
                    c.link(nc.vector.tensor_tensor_scan(mu[:], ra[:, j % 2], i_, 0.0, ALU.mult, ALU.add))
                    dve.wait_ge(s_ly, j + 1)
                    dve.wait_ge(s_y[j % 2], 16 * (j // 2 + 2))
                    nc.vector.tensor_tensor(yo[:, j % 2], mu[:], gl[:, j], ALU.mult).then_inc(y_ready.sem, 1)


def norm_route(nc, S, x_dram, hf_dram, wr_dram, rows, K, K2, R):
    with ExitStack() as ctx:
        sb = lambda name, shape, dt=F32: ctx.enter_context(nc.sbuf_tensor(name, shape, dt))
        xt = sb("nr_x", [P, 2, D])
        sq = sb("nr_sq", [P, D])
        xn = sb("nr_n", [P, 2, D])
        hT = sb("nr_hT", [P, 2, KT, P])
        ss = sb("nr_ss", [P, TT])
        rstd = sb("nr_r", [P, TT])
        wr = sb("nr_w", [P, KT, N_GROUPS + N_EXP])
        L = sb("nr_L", [P, TT, N_GROUPS + N_EXP])
        ps = ctx.enter_context(nc.psum_tensor("nr_ps", [P, 2, KT, P], F32))
        pl = [ctx.enter_context(nc.psum_tensor(f"nr_pl{i}", [P, HALF], F32)) for i in range(2)]
        pt = [ctx.enter_context(nc.psum_tensor(f"nr_pt{i}", [P, HALF], F32)) for i in range(2)]
        s_x, s_st = [S("nr_x0"), S("nr_x1")], [S("nr_s0"), S("nr_s1")]
        s_w, s_sq, s_rs, s_n, s_t, s_h, s_l, s_L, s_pc, s_c = (S("nr_w"), S("nr_sq"), S("nr_rs"), S("nr_n"), S("nr_t"),
            S("nr_h"), S("nr_l"), S("nr_L"), S("nr_pool"), S("nr_chain"))
        s_a, s_a2, s_M, s_cnt = S("nr_a"), S("nr_a2"), S("nr_M"), S("nr_cnt")
        G = lambda name, *shape: sb("nr_" + name, [P, *shape])
        gm, gs, oh4, em = G("gm", TT), G("gs", TT), G("oh4", TT, 4), G("em", TT, N_EXP)
        oh = G("oh", 2, TT, N_EXP)
        mm, mx, tmp, tmp4, M = G("mm", 2, TT), G("mx", TT), G("tmp", TT, N_EXP), G("tmp4", TT, 4), G("M", TT, N_EXP)
        pos, cum, nb, incl, ex, ob = (G("pos", TT, N_EXP), G("cum", TT + 1, N_EXP), G("nb", N_EXP), G("incl", N_EXP),
                                      G("ex", N_OVER, N_EXP), G("ob", N_OVER + 1))
        one = G("one", N_EXP)
        sl = G("sl", 2, TT)
        gx = G("gx", 4, TT)
        spread = lambda ap, n: ap.unsqueeze(2).broadcast_to([P, TT, n])
        across = lambda ap, n: ap.unsqueeze(1).broadcast_to([P, TT, n])
        with nc.Block() as block:
            @block.sync
            def _(sp):
                sp.dma_start(wr[:], wr_dram).then_inc(s_w, 16)
                for t in range(TT):
                    if t >= 2:
                        sp.wait_ge(s_sq, t - 1)
                        sp.wait_ge(s_n, t - 1)
                    sp.dma_start(xt[:, t % 2, :], x_dram[t * P:(t + 1) * P, :]).then_inc(s_x[t % 2], 16)

            def store(act, t):
                act.wait_ge(s_n, t + 1)
                act.dma_start(hf_dram[t * P:(t + 1) * P, :], xn[:, t % 2, :]).then_inc(s_st[t % 2], 16)

            @block.scalar
            def _(act):
                for t in range(TT):
                    act.wait_ge(s_x[t % 2], 16 * (t // 2 + 1))
                    if t:
                        act.wait_ge(s_sq, t)
                    nc.scalar.activation(sq[:], xt[:, t % 2, :], ACT.Square, accum_out=ss[:, t:t + 1]).then_inc(s_sq, 1)
                    if t:
                        store(act, t - 1)
                store(act, TT - 1)
                act.wait_ge(s_a, 1)
                nc.scalar.activation(tmp4[:], tmp4[:], ACT.Exp).then_inc(s_a2, 1)
                act.wait_ge(s_a, 2)
                nc.scalar.activation(gx[:, 0, :], gx[:, 0, :], ACT.Exp).then_inc(s_a2, 1)
                for j in range(2):
                    act.wait_ge(s_st[j], 16 * TT // 2)

            @block.gpsimd
            def _(pool):
                c = Chain(pool, s_pc)
                for t in range(TT):
                    pool.wait_ge(s_sq, t + 1)
                    rsqrt_of_mean(nc, c, rstd[:, t:t + 1], ss[:, t:t + 1], D, K[:, P:P + 1]).then_inc(s_rs, 1)

            def logits(pe, t):
                if t == 0:
                    pe.wait_ge(s_w, 16)
                pe.wait_ge(s_h, t + 1)
                if t >= 2:
                    pe.wait_ge(s_L, t - 1)
                for k in range(KT):
                    last = nc.tensor.matmul(pl[t % 2][:, 0:36], hT[:, t % 2, k, :], wr[:, k, :], start=(k == 0), stop=(k == KT - 1))
                last.then_inc(s_l, 1)

            @block.tensor
            def _(pe):
                for t in range(TT):
                    pe.wait_ge(s_n, t + 1)
                    if t >= 2:
                        pe.wait_ge(s_h, t - 1)
                    for k in range(KT):
                        last = nc.tensor.transpose(ps[:, t % 2, k, :], xn[:, t % 2, k * P:(k + 1) * P], K[:, K_ID:K_ID + P])
                    last.then_inc(s_t, 1)
                    if t:
                        logits(pe, t - 1)
                logits(pe, TT - 1)
                pe.wait_ge(s_M, 1)
                flat = M[:].rearrange("p t e -> p (t e)")
                nc.tensor.matmul(pt[0][:, 0:TT * N_EXP], K2[:, K2_TRI:K2_TRI + P], flat, start=True, stop=True)
                nc.tensor.matmul(pt[1][:, 0:TT * N_EXP], K2[:, K2_ONE:K2_ONE + P], flat, start=True, stop=True).then_inc(s_cnt, 1)

            def add_bias(dve, t):
                dve.wait_ge(s_l, t + 1)
                nc.vector.tensor_tensor(L[:, t, :], pl[t % 2][:, 0:36], rows[:, R2_B:R2_B + 36], ALU.add).then_inc(s_L, 1)

            @block.vector
            def _(dve):
                c = Chain(dve, s_c)
                for t in range(TT):
                    dve.wait_ge(s_rs, t + 1)
                    dve.wait_ge(s_x[t % 2], 16 * (t // 2 + 1))
                    if t >= 2:
                        dve.wait_ge(s_t, t - 1)
                        dve.wait_ge(s_st[t % 2], 16 * (t // 2))
                    nc.vector.scalar_tensor_tensor(xn[:, t % 2, :], xt[:, t % 2, :], rstd[:, t:t + 1],
                                                   rows[:, R2_FFN:R2_FFN + D], ALU.mult, ALU.mult).then_inc(s_n, 1)
                    dve.wait_ge(s_t, t + 1)
                    if t >= 2:
                        dve.wait_ge(s_l, t - 1)
                    nc.vector.tensor_copy(hT[:, t % 2], ps[:, t % 2]).then_inc(s_h, 1)
                    if t:
                        add_bias(dve, t - 1)
                add_bias(dve, TT - 1)
                dve.wait_ge(s_L, TT)
                V = nc.vector
                gl, el = L[:, :, 0:4], L[:, :, 4:36]
                c.link(V.tensor_reduce(gm[:], gl, AX.X, ALU.max))
                V.tensor_tensor(tmp4[:], gl, spread(gm[:], 4), ALU.subtract).then_inc(s_a, 1)
                c.link(V.tensor_tensor(oh4[:], gl, spread(gm[:], 4), ALU.is_equal))
                c.link(V.tensor_tensor(oh4[:], oh4[:], across(K2[:, K2_REVG:K2_REVG + 4], 4), ALU.mult))
                c.link(V.tensor_reduce(gs[:], oh4[:], AX.X, ALU.max))
                c.link(V.tensor_tensor(oh4[:], across(K2[:, K2_REVG:K2_REVG + 4], 4), spread(gs[:], 4), ALU.is_equal))
                c.link(V.tensor_scalar(oh4[:], oh4[:], BIG, -BIG, ALU.mult, ALU.add))
                for g in range(N_GROUPS):
                    cols8 = slice(g * PER_GROUP, (g + 1) * PER_GROUP)
                    c.did(V.tensor_tensor(em[:, :, cols8], L[:, :, 4 + g * PER_GROUP:4 + (g + 1) * PER_GROUP],
                                          spread(oh4[:, :, g], PER_GROUP), ALU.add))
                c.wait()
                rev = across(K2[:, K2_REV:K2_REV + N_EXP], N_EXP)
                for n in range(2):
                    c.link(V.tensor_reduce(mm[:, n, :], em[:], AX.X, ALU.max))
                    c.link(V.tensor_tensor(tmp[:], em[:], spread(mm[:, n, :], N_EXP), ALU.is_equal))
                    c.link(V.tensor_tensor(tmp[:], tmp[:], rev, ALU.mult))
                    c.link(V.tensor_reduce(mx[:], tmp[:], AX.X, ALU.max))
                    c.link(V.tensor_tensor(oh[:, n], rev, spread(mx[:], N_EXP), ALU.is_equal))
                    if n == 0:
                        c.link(V.tensor_scalar(tmp[:], oh[:, 0], -2 * BIG, None, ALU.mult))
                        c.link(V.tensor_tensor(em[:], em[:], tmp[:], ALU.add))
                V.tensor_tensor(M[:], oh[:, 0], oh[:, 1], ALU.add).then_inc(s_M, 1)
                V.tensor_tensor(gx[:, 0, :], mm[:, 1, :], mm[:, 0, :], ALU.subtract).then_inc(s_a, 1)
                dve.wait_ge(s_a2, 2)
                c.link(V.reduce_sum(gs[:], tmp4[:], AX.X))
                c.link(V.tensor_scalar(gx[:, 1, :], gx[:, 0, :], 1.0, None, ALU.add))
                c.link(V.tensor_tensor(gs[:], gs[:], gx[:, 1, :], ALU.mult))
                c.link(V.reciprocal(R["gates"][:, 0, :], gs[:]))
                c.link(V.tensor_tensor(R["gates"][:, 1, :], R["gates"][:, 0, :], gx[:, 0, :], ALU.mult))
                dve.wait_ge(s_cnt, 1)
                c.link(V.memset(cum[:, 0, :], 0.0))
                for t in range(TT):
                    c.link(V.tensor_tensor(cum[:, t + 1, :], cum[:, t, :], pt[1][:, t * N_EXP:(t + 1) * N_EXP], ALU.add))
                c.link(V.tensor_tensor(pos[:], pt[0][:, 0:TT * N_EXP].rearrange("p (t e) -> p t e", e=N_EXP), cum[:, 0:TT, :],
                                       ALU.add))
                c.did(V.memset(one[:], 1.0))
                c.link(V.tensor_scalar(nb[:], cum[:, TT, :], float(P), None, ALU.is_gt))
                for k in range(2, TT):
                    c.link(V.scalar_tensor_tensor(nb[:], cum[:, TT, :], float(P * k), nb[:], ALU.is_gt, ALU.add))
                c.link(V.tensor_tensor_scan(incl[:], one[:], nb[:], 0.0, ALU.mult, ALU.add))
                c.link(V.tensor_tensor(nb[:], incl[:], nb[:], ALU.subtract))
                c.link(V.tensor_tensor(nb[:], nb[:], K2[:, K2_E:K2_E + N_EXP], ALU.subtract))
                c.link(V.tensor_scalar(nb[:], nb[:], float(N_EXP - 1), float(P), ALU.add, ALU.mult))
                c.link(V.tensor_scalar(tmp[:], pos[:], float(P), None, ALU.is_ge))
                c.link(V.tensor_tensor(tmp[:], tmp[:], across(nb[:], N_EXP), ALU.mult))
                c.link(V.tensor_tensor(pos[:], pos[:], tmp[:], ALU.add))
                c.link(V.tensor_scalar(one[:], K2[:, K2_E:K2_E + N_EXP], float(P), None, ALU.mult))
                c.link(V.tensor_tensor(pos[:], pos[:], across(one[:], N_EXP), ALU.add))
                for n in range(2):
                    c.link(V.tensor_tensor(tmp[:], pos[:], oh[:, n], ALU.mult))
                    c.link(V.reduce_sum(sl[:, n, :], tmp[:], AX.X))
                c.link(V.tensor_copy(R["slots"], sl[:]))
                c.did(V.tensor_copy(ob[:, 0:1], incl[:, N_EXP - 1:N_EXP]))
                c.link(V.tensor_tensor(ex[:], incl[:].unsqueeze(1).broadcast_to([P, N_OVER, N_EXP]),
                                       K2[:, K2_O:K2_O + N_OVER].unsqueeze(2).broadcast_to([P, N_OVER, N_EXP]), ALU.is_le))
                c.link(V.reduce_sum(ob[:, 1:], ex[:], AX.X))
                c.link(V.tensor_scalar(ob[:, 1:], ob[:, 1:], float(N_EXP - 1), None, ALU.min))
                c.link(V.tensor_copy(R["over"], ob[:]))


def token_lists(nc, S, R, tok, idx_dram, idx, K):
    NB = N_SLOTS // P
    with ExitStack() as ctx:
        zero = ctx.enter_context(nc.sbuf_tensor("tl_zero", [NB, P], F32))
        lists = ctx.enter_context(nc.sbuf_tensor("tl_lists", [NB, P], F32))
        ps = ctx.enter_context(nc.psum_tensor("tl_ps", [P, NB], F32))
        s_z, s_zd, s_in, s_t, s_i = S("tl_z"), S("tl_zd"), S("tl_in"), S("tl_t"), S("tl_i")
        s_sc = S("tl_sc")
        by_block = idx_dram.rearrange("(b p) o -> b (p o)", p=P)
        with nc.Block() as block:
            @block.vector
            def _(dve):
                nc.vector.memset(zero[:], 0.0).then_inc(s_z, 1)
                dve.wait_ge(s_t, 1)
                nc.vector.tensor_copy(idx[:], ps[:]).then_inc(s_i, 1)

            @block.sync
            def _(sp):
                sp.wait_ge(s_z, 1)
                sp.dma_start(by_block, zero[:]).then_inc(s_zd, 16)
                sp.wait_ge(s_sc, 16 * 2 * TT)
                sp.dma_start(lists[:], by_block).then_inc(s_in, 16)

            @block.gpsimd
            def _(pool):
                pool.wait_ge(s_zd, 16)
                for n in range(2):
                    for t in range(TT):
                        nc.gpsimd.indirect_dma_start(
                            idx_dram, bass.IndirectOffsetOnAxis(ap=R["slots"][:, n, t:t + 1], axis=0),
                            tok[:, t:t + 1], None).then_inc(s_sc, 16)

            @block.tensor
            def _(pe):
                pe.wait_ge(s_in, 16)
                nc.tensor.transpose(ps[:], lists[:], K[0:NB, K_ID:K_ID + NB]).then_inc(s_t, 1)


def experts(nc, S, w1, w3, w2, hf_dram, y_slots, idx, K):
    with ExitStack() as ctx:
        sb = lambda name, shape, dt=F32: ctx.enter_context(nc.sbuf_tensor(name, shape, dt))
        wa = sb("ex_w13", [P, 2, 2, KT, D_EXP])
        wb = sb("ex_w2", [P, 2, FT, D])
        xe = sb("ex_x", [P, 2, D])
        xT = sb("ex_xT", [P, 2, KT, P])
        sil = sb("ex_s", [P, D_EXP])
        hid = sb("ex_h", [P, D_EXP])
        hidT = sb("ex_hT", [P, 2, FT, P])
        ye = sb("ex_y", [P, 2, D])
        p_x = ctx.enter_context(nc.psum_tensor("ex_px", [P, KT, P], F32))
        p_1 = ctx.enter_context(nc.psum_tensor("ex_p1", [P, D_EXP], F32))
        p_3 = ctx.enter_context(nc.psum_tensor("ex_p3", [P, D_EXP], F32))
        p_t = ctx.enter_context(nc.psum_tensor("ex_pt", [P, FT, P], F32))
        p_y = ctx.enter_context(nc.psum_tensor("ex_py", [P, D], F32))
        s_wa, s_wb = [S("ex_wa0"), S("ex_wa1")], [S("ex_wb0"), S("ex_wb1")]
        s_g, s_o = [S("ex_g0"), S("ex_g1")], [S("ex_o0"), S("ex_o1")]
        x_turned, x_read, h_done, h_act, h_mul, h_turned, h_read, y_done, y_read = (
            S("ex_xt"), S("ex_xr"), S("ex_hd"), S("ex_ha"), S("ex_hm"), S("ex_ht"), S("ex_hr"), S("ex_yd"), S("ex_yr"))
        ident = K[:, K_ID:K_ID + P]
        PAIRS = N_EXP // 2

        with nc.Block() as block:
            @block.sync
            def _(sp):
                def load(e, par, wait):
                    if wait is not None:
                        sp.wait_ge(h_done, wait)
                    for n, w in enumerate((w1, w3)):
                        sp.dma_start(wa[:, par, n], w(e)).then_inc(s_wa[par], 16)
                    if wait is not None:
                        sp.wait_ge(y_done, wait)
                    sp.dma_start(wb[:, par], w2(e)).then_inc(s_wb[par], 16)

                for par in range(2):
                    load(par, par, None)
                with sp.Fori(1, PAIRS) as r:
                    for par in range(2):
                        load(2 * r + par, par, 2 * r + par - 1)

            @block.gpsimd
            def _(pool):
                for e in range(N_EXP):
                    if e >= 2:
                        pool.wait_ge(x_turned, e - 1)
                    nc.gpsimd.indirect_dma_start(xe[:, e % 2, :], None, hf_dram,
                                                 bass.IndirectOffsetOnAxis(ap=idx[:, e:e + 1], axis=0)).then_inc(s_g[e % 2], 16)

            @block.tensor
            def _(pe):
                def turn_x(e, par):
                    pe.wait_ge(s_g[par], 16 * ((e - par) // 2 + 1) if isinstance(e, int) else 8 * (e - par) + 16)
                    if not (isinstance(e, int) and e == 0):
                        pe.wait_ge(x_read, e)
                    for k in range(KT):
                        last = nc.tensor.transpose(p_x[:, k, :], xe[:, par, k * P:(k + 1) * P], ident)
                    last.then_inc(x_turned, 1)

                def first(e, par):
                    pe.wait_ge(s_wa[par], 32 * ((e - par) // 2 + 1) if isinstance(e, int) else 16 * (e - par) + 32)
                    pe.wait_ge(x_read, e + 1)
                    if not (isinstance(e, int) and e == 0):
                        pe.wait_ge(h_mul, e)
                    for n, ps in enumerate((p_1, p_3)):
                        for k in range(KT):
                            last = nc.tensor.matmul(ps[:], xT[:, par, k, :], wa[:, par, n, k, :], start=(k == 0), stop=(k == KT - 1))
                    last.then_inc(h_done, 1)

                def turn_h(e, par):
                    pe.wait_ge(h_mul, e + 1)
                    if not (isinstance(e, int) and e == 0):
                        pe.wait_ge(h_read, e)
                    for k in range(FT):
                        last = nc.tensor.transpose(p_t[:, k, :], hid[:, k * P:(k + 1) * P], ident)
                    last.then_inc(h_turned, 1)

                def second(e, par):
                    pe.wait_ge(s_wb[par], 16 * ((e - par) // 2 + 1) if isinstance(e, int) else 8 * (e - par) + 16)
                    pe.wait_ge(h_read, e + 1)
                    if not (isinstance(e, int) and e == 0):
                        pe.wait_ge(y_read, e)
                    for k in range(FT):
                        for f in range(2):
                            last = nc.tensor.matmul(p_y[:, f * HALF:(f + 1) * HALF], hidT[:, par, k, :],
                                                    wb[:, par, k, f * HALF:(f + 1) * HALF], start=(k == 0), stop=(k == FT - 1))
                    last.then_inc(y_done, 1)

                turn_x(0, 0)
                first(0, 0)
                turn_x(1, 1)
                turn_h(0, 0)

                def middle(e, n):
                    first(e, n % 2)
                    turn_x(e + 1, (n + 1) % 2)
                    second(e - 1, (n + 1) % 2)
                    turn_h(e, n % 2)

                middle(1, 1)
                middle(2, 2)
                with pe.Fori(1, PAIRS - 1) as r:
                    for n in range(1, 3):
                        middle(2 * r + n, n)
                first(N_EXP - 1, 1)
                second(N_EXP - 2, 0)
                turn_h(N_EXP - 1, 1)
                second(N_EXP - 1, 1)

            @block.scalar
            def _(act):
                def copy_x(e, par, later):
                    act.wait_ge(x_turned, e + 1)
                    if later:
                        act.wait_ge(h_done, e - 1)
                    nc.scalar.activation(xT[:, par], p_x[:], ACT.Copy).then_inc(x_read, 1)

                def silu(e, later):
                    act.wait_ge(h_done, e + 1)
                    if later:
                        act.wait_ge(h_mul, e)
                    nc.scalar.activation(sil[:], p_1[:], ACT.Silu).then_inc(h_act, 1)

                def copy_h(e, par, later):
                    act.wait_ge(h_turned, e + 1)
                    if later:
                        act.wait_ge(y_done, e - 1)
                    nc.scalar.activation(hidT[:, par], p_t[:], ACT.Copy).then_inc(h_read, 1)

                def store(e, par):
                    act.wait_ge(y_read, e + 1)
                    act.dma_start(y_slots(e), ye[:, par]).then_inc(s_o[par], 16)

                def middle(e, n):
                    later = not isinstance(e, int) or e >= 2
                    silu(e, True)
                    copy_x(e + 1, (n + 1) % 2, True)
                    copy_h(e, n % 2, later)
                    store(e - 1, (n + 1) % 2)

                copy_x(0, 0, False)
                silu(0, False)
                copy_x(1, 1, False)
                copy_h(0, 0, False)
                middle(1, 1)
                middle(2, 2)
                with act.Fori(1, PAIRS - 1) as r:
                    for n in range(1, 3):
                        middle(2 * r + n, n)
                silu(N_EXP - 1, True)
                copy_h(N_EXP - 1, 1, True)
                store(N_EXP - 2, 0)
                store(N_EXP - 1, 1)
                for j in range(2):
                    act.wait_ge(s_o[j], 16 * PAIRS)

            @block.vector
            def _(dve):
                def steps(e, par, later):
                    dve.wait_ge(h_act, e + 1)
                    if later:
                        dve.wait_ge(h_turned, e)
                    nc.vector.tensor_tensor(hid[:], p_3[:], sil[:], ALU.mult).then_inc(h_mul, 1)

                def result(e, par, later):
                    dve.wait_ge(y_done, e + 1)
                    if later:
                        dve.wait_ge(s_o[par], 8 * (e - par))
                    nc.vector.tensor_copy(ye[:, par], p_y[:]).then_inc(y_read, 1)

                steps(0, 0, False)
                steps(1, 1, True)
                result(0, 0, False)
                steps(2, 0, True)
                result(1, 1, False)
                with dve.Fori(1, PAIRS - 1) as r:
                    for n in range(1, 3):
                        e = 2 * r + n
                        steps(e, n % 2, True)
                        result(e - 1, (n + 1) % 2, True)
                steps(N_EXP - 1, 1, True)
                result(N_EXP - 2, 0, True)
                result(N_EXP - 1, 1, True)


def extra_blocks(nc, S, sems, w1, w3, w2, hf_dram, y_slots, idx, K, over):
    with ExitStack() as ctx:
        sb = lambda name, shape, dt=F32: ctx.enter_context(nc.sbuf_tensor(name, shape, dt))
        wa = sb("xb_w13", [P, 2, KT, D_EXP])
        wb = sb("xb_w2", [P, FT, D])
        xe = sb("xb_x", [P, D])
        xT = sb("xb_xT", [P, KT, P])
        sil = sb("xb_s", [P, D_EXP])
        hidT = sb("xb_hT", [P, FT, P])
        ye = sb("xb_y", [P, D])
        col = sb("xb_i", [P, 1], I32)
        p_x = ctx.enter_context(nc.psum_tensor("xb_px", [P, KT, P], F32))
        p_1 = ctx.enter_context(nc.psum_tensor("xb_p1", [P, D_EXP], F32))
        p_3 = ctx.enter_context(nc.psum_tensor("xb_p3", [P, D_EXP], F32))
        p_t = ctx.enter_context(nc.psum_tensor("xb_pt", [P, FT, P], F32))
        p_y = ctx.enter_context(nc.psum_tensor("xb_py", [P, D], F32))
        first_sem = len(sems)
        s_w, s_i, s_t, s_r, s_h, s_a, s_m, s_y, s_e, s_o = (S("xb_w"), S("xb_i"), S("xb_t"), S("xb_r"), S("xb_h"),
                                                            S("xb_a"), S("xb_m"), S("xb_y"), S("xb_e"), S("xb_o"))
        s_g = ctx.enter_context(nc.semaphore("xb_gathered"))
        ident = K[:, K_ID:K_ID + P]
        n_over = nc.values_load(over[0:1, 0:1], min_val=0, max_val=N_OVER)
        with nc.If(n_over > 0):
            with nc.Fori(0, N_OVER) as o:
                with nc.If(n_over > o):
                    with nc.Block() as block:
                        @block.sync
                        def _(sp):
                            e = sp.value_load(over[0:1, bass.ds(o + 1, 1)], min_val=0, max_val=N_EXP - 1)
                            for n, w in enumerate((w1, w3)):
                                sp.dma_start(wa[:, n], w(e)).then_inc(s_w, 16)
                            sp.dma_start(wb[:], w2(e)).then_inc(s_w, 16)
                            sp.wait_ge(s_e, 1)
                            sp.dma_start(y_slots(o + N_EXP), ye[:]).then_inc(s_o, 16)
                            sp.wait_ge(s_o, 16)

                        @block.gpsimd
                        def _(pool):
                            pool.wait_ge(s_i, 1)
                            nc.gpsimd.indirect_dma_start(xe[:], None, hf_dram,
                                                         bass.IndirectOffsetOnAxis(ap=col[:], axis=0)).then_inc(s_g, 16)

                        @block.tensor
                        def _(pe):
                            pe.wait_ge(s_g, 16 * o + 16)
                            for k in range(KT):
                                last = nc.tensor.transpose(p_x[:, k, :], xe[:, k * P:(k + 1) * P], ident)
                            last.then_inc(s_t, 1)
                            pe.wait_ge(s_w, 48)
                            pe.wait_ge(s_r, 1)
                            for n, ps in enumerate((p_1, p_3)):
                                for k in range(KT):
                                    last = nc.tensor.matmul(ps[:], xT[:, k, :], wa[:, n, k, :], start=(k == 0), stop=(k == KT - 1))
                            last.then_inc(s_h, 1)
                            pe.wait_ge(s_m, 1)
                            for k in range(FT):
                                last = nc.tensor.transpose(p_t[:, k, :], sil[:, k * P:(k + 1) * P], ident)
                            last.then_inc(s_t, 1)
                            pe.wait_ge(s_r, 2)
                            for k in range(FT):
                                for f in range(2):
                                    last = nc.tensor.matmul(p_y[:, f * HALF:(f + 1) * HALF], hidT[:, k, :],
                                                            wb[:, k, f * HALF:(f + 1) * HALF], start=(k == 0), stop=(k == FT - 1))
                            last.then_inc(s_y, 1)

                        @block.scalar
                        def _(act):
                            act.wait_ge(s_t, 1)
                            nc.scalar.activation(xT[:], p_x[:], ACT.Copy).then_inc(s_r, 1)
                            act.wait_ge(s_h, 1)
                            nc.scalar.activation(sil[:], p_1[:], ACT.Silu).then_inc(s_a, 1)
                            act.wait_ge(s_t, 2)
                            nc.scalar.activation(hidT[:], p_t[:], ACT.Copy).then_inc(s_r, 1)

                        @block.vector
                        def _(dve):
                            nc.vector.tensor_copy(col[:], idx[:, bass.ds(o + N_EXP, 1)]).then_inc(s_i, 1)
                            dve.wait_ge(s_a, 1)
                            nc.vector.tensor_tensor(sil[:], p_3[:], sil[:], ALU.mult).then_inc(s_m, 1)
                            dve.wait_ge(s_y, 1)
                            nc.vector.tensor_copy(ye[:], p_y[:]).then_inc(s_e, 1)
                    nc.all_engine_barrier()
                    for s in sems[first_sem:]:
                        nc.gpsimd.sem_clear(s)
                    nc.all_engine_barrier()


def finish(nc, S, x_dram, p_dram, w_ple, w_gate, y_dram, out_dram, R, rows, K):
    KP = PLE // P
    with ExitStack() as ctx:
        sb = lambda name, shape, dt=F32: ctx.enter_context(nc.sbuf_tensor(name, shape, dt))
        wg = sb("fn_wg", [P, KT, D])
        wp = sb("fn_wp", [P, KP, D])
        xt = sb("fn_x", [P, 2, D])
        pt_ = sb("fn_p", [P, 2, PLE])
        pT = sb("fn_pT", [P, 2, KP, P])
        y = sb("fn_y", [P, 2, 2, D])
        xn = sb("fn_n", [P, D])
        xT = sb("fn_xT", [P, 2, KT, P])
        em = sb("fn_e", [P, D])
        sg = sb("fn_s", [P, D])
        fo = sb("fn_o", [P, 2, D])
        sq = sb("fn_sq", [P, D])
        ss = sb("fn_ss", [P, 3, TT])
        rs = sb("fn_rs", [P, 3, TT])
        p_t = ctx.enter_context(nc.psum_tensor("fn_pt", [P, KT, P], F32))
        p_g = ctx.enter_context(nc.psum_tensor("fn_pg", [P, D], F32))
        p_e = ctx.enter_context(nc.psum_tensor("fn_pe", [P, D], F32))
        p_p = ctx.enter_context(nc.psum_tensor("fn_pp", [P, HALF], F32))
        s_w = S("fn_w")
        two = lambda n: [S(f"fn_{n}0"), S(f"fn_{n}1")]
        s_x, s_p, s_y, s_o = two("x"), two("p"), [ctx.enter_context(nc.semaphore(f"fn_y{i}")) for i in range(2)], two("o")
        (s_ad, s_sq, s_rs, s_n, s_t, s_r, s_g, s_sg, s_pt, s_pr, s_e, s_er, s_x5, s_f, s_c, s_pc) = (
            S("fn_" + n) for n in ("ad", "sq", "rs", "n", "t", "r", "g", "sg", "pt", "pr", "e", "er", "x5", "f", "c", "pc"))
        ident = K[:, K_ID:K_ID + P]
        with nc.Block() as block:
            @block.sync
            def _(sp):
                sp.dma_start(wp[:], w_ple).then_inc(s_w, 16)
                for t in range(TT):
                    if t >= 2:
                        sp.wait_ge(s_pt, t - 1)
                    sp.dma_start(pt_[:, t % 2], p_dram[t * P:(t + 1) * P, :]).then_inc(s_p[t % 2], 16)
                    if t >= 2:
                        sp.wait_ge(s_f, t - 1)
                    sp.dma_start(xt[:, t % 2], x_dram[t * P:(t + 1) * P, :]).then_inc(s_x[t % 2], 16)
                    if t == 0:
                        sp.dma_start(wg[:], w_gate).then_inc(s_w, 16)

            @block.gpsimd
            def _(pool):
                c = Chain(pool, s_pc)
                half_ = K[:, P:P + 1]

                def gather(t):
                    if t >= 2:
                        pool.wait_ge(s_ad, t - 1)
                    for n in range(2):
                        nc.gpsimd.indirect_dma_start(y[:, t % 2, n, :], None, y_dram, bass.IndirectOffsetOnAxis(
                            ap=R["slots"][:, n, t:t + 1], axis=0)).then_inc(s_y[t % 2], 16)

                gather(0)
                gather(1)
                for t in range(TT):
                    for n in range(3):
                        pool.wait_ge(s_sq, 3 * t + n + 1)
                        rsqrt_of_mean(nc, c, rs[:, n, t:t + 1], ss[:, n, t:t + 1], D, half_).then_inc(s_rs, 1)
                    if t + 2 < TT:
                        gather(t + 2)

            @block.tensor
            def _(pe):
                for t in range(TT):
                    pe.wait_ge(s_p[t % 2], 16 * (t // 2 + 1))
                    if t:
                        pe.wait_ge(s_pr, t)
                    for k in range(KP):
                        last = nc.tensor.transpose(p_p[:, k * P:(k + 1) * P], pt_[:, t % 2, k * P:(k + 1) * P], ident)
                    last.then_inc(s_pt, 1)
                    pe.wait_ge(s_pr, t + 1)
                    if t == 0:
                        pe.wait_ge(s_w, 32)
                    if t:
                        pe.wait_ge(s_er, t)
                    for k in range(KP):
                        for f in range(2):
                            last = nc.tensor.matmul(p_e[:, f * HALF:(f + 1) * HALF], pT[:, t % 2, k, :],
                                                    wp[:, k, f * HALF:(f + 1) * HALF], start=(k == 0), stop=(k == KP - 1))
                    last.then_inc(s_e, 1)
                    pe.wait_ge(s_n, t + 1)
                    if t:
                        pe.wait_ge(s_r, t)
                    for k in range(KT):
                        last = nc.tensor.transpose(p_t[:, k, :], xn[:, k * P:(k + 1) * P], ident)
                    last.then_inc(s_t, 1)
                    pe.wait_ge(s_r, t + 1)
                    if t:
                        pe.wait_ge(s_sg, t)
                    for k in range(KT):
                        for f in range(2):
                            last = nc.tensor.matmul(p_g[:, f * HALF:(f + 1) * HALF], xT[:, t % 2, k, :],
                                                    wg[:, k, f * HALF:(f + 1) * HALF], start=(k == 0), stop=(k == KT - 1))
                    last.then_inc(s_g, 1)

            @block.scalar
            def _(act):
                def square(src, n, t):
                    if n + t:
                        act.wait_ge(s_sq, 3 * t + n)
                    nc.scalar.activation(sq[:], src, ACT.Square, accum_out=ss[:, n, t:t + 1]).then_inc(s_sq, 1)

                def store(t):
                    act.wait_ge(s_f, t + 1)
                    act.dma_start(out_dram[t * P:(t + 1) * P, :], fo[:, t % 2]).then_inc(s_o[t % 2], 16)

                for t in range(TT):
                    act.wait_ge(s_pt, t + 1)
                    nc.scalar.activation(pT[:, t % 2].rearrange("p k c -> p (k c)"), p_p[:, 0:PLE], ACT.Copy).then_inc(s_pr, 1)
                    act.wait_ge(s_e, t + 1)
                    square(p_e[:], 0, t)
                    act.wait_ge(s_ad, t + 1)
                    square(xt[:, t % 2], 1, t)
                    if t:
                        store(t - 1)
                    act.wait_ge(s_t, t + 1)
                    nc.scalar.activation(xT[:, t % 2], p_t[:], ACT.Copy).then_inc(s_r, 1)
                    act.wait_ge(s_g, t + 1)
                    if t:
                        act.wait_ge(s_x5, t)
                    nc.scalar.activation(sg[:], p_g[:], ACT.Sigmoid).then_inc(s_sg, 1)
                    act.wait_ge(s_x5, t + 1)
                    square(xt[:, t % 2], 2, t)
                store(TT - 1)
                for j in range(2):
                    act.wait_ge(s_o[j], 16 * TT // 2)

            @block.vector
            def _(dve):
                c = Chain(dve, s_c)
                V = nc.vector
                for t in range(TT):
                    x = xt[:, t % 2]
                    dve.wait_ge(s_x[t % 2], 16 * (t // 2 + 1))
                    dve.wait_ge(s_y[t % 2], 32 * (t // 2 + 1))
                    c.link(V.scalar_tensor_tensor(x, y[:, t % 2, 0], R["gates"][:, 0, t:t + 1], x, ALU.mult, ALU.add))
                    V.scalar_tensor_tensor(x, y[:, t % 2, 1], R["gates"][:, 1, t:t + 1], x, ALU.mult, ALU.add).then_inc(s_ad, 1)
                    dve.wait_ge(s_rs, 3 * t + 1)
                    V.scalar_tensor_tensor(em[:], p_e[:], rs[:, 0, t:t + 1], rows[:, R2_PROJ:R2_PROJ + D],
                                           ALU.mult, ALU.mult).then_inc(s_er, 1)
                    dve.wait_ge(s_ad, t + 1)
                    dve.wait_ge(s_rs, 3 * t + 2)
                    if t:
                        dve.wait_ge(s_t, t)
                    V.scalar_tensor_tensor(xn[:], x, rs[:, 1, t:t + 1], rows[:, R2_PLE:R2_PLE + D],
                                           ALU.mult, ALU.mult).then_inc(s_n, 1)
                    dve.wait_ge(s_sg, t + 1)
                    dve.wait_ge(s_er, t + 1)
                    c.link(V.tensor_tensor(em[:], em[:], sg[:], ALU.mult))
                    V.tensor_tensor(x, x, em[:], ALU.add).then_inc(s_x5, 1)
                    dve.wait_ge(s_x5, t + 1)
                    dve.wait_ge(s_rs, 3 * t + 3)
                    if t >= 2:
                        dve.wait_ge(s_o[t % 2], 16 * (t // 2))
                    V.scalar_tensor_tensor(fo[:, t % 2], x, rs[:, 2, t:t + 1], rows[:, R2_FIN:R2_FIN + D],
                                           ALU.mult, ALU.mult).then_inc(s_f, 1)


def second_block(nc, d, x_dram, out):
    hf = nc.dram_tensor("hf", [SEQ, D], F32, kind="Internal").ap()
    x3 = nc.dram_tensor("x_mixed", [SEQ, D], F32, kind="Internal").ap()
    y_mix = nc.dram_tensor("mixed2", [KT, P, SEQ], F32, kind="Internal").ap()
    idx_dram = nc.dram_tensor("slot_tokens", [N_SLOTS, 1], F32, kind="Internal").ap()
    y_slots = nc.dram_tensor("slot_results", [N_SLOTS, D], F32, kind="Internal").ap()
    tile_of = lambda ap: (lambda t: ap[t * P:(t + 1) * P, :])
    with ExitStack() as ctx:
        sems = []

        def S(name):
            s = ctx.enter_context(nc.semaphore(name))
            sems.append(s)
            return s

        sb = lambda c, name, shape, dt=F32: c.enter_context(nc.sbuf_tensor(name, shape, dt))
        K2 = sb(ctx, "consts2", [P, K2_N])
        K = sb(ctx, "consts_b", [P, P + 1])
        R = {"slots": sb(ctx, "slots", [P, 2, TT], I32)[:], "gates": sb(ctx, "gates", [P, 2, TT])[:],
             "over": sb(ctx, "over", [P, 1 + N_OVER], I32)[:]}
        idx = sb(ctx, "slot_idx", [P, N_SLOTS // P], I32)
        cols = sb(ctx, "cols2", [P, C2_N])
        s_par = S("params2")
        minus_half = K[:, P:P + 1]
        zero = sb(ctx, "zero_row", [P, D])
        s_zero = S("zero_set")
        slot_rows = y_slots.rearrange("(b p) n -> b p n", p=P)

        def clear_extra(sp, sem):
            sp.dma_start(slot_rows[N_EXP:].rearrange("b p n -> p b n"),
                         zero[:].unsqueeze(1).broadcast_to([P, N_OVER, D])).then_inc(sem, 16)

        with nc.Block() as block:
            @block.sync
            def _(sp):
                sp.dma_start(K2[:], d["consts2"]).then_inc(s_par, 16)
                sp.dma_start(K[:], d["consts_b"]).then_inc(s_par, 16)
                sp.dma_start(cols[:], d["cols2"]).then_inc(s_par, 16)
                sp.wait_ge(s_par, 48)
                sp.wait_ge(s_zero, 1)

            @block.gpsimd
            def _(pool):
                nc.gpsimd.memset(zero[:], 0.0).then_inc(s_zero, 1)
        with ExitStack() as m:
            hT = sb(m, "hT2", [P, KT, SEQ])
            norm_transpose(nc, S, tile_of(x_dram), cols[:, C2_MIX:C2_MIX + 8], hT, K[:, K_ID:K_ID + P], minus_half, "b_")
            w = d["w_in_2"]
            mixer(nc, S, lambda off: w[:, off:off + P].rearrange("(k p) n -> p k n", p=P), d["wri"], hT, y_mix, K2, cols,
                  clear_extra)
        out_project(nc, S, y_mix, d["w_out_2"].rearrange("(k p) n -> p k n", p=P), tile_of(x_dram), tile_of(x3), None,
                    minus_half, "b_")
        with ExitStack() as m:
            rows = sb(m, "rows2", [P, R2_N])
            s_r = S("rows2_in")
            with nc.Block() as block:
                @block.sync
                def _(sp):
                    sp.dma_start(rows[:], d["rows2"].broadcast_to([P, R2_N])).then_inc(s_r, 16)
                    sp.wait_ge(s_r, 16)
            norm_route(nc, S, x3, hf, d["w_route"].rearrange("(k p) n -> p k n", p=P), rows, K, K2, R)
            token_lists(nc, S, R, K2[:, K2_TOK:K2_TOK + TT], idx_dram, idx, K)
        one = lambda w, e, split: w[bass.ds(e, 1)].rearrange("o (k p) n -> p (o k) n", p=P)
        w1 = lambda e: one(d["w1"], e, KT)
        w3 = lambda e: one(d["w3"], e, KT)
        w2 = lambda e: one(d["w2"], e, FT)
        slots = lambda b: slot_rows[bass.ds(b, 1)].rearrange("o p n -> p (o n)")
        experts(nc, S, w1, w3, w2, hf, slots, idx, K)
        extra_blocks(nc, S, sems, w1, w3, w2, hf, slots, idx, K, R["over"])
        with ExitStack() as m:
            rows = sb(m, "rows3", [P, R2_N])
            s_r = S("rows3_in")
            with nc.Block() as block:
                @block.sync
                def _(sp):
                    sp.dma_start(rows[:], d["rows2"].broadcast_to([P, R2_N])).then_inc(s_r, 16)
                    sp.wait_ge(s_r, 16)
            finish(nc, S, x3, d["p_2"], d["w_ple"].rearrange("(k p) n -> p k n", p=P),
                   d["w_gate"].rearrange("(k p) n -> p k n", p=P), y_slots, out, R, rows, K)
def constants():
    c = np.zeros((P, K_N), np.float32)
    i = np.arange(P)
    c[i, K_ID + i] = 1
    c[:, K_NH] = -0.5
    for j in range(P):
        if j % 64 < 32:
            c[j + 32, K_ROT + j] = -1
        else:
            c[j - 32, K_ROT + j] = 1
    for m in range(P):
        c[:, K_G0 + m] = i // 32 == m // 64
        c[:, K_G1 + m] = i // 32 == 2 + m // 64
        c[:, K_H + m] = i // 64 == m // 64
    for j in range(CPT):
        c[:, K_MASK + j] = i // CHUNK == j
    inv = (np.float32(ROPE_THETA) ** (-np.arange(0, DIFF_HD, 2, dtype=np.float32) / np.float32(DIFF_HD))).astype(np.float32)
    ang = np.arange(SEQ, dtype=np.float32)[:, None] * inv[None, :]
    c[:, K_COS:K_COS + SEQ] = np.cos(ang).T[i % 32]
    c[:, K_SIN:K_SIN + SEQ] = np.sin(ang).T[i % 32]
    return c


def constants2():
    c = np.zeros((P, K2_N), np.float32)
    i = np.arange(P)
    c[:, K2_ONE:K2_ONE + P] = 1
    c[:, K2_MEAN:K2_MEAN + P] = 1.0 / D_CONV
    c[:, K2_TRI:K2_TRI + P] = i[:, None] < i[None, :]
    c[:, K2_REV:K2_REV + N_EXP] = N_EXP - np.arange(N_EXP)
    c[:, K2_REVG:K2_REVG + N_GROUPS] = N_GROUPS - np.arange(N_GROUPS)
    c[:, K2_E:K2_E + N_EXP] = np.arange(N_EXP)
    c[:, K2_O:K2_O + N_OVER] = np.arange(N_OVER)
    c[:, K2_TOK:K2_TOK + TT] = np.arange(TT) * P + i[:, None]
    c[:, K2_EPS] = EPS
    return c


def kernel(**inputs):
    import concourse.bacc as bacc
    from concourse.bass_utils import run_bass_kernel_spmd

    a = {k: np.asarray(v) for k, v in inputs.items()}
    wide = lambda v: np.ascontiguousarray(v.reshape(-1, P).T)
    per_layer, rows, wa2 = [], [], []
    for l in range(DEPTH):
        per_layer.append(np.concatenate([
            wide(a["norm_pre"][l]), wide(a["gla_ba_fwd"][l]), wide(a["gla_ba_bwd"][l]),
            wide(np.concatenate([a["gla_norm"][l]] * 2)), wide(np.concatenate([a["hgrn_norm"][l]] * 2)),
            wide(a["hgrn_lb_logits"][0]), wide(a["hgrn_lb_logits"][1]), np.full((P, 1), float(l), np.float32)], axis=1))
        li = 0.8 - 0.6 * math.exp(-0.3 * l)
        rows.append(np.concatenate([a["norm_post"][l], a["diff_norm"][l], a["diff_lq1"][l], a["diff_lk1"][l],
                                    a["diff_lq2"][l], a["diff_lk2"][l], np.array([li, 1.0 - li], np.float32)]))
        z = np.zeros((GLA_RANK, P), np.float32)
        wa2.append(np.concatenate([np.concatenate([a["gla_wa2_fwd"][l], z], 1),
                                   np.concatenate([z, a["gla_wa2_bwd"][l]], 1)], 0))
    given = {"x": a["x"], "w_in": a["w_in"], "w_out": a["w_out"], "cols": np.stack(per_layer), "rows": np.stack(rows),
             "wa2": np.stack(wa2), "consts": constants()}
    by_tap = lambda w: np.concatenate([wide(row) for row in w], axis=1)
    one = {k[:-2]: v[0] for k, v in a.items() if k.endswith("_2") and v.shape[0] == 1}
    given["cols2"] = np.concatenate([
        wide(one["g_mix"]), by_tap(one["conv_dw_w"]), wide(one["conv_dw_b"]), wide(one["conv_ln_g"]), wide(one["conv_ln_b"]),
        by_tap(one["lru_conv_w"]), wide(one["lru_conv_b"]), wide(one["lru_b_r"]), wide(one["lru_b_i"]),
        wide(one["lru_lambda"])], axis=1)
    wri = np.zeros((P, 2, CT, P), np.float32)
    for n, name in enumerate(("lru_w_r", "lru_w_i")):
        for h in range(2 * CT):
            wri[64 * (h % 2):64 * (h % 2) + 64, n, h // 2, 64 * (h % 2):64 * (h % 2) + 64] = one[name][h]
    given["wri"] = wri
    given["rows2"] = np.concatenate([one["g_ffn"], one["b_group"], one["b_expert"], one["g_ple"], one["g_ple_proj"],
                                     a["g_final_2"]])[None, :]
    given["w_route"] = np.concatenate([one["w_group"], one["w_expert"]], axis=1)
    given["consts2"] = constants2()
    given["consts_b"] = np.concatenate([given["consts"][:, :P], np.full((P, 1), -0.5, np.float32)], axis=1)
    given.update(w_in_2=one["w_in"], w_out_2=one["w_out"], w1=one["w1"], w3=one["w3"], w2=one["w2"], w_ple=one["w_ple"],
                 w_gate=one["w_ple_gate"], p_2=one["p"][0])
    given = {k: np.ascontiguousarray(v) for k, v in given.items()}
    nc = bacc.Bacc("TRN2", target_bir_lowering=False, num_devices=1)
    d = {k: nc.dram_tensor(f"in_{k}", v.shape, mybir.dt.from_np(v.dtype), kind="ExternalInput").ap() for k, v in given.items()}
    out = nc.dram_tensor("out_0", (1, SEQ, D), F32, kind="ExternalOutput").ap()
    x_all = bass_stack(nc, d, out)
    second_block(nc, d, x_all[DEPTH], out.rearrange("b s d -> (b s) d"))
    r = run_bass_kernel_spmd(nc, [{f"in_{k}": v for k, v in given.items()}], core_ids=[0])
    return r.results[0]["out_0"]
```

```python
from contextlib import ExitStack
import math

import numpy as np

import concourse.bass as bass
from concourse import mybir

F32 = mybir.dt.float32
I32 = mybir.dt.int32
U32 = mybir.dt.uint32
ALU = mybir.AluOpType
ACT = mybir.ActivationFunctionType
AX = mybir.AxisListType

P = 128
D = 1024
SEQ = 1024
DEPTH = 2
KT = D // P
TT = SEQ // P
HALF = 512
EPS = 1e-6
F_FLOOR = 1e-30

GLA_HEADS, GLA_DK, GLA_DV, GLA_RANK, GATE_TEMP = 4, 32, 64, 16, 16.0
DIFF_HEADS, DIFF_HD = 4, 64
HGRN_HEADS, HGRN_DK = 4, 64
CHUNK = 16
NCH = SEQ // CHUNK
CPT = P // CHUNK
IN_SIZES = (128, 128, 256, 256, 16, 16, 512, 512, 512, 512, 256, 256, 256, 256, 256)
IN_OFF = [sum(IN_SIZES[:i]) for i in range(len(IN_SIZES) + 1)]
IN_W = IN_OFF[-1]
(GQ, GK, GV, GG, GAF, GAB, DQ, DK, DV, DG, HQ, HZF, HZB, HI, HG) = IN_OFF[:-1]
ROPE_THETA = 10000.0

C_PRE, C_BA, C_GLAN, C_HGRNN, C_LB, C_FLAG, C_N = 0, 8, 10, 11, 12, 16, 17
R_POST, R_DN, R_LQ, R_LINIT, R_N = 0, 1024, 1152, 1408, 1410
K_ID, K_ROT, K_G0, K_G1, K_H, K_MASK, K_COS, K_SIN = 0, 128, 256, 384, 512, 640, 648, 1672
K_NH, K_EPS, K_MASKB = 2696, 2697, 2698
K_N = 2706


class Signal:

    def __init__(self, sem, keys):
        self.sem = sem
        self.order = {k: n + 1 for n, k in enumerate(keys)}

    def wait(self, eng, key):
        eng.wait_ge(self.sem, self.order[key])

    def all(self, eng):
        eng.wait_ge(self.sem, len(self.order))


class Chain:

    def __init__(self, eng, sem):
        self.eng, self.sem, self.n = eng, sem, 0

    def did(self, ins):
        self.n += 1
        ins.then_inc(self.sem, 1)
        return self.n

    def wait(self, n=None):
        self.eng.wait_ge(self.sem, self.n if n is None else n)

    def link(self, ins):
        self.did(ins)
        self.wait()


def rsqrt_of_mean(nc, chain, out, total, n, minus_half):
    chain.link(nc.gpsimd.tensor_scalar(out, total, 1.0 / n, EPS, ALU.mult, ALU.add))
    return nc.gpsimd.tensor_tensor(out, out, minus_half, ALU.pow)


def norm_transpose(nc, S, x_tile, col, hT, ident, minus_half, tag):
    with ExitStack() as ctx:
        sb = lambda name, shape, dt=F32: ctx.enter_context(nc.sbuf_tensor(name, shape, dt))
        xt = sb(tag + "nt_x", [P, 2, D])
        sq = sb(tag + "nt_sq", [P, D])
        xn = sb(tag + "nt_n", [P, 2, D])
        ss = sb(tag + "nt_ss", [P, TT])
        rstd = sb(tag + "nt_r", [P, TT])
        ps = ctx.enter_context(nc.psum_tensor(tag + "nt_ps", [P, 2, KT, P], F32))
        s_x = [S(tag + "nt_x0"), S(tag + "nt_x1")]
        s_sq, s_n, s_t, s_h, s_c, s_rs = S(tag + "nt_sq"), S(tag + "nt_n"), S(tag + "nt_t"), S(tag + "nt_h"), S(tag + "nt_chain"), S(tag + "nt_rs")
        with nc.Block() as block:
            @block.sync
            def _(sp):
                for t in range(TT):
                    if t >= 2:
                        sp.wait_ge(s_sq, t - 1)
                        sp.wait_ge(s_n, t - 1)
                    sp.dma_start(xt[:, t % 2, :], x_tile(t)).then_inc(s_x[t % 2], 16)

            @block.gpsimd
            def _(pool):
                c = Chain(pool, s_c)
                for t in range(TT):
                    pool.wait_ge(s_sq, t + 1)
                    rsqrt_of_mean(nc, c, rstd[:, t:t + 1], ss[:, t:t + 1], D, minus_half).then_inc(s_rs, 1)

            @block.scalar
            def _(act):
                for t in range(TT):
                    act.wait_ge(s_x[t % 2], 16 * (t // 2 + 1))
                    if t:
                        act.wait_ge(s_sq, t)
                    nc.scalar.activation(sq[:], xt[:, t % 2, :], ACT.Square,
                                         accum_out=ss[:, t:t + 1]).then_inc(s_sq, 1)

            def evacuate(dve, t):
                dve.wait_ge(s_t, t + 1)
                nc.vector.tensor_tensor(hT[:, :, t * P:(t + 1) * P], ps[:, t % 2],
                                        col.unsqueeze(2).broadcast_to([P, KT, P]),
                                        ALU.mult).then_inc(s_h, 1)

            @block.vector
            def _(dve):
                for t in range(TT):
                    dve.wait_ge(s_rs, t + 1)
                    dve.wait_ge(s_x[t % 2], 16 * (t // 2 + 1))
                    if t >= 2:
                        dve.wait_ge(s_t, t - 1)
                    nc.vector.tensor_scalar(xn[:, t % 2, :], xt[:, t % 2, :], rstd[:, t:t + 1], None,
                                            ALU.mult).then_inc(s_n, 1)
                    if t:
                        evacuate(dve, t - 1)
                evacuate(dve, TT - 1)

            @block.tensor
            def _(pe):
                for t in range(TT):
                    pe.wait_ge(s_n, t + 1)
                    if t >= 2:
                        pe.wait_ge(s_h, t - 1)
                    for k in range(KT):
                        last = nc.tensor.transpose(ps[:, t % 2, k, :], xn[:, t % 2, k * P:(k + 1) * P],
                                                   ident)
                    last.then_inc(s_t, 1)


def rope_units():
    return [(h, w, f) for h in range(DIFF_HEADS) for w in range(2) for f in range(2)]


def diff_attention(nc, S, l, w_in, hT, y_dram, K, rows):
    NQ = TT
    STEPS = DIFF_HEADS * NQ
    with ExitStack() as ctx:
        sb = lambda name, shape, dt=F32: ctx.enter_context(nc.sbuf_tensor(name, shape, dt))
        wqk = sb("da_wqk", [P, 2, KT, 512])
        vt = sb("da_v", [P, TT, 512])
        gt = sb("da_g", [P, TT, 512])
        qk = sb("da_qk", [P, 2, 2, SEQ])
        raw = sb("da_raw", [P, 2, HALF])
        rs_ = sb("da_rs", [P, HALF])
        small = sb("da_small", [P, 16])
        st = sb("da_st", [P, STEPS, 10])
        with ExitStack() as ctx2:
            pr = [ctx2.enter_context(nc.psum_tensor(f"da_p{i}", [P, HALF], F32)) for i in range(4)]
            wvg = ctx2.enter_context(nc.sbuf_tensor("da_wvg", [P, 2, KT, 512], F32))
            sig = ctx2.enter_context(nc.sbuf_tensor("da_sig", [P, 2, 512], F32))
            s_w, s_p, s_v, s_sg, s_g, s_g1, s_lam, s_lr, s_le = (S("da_w"), S("da_p"), S("da_v"), S("da_sg"), S("da_g"),
                                                 S("da_g1"), S("da_lam"), S("da_lr"), S("da_le"))
            with nc.Block() as block:
                @block.sync
                def _(sp):
                    for j, off in enumerate((DV, DG)):
                        sp.dma_start(wvg[:, j], w_in(l, off, 512)).then_inc(s_w, 16)
                        sp.wait_ge(s_w, 16 * (j + 1))
                    for j, off in enumerate((DQ, DK)):
                        sp.dma_start(wqk[:, j], w_in(l, off, 512)).then_inc(s_w, 16)
                    sp.wait_ge(s_w, 64)

                @block.tensor
                def _(pe):
                    for n in range(2 * TT):
                        j, t = divmod(n, TT)
                        if t == 0:
                            pe.wait_ge(s_w, 16 * (j + 1))
                        if n >= 4:
                            m = n - 4
                            if m < TT:
                                pe.wait_ge(s_v, m + 1)
                            else:
                                pe.wait_ge(s_g1, m - TT + 1)
                        for k in range(KT):
                            last = nc.tensor.matmul(pr[n % 4][:], hT[:, k, t * P:(t + 1) * P],
                                                    wvg[:, j, k, :], start=(k == 0), stop=(k == KT - 1))
                        last.then_inc(s_p, 1)

                @block.scalar
                def _(act):
                    act.wait_ge(s_lr, 2)
                    nc.scalar.activation(small[:, 2:4], small[:, 0:2], ACT.Exp).then_inc(s_le, 1)
                    for t in range(TT):
                        act.wait_ge(s_p, t + 1)
                        nc.scalar.activation(vt[:, t, :], pr[t % 4][:], ACT.Copy).then_inc(s_v, 1)
                    for t in range(TT):
                        act.wait_ge(s_p, TT + t + 1)
                        if t >= 2:
                            act.wait_ge(s_g1, t - 1)
                        nc.scalar.activation(sig[:, t % 2, :], pr[(TT + t) % 4][:], ACT.Sigmoid).then_inc(s_sg, 1)

                @block.vector
                def _(dve):
                    for j in range(2):
                        a = rows[:, R_LQ + 128 * j:R_LQ + 128 * j + 64]
                        b = rows[:, R_LQ + 128 * j + 64:R_LQ + 128 * j + 128]
                        nc.vector.tensor_tensor_reduce(sig[:, j, 0:64], a, b, 1.0, 0.0, ALU.mult, ALU.add,
                                                       small[:, j:j + 1]).then_inc(s_lr, 1)
                    dve.wait_ge(s_le, 1)
                    nc.vector.tensor_tensor(small[:, 4:5], small[:, 3:4], small[:, 2:3], ALU.subtract).then_inc(s_lam, 1)
                    dve.wait_ge(s_lam, 1)
                    nc.vector.tensor_tensor(small[:, 5:6], small[:, 4:5], rows[:, R_LINIT:R_LINIT + 1],
                                            ALU.subtract).then_inc(s_lam, 1)
                    nc.vector.tensor_scalar(rs_[:, 0:128], rows[:, R_DN:R_DN + 128],
                                            rows[:, R_LINIT + 1:R_LINIT + 2], None, ALU.mult).then_inc(s_lam, 1)
                    dve.wait_ge(s_lam, 3)
                    for t in range(TT):
                        dve.wait_ge(s_sg, t + 1)
                        nc.vector.tensor_tensor(gt[:, t, :], pr[(TT + t) % 4][:], sig[:, t % 2, :],
                                                ALU.mult).then_inc(s_g1, 1)
                        dve.wait_ge(s_g1, t + 1)
                        g4 = gt[:, t, :].rearrange("p (h v) -> p h v", h=DIFF_HEADS)
                        nc.vector.tensor_tensor(g4, g4, rs_[:, 0:128].unsqueeze(1).broadcast_to([P, DIFF_HEADS, 128]),
                                                ALU.mult).then_inc(s_g, 1)

        e = sb("da_e", [P, 2, 2, SEQ])
        w = sb("da_wt", [P, 2, SEQ])
        wT = sb("da_wT", [P, 2, TT, P])
        y = sb("da_y", [P, 2, P])
        osb = sb("da_o", [P, 4, P])
        junk = sb("da_j", [P, P])
        yst = sb("da_yst", [P, 2, SEQ])
        s_st = [S("da_st0"), S("da_st1")]
        ps_s = ctx.enter_context(nc.psum_tensor("da_ps", [P, 2, SEQ], F32))
        ps_t = ctx.enter_context(nc.psum_tensor("da_pt", [P, TT, P], F32))
        ps_o = ctx.enter_context(nc.psum_tensor("da_po", [P, HALF], F32))
        ps_r = ctx.enter_context(nc.psum_tensor("da_pr", [P, HALF], F32))
        s_s, s_m, s_e, s_w2, s_t2, s_wT, s_pv, s_y, s_yt, s_ye, s_c = (
            S("da_s"), S("da_m"), S("da_e"), S("da_w2"), S("da_t2"), S("da_wT"), S("da_pv"), S("da_y"),
            S("da_yt"), S("da_ye"), S("da_chain"))
        s_pj, s_rw, s_rt, s_rc, s_rd = S("da_pj"), S("da_rw"), S("da_rt"), S("da_rc"), S("da_rd")
        s_pv_read, s_oss, s_ors, s_pc = S("da_pvr"), S("da_oss"), S("da_ors"), S("da_pool")
        units = rope_units()

        def unit_at(g, odd):
            n = 4 + (g // 2)
            return n if g % 2 == odd and g >= 0 and n < len(units) else None

        with nc.Block() as block:
            @block.sync
            def _(sp):
                for h in range(DIFF_HEADS):
                    sp.wait_ge(s_ye, NQ * (h + 1))
                    sp.dma_start(y_dram[2 + h], yst[:, h % 2, :]).then_inc(s_st[h % 2], 16)
                for j in range(2):
                    sp.wait_ge(s_st[j], 16 * DIFF_HEADS // 2)

            @block.gpsimd
            def _(pool):
                c = Chain(pool, s_pc)
                for a in range(STEPS):
                    pool.wait_ge(s_oss, a + 1)
                    rsqrt_of_mean(nc, c, st[:, a, 7:8], st[:, a, 6:7], 2 * DIFF_HD, K[:, K_NH:K_NH + 1]).then_inc(s_ors, 1)

            @block.tensor
            def _(pe):
                def project(n):
                    h, wh, f = units[n]
                    if n >= 1:
                        pe.wait_ge(s_rd, n)
                    for k in range(KT):
                        last = nc.tensor.matmul(ps_r[:], wqk[:, wh, k, h * P:(h + 1) * P],
                                                hT[:, k, f * HALF:(f + 1) * HALF], start=(k == 0), stop=(k == KT - 1))
                    last.then_inc(s_pj, 1)

                def turn(n):
                    pe.wait_ge(s_rw, n + 1)
                    nc.tensor.matmul(ps_r[:], K[:, K_ROT:K_ROT + P], raw[:, n % 2, :], start=True,
                                     stop=True).then_inc(s_rt, 1)

                for n in range(4):
                    project(n)
                    turn(n)
                for g in range(STEPS + 4):
                    if 4 <= g:
                        a = g - 4
                        pe.wait_ge(s_y, a + 1)
                        if a:
                            pe.wait_ge(s_ye, a)
                        done = [n for n in range(4, len(units)) if 2 * (n - 4) + 1 < g]
                        pe.wait_ge(s_rd, 4 + len(done))
                        raws = [n for n in range(4, len(units)) if 2 * (n - 4) < g]
                        pe.wait_ge(s_rw, 4 + len(raws))
                        nc.tensor.transpose(ps_r[:, 0:P], y[:, a % 2, :], K[:, K_ID:K_ID + P]).then_inc(s_yt, 1)
                    if g < STEPS:
                        h, i = divmod(g, NQ)
                        if i == 0:
                            pe.wait_ge(s_rc, 4 * (h + 1))
                        if g:
                            pe.wait_ge(s_e, 2 * g)
                        for c in range(2):
                            rows_ = slice(64 * c, 64 * c + 64)
                            for f in range(2):
                                last = nc.tensor.matmul(
                                    ps_s[:, c, f * HALF:(f + 1) * HALF], qk[rows_, h % 2, 0, i * P:(i + 1) * P],
                                    qk[rows_, h % 2, 1, f * HALF:(f + 1) * HALF], start=True, stop=True)
                            last.then_inc(s_s, 1)
                    if g >= 4 and (unit_at(g, 0) is not None or unit_at(g, 1) is not None):
                        pe.wait_ge(s_ye, g - 3)
                    if unit_at(g, 0) is not None:
                        project(unit_at(g, 0))
                    if unit_at(g, 1) is not None:
                        turn(unit_at(g, 1))
                    if 1 <= g <= STEPS:
                        a = g - 1
                        pe.wait_ge(s_w2, a + 1)
                        if a >= 1:
                            pe.wait_ge(s_wT, a)
                        for k in range(TT):
                            last = nc.tensor.transpose(ps_t[:, k, :], w[:, a % 2, k * P:(k + 1) * P], K[:, K_ID:K_ID + P])
                        last.then_inc(s_t2, 1)
                    if 2 <= g <= STEPS + 1:
                        a = g - 2
                        ha = a // NQ
                        pe.wait_ge(s_wT, a + 1)
                        if a:
                            pe.wait_ge(s_pv_read, a)
                        for k in range(TT):
                            last = nc.tensor.matmul(ps_o[:, 0:P], wT[:, a % 2, k, :], vt[:, k, ha * P:(ha + 1) * P],
                                                    start=(k == 0), stop=(k == TT - 1))
                        last.then_inc(s_pv, 1)

            @block.scalar
            def _(act):
                def raw_copy(n):
                    act.wait_ge(s_pj, n + 1)
                    if n >= 2:
                        act.wait_ge(s_rc, n - 1)
                    nc.scalar.activation(raw[:, n % 2, :], ps_r[:], ACT.Copy).then_inc(s_rw, 1)

                for n in range(4):
                    raw_copy(n)
                for g in range(STEPS + 4):
                    if 4 <= g:
                        a = g - 4
                        ha, ia = divmod(a, NQ)
                        act.wait_ge(s_yt, a + 1)
                        if ia == 0 and ha >= 2:
                            act.wait_ge(s_st[ha % 2], 16 * (ha // 2))
                        nc.scalar.activation(yst[:, ha % 2, ia * P:(ia + 1) * P], ps_r[:, 0:P],
                                             ACT.Copy).then_inc(s_ye, 1)
                    if g < STEPS:
                        for c in range(2):
                            act.wait_ge(s_m, 2 * g + c + 1)
                            if g >= 2 and c == 0:
                                act.wait_ge(s_w2, g - 1)
                            nc.scalar.activation(e[:, g % 2, c, :], ps_s[:, c, :], ACT.Exp,
                                                 bias=st[:, g, c:c + 1], scale=DIFF_HD ** -0.5,
                                                 accum_out=st[:, g, 2 + c:3 + c]).then_inc(s_e, 1)
                    if unit_at(g, 0) is not None:
                        raw_copy(unit_at(g, 0))
                    if 1 <= g <= STEPS:
                        a = g - 1
                        act.wait_ge(s_t2, a + 1)
                        if a >= 2:
                            act.wait_ge(s_pv, a - 1)
                        nc.scalar.activation(wT[:, a % 2], ps_t[:], ACT.Copy).then_inc(s_wT, 1)

            @block.vector
            def _(dve):
                c_ = Chain(dve, s_c)

                def turned(n):
                    h, wh, f = units[n]
                    cols = slice(f * HALF, (f + 1) * HALF)
                    dve.wait_ge(s_rt, n + 1)
                    if n:
                        dve.wait_ge(s_rc, n)
                    if units[n][0] >= 2:
                        dve.wait_ge(s_s, 2 * NQ * (h - 1))
                    nc.vector.tensor_tensor(rs_[:], ps_r[:], K[:, K_SIN + f * HALF:K_SIN + (f + 1) * HALF],
                                            ALU.mult).then_inc(s_rd, 1)
                    c_.did(nc.vector.tensor_tensor(qk[:, h % 2, wh, cols], raw[:, n % 2, :],
                                                   K[:, K_COS + f * HALF:K_COS + (f + 1) * HALF], ALU.mult))
                    c_.wait()
                    dve.wait_ge(s_rd, n + 1)
                    nc.vector.tensor_tensor(qk[:, h % 2, wh, cols], qk[:, h % 2, wh, cols], rs_[:],
                                            ALU.add).then_inc(s_rc, 1)

                for n in range(4):
                    turned(n)
                for g in range(STEPS + 3):
                    if 1 <= g <= STEPS:
                        a = g - 1
                        dve.wait_ge(s_e, 2 * a + 2)
                        c_.link(nc.vector.reciprocal(st[:, a, 4:6], st[:, a, 2:4]))
                        c_.link(nc.vector.scalar_tensor_tensor(st[:, a, 6:7], st[:, a, 2:3], st[:, a, 5:6],
                                                               small[:, 5:6], ALU.mult, ALU.mult))
                        if a >= 2:
                            dve.wait_ge(s_t2, a - 1)
                        nc.vector.scalar_tensor_tensor(w[:, a % 2, :], e[:, a % 2, 1, :], st[:, a, 6:7],
                                                       e[:, a % 2, 0, :], ALU.mult, ALU.add).then_inc(s_w2, 1)
                    if g < STEPS:
                        for c in range(2):
                            dve.wait_ge(s_s, 2 * g + c + 1)
                            c_.link(nc.vector.tensor_reduce(st[:, g, 8 + c:9 + c], ps_s[:, c, :], AX.X, ALU.max))
                            nc.vector.tensor_scalar(st[:, g, c:c + 1], st[:, g, 8 + c:9 + c], -DIFF_HD ** -0.5, None,
                                                    ALU.mult).then_inc(s_m, 1)
                    if unit_at(g, 1) is not None:
                        turned(unit_at(g, 1))
                    if 2 <= g <= STEPS + 1:
                        a = g - 2
                        ha, ia = divmod(a, NQ)
                        dve.wait_ge(s_pv, a + 1)
                        nc.vector.tensor_scalar(osb[:, a % 4, :], ps_o[:, 0:P], st[:, a, 4:5], None,
                                                ALU.mult).then_inc(s_pv_read, 1)
                        dve.wait_ge(s_pv_read, a + 1)
                        if a >= 1:
                            dve.wait_ge(s_oss, a)
                        nc.vector.tensor_tensor_reduce(junk[:], osb[:, a % 4, :], osb[:, a % 4, :], 1.0, 0.0,
                                                       ALU.mult, ALU.add, st[:, a, 6:7]).then_inc(s_oss, 1)
                    if 3 <= g <= STEPS + 2:
                        a = g - 3
                        ha, ia = divmod(a, NQ)
                        dve.wait_ge(s_ors, a + 1)
                        if a >= 2:
                            dve.wait_ge(s_yt, a - 1)
                        nc.vector.scalar_tensor_tensor(y[:, a % 2, :], osb[:, a % 4, :], st[:, a, 7:8],
                                                       gt[:, ia, ha * P:(ha + 1) * P], ALU.mult, ALU.mult).then_inc(s_y, 1)


def out_project(nc, S, y_dram, w_dram, x_tile, x_out, post, minus_half, tag):
    with ExitStack() as ctx:
        sb = lambda name, shape, dt=F32: ctx.enter_context(nc.sbuf_tensor(name, shape, dt))
        w = sb(tag + "op_w", [P, KT, D])
        yT = sb(tag + "op_y", [P, KT, SEQ])
        xt = sb(tag + "op_x", [P, 2, D])
        xo = sb(tag + "op_o", [P, 2, D])
        sq = sb(tag + "op_sq", [P, D])
        ss = sb(tag + "op_ss", [P, TT])
        rstd = sb(tag + "op_r", [P, TT])
        s_pc = S(tag + "op_pool")
        ps = [ctx.enter_context(nc.psum_tensor(f"{tag}op_ps{i}", [P, D], F32)) for i in range(2)]
        WP = 4
        s_w = [S(f"{tag}op_w{j}") for j in range(WP)]
        s_yf, s_yr = S(tag + "op_yf"), S(tag + "op_yr")
        s_x = [S(tag + "op_x0"), S(tag + "op_x1")]
        s_o = [S(tag + "op_o0"), S(tag + "op_o1")]
        s_p, s_sq, s_s, s_y, s_c = S(tag + "op_p"), S(tag + "op_sq"), S(tag + "op_s"), S(tag + "op_y"), S(tag + "op_chain")
        with nc.Block() as block:
            @block.sync
            def _(sp):
                y_view = y_dram.rearrange("k p s -> p k s")
                sp.dma_start(yT[:, :, 0:2 * P], y_view[:, :, 0:2 * P]).then_inc(s_yf, 16)
                for j in range(WP):
                    sp.dma_start(w[:, 2 * j:2 * j + 2, :], w_dram[:, 2 * j:2 * j + 2, :]).then_inc(s_w[j], 16)
                sp.dma_start(yT[:, :, 2 * P:SEQ], y_view[:, :, 2 * P:SEQ]).then_inc(s_yr, 16)
                for t in range(TT):
                    if t >= 2:
                        sp.wait_ge(s_y, t - 1)
                    sp.dma_start(xt[:, t % 2, :], x_tile(t)).then_inc(s_x[t % 2], 16)

            @block.tensor
            def _(pe):
                def product(t, k):
                    for f in range(2):
                        last = nc.tensor.matmul(ps[t % 2][:, f * HALF:(f + 1) * HALF], yT[:, k, t * P:(t + 1) * P],
                                                w[:, k, f * HALF:(f + 1) * HALF], start=(k == 0), stop=(k == KT - 1))
                    if k == KT - 1:
                        last.then_inc(s_p, 1)

                pe.wait_ge(s_yf, 16)
                for j in range(WP):
                    pe.wait_ge(s_w[j], 16)
                    for t in range(2):
                        product(t, 2 * j)
                        product(t, 2 * j + 1)
                pe.wait_ge(s_yr, 16)
                for t in range(2, TT):
                    pe.wait_ge(s_y, t - 1)
                    for k in range(KT):
                        product(t, k)

            @block.gpsimd
            def _(pool):
                c = Chain(pool, s_pc)
                for t in range(TT if post is not None else 0):
                    pool.wait_ge(s_sq, t + 1)
                    rsqrt_of_mean(nc, c, rstd[:, t:t + 1], ss[:, t:t + 1], D, minus_half).then_inc(s_s, 1)

            @block.scalar
            def _(act):
                for t in range(TT):
                    if post is not None:
                        act.wait_ge(s_p, t + 1)
                        if t:
                            act.wait_ge(s_sq, t)
                        nc.scalar.activation(sq[:], ps[t % 2][:], ACT.Square, accum_out=ss[:, t:t + 1]).then_inc(s_sq, 1)
                    act.wait_ge(s_y, t + 1)
                    act.dma_start(x_out(t), xo[:, t % 2, :]).then_inc(s_o[t % 2], 16)
                for j in range(2):
                    act.wait_ge(s_o[j], 16 * TT // 2)

            @block.vector
            def _(dve):
                c = Chain(dve, s_c)
                for t in range(TT):
                    if t >= 2:
                        dve.wait_ge(s_o[t % 2], 16 * (t // 2))
                    if post is not None:
                        dve.wait_ge(s_s, t + 1)
                        c.link(nc.vector.scalar_tensor_tensor(xo[:, t % 2, :], ps[t % 2][:], rstd[:, t:t + 1], post,
                                                              ALU.mult, ALU.mult))
                        dve.wait_ge(s_x[t % 2], 16 * (t // 2 + 1))
                        nc.vector.tensor_tensor(xo[:, t % 2, :], xo[:, t % 2, :], xt[:, t % 2, :], ALU.add).then_inc(s_y, 1)
                    else:
                        dve.wait_ge(s_p, t + 1)
                        dve.wait_ge(s_x[t % 2], 16 * (t // 2 + 1))
                        nc.vector.tensor_tensor(xo[:, t % 2, :], ps[t % 2][:], xt[:, t % 2, :], ALU.add).then_inc(s_y, 1)


def by_chunk(ap):
    return ap.rearrange("p (n i) -> p n i", i=CHUNK)


def gated_scans(nc, S, l, w_in, wa2, hT, y_dram, K, cols):
    LAGS = CHUNK
    INC = 5
    units = (dict(nv=2, heads=4, dk=32, yt=(0, 1)), dict(nv=1, heads=2, dk=64, yt=(6,)),
             dict(nv=1, heads=2, dk=64, yt=(7,)))
    NU = len(units)
    proj = [
        [("a", GAF, 32), ("zf", None, P), ("zb", None, P), ("k", GK, P), ("q", GQ, P), ("v0", GV, P), ("v1", GV + P, P),
         ("g0", GG, P), ("g1", GG + P, P)],
    ] + [[("zf", HZF + P * j, P), ("zb", HZB + P * j, P), ("v0", HI + P * j, P), ("q", HQ + P * j, P),
          ("g0", HG + P * j, P)] for j in range(2)]
    WR = 2
    EARLY = (2, 3, 2)
    banks = [(u, name, f) for u in range(NU) for name, _, _ in proj[u] for f in range(2)]
    bank_no = {b: i for i, b in enumerate(banks)}

    with ExitStack() as ctx:
        sb = lambda name, shape, dt=F32: ctx.enter_context(nc.sbuf_tensor(name, shape, dt))
        wt = sb("gs_w", [P, WR, KT, P])
        wa = sb("gs_wa", [32, 2 * P])
        q = sb("gs_q", [P, SEQ])
        kd = sb("gs_k", [P, 2, SEQ])
        fd = sb("gs_f", [P, 2, SEQ])
        v = sb("gs_v", [P, 2, SEQ])
        gate = sb("gs_g", [P, 2, SEQ])
        vtok = sb("gs_vt", [P, TT, 2 * P])
        ats = sb("gs_a", [32, SEQ])
        pre = sb("gs_pre", [P, 2, SEQ])
        suf = sb("gs_suf", [P, 2, SEQ])
        R = sb("gs_R", [P, 2, SEQ])
        ys = sb("gs_y", [P, 2, HALF])
        Pq = sb("gs_P", [P, 2, SEQ])
        oacc = sb("gs_o", [P, 2, SEQ])
        tmp = sb("gs_tmp", [P, 2, HALF])
        qx = sb("gs_qx", [P, 2, SEQ])
        ktok = sb("gs_kt", [P, TT, P])
        U = sb("gs_U", [P, GLA_DV, NCH])
        factors = sb("gs_th2", [P, GLA_DV, NCH])
        Vx = sb("gs_Vx", [P, 4, CPT, GLA_DV])
        lb = sb("gs_lb", [P, 8])
        through = sb("gs_th", [P, 4, NCH])
        pb = [ctx.enter_context(nc.psum_tensor(f"gs_b{i}", [P, HALF], F32)) for i in range(2)]
        plag = [ctx.enter_context(nc.psum_tensor(f"gs_l{i}", [P, HALF], F32)) for i in range(4)]
        pu = ctx.enter_context(nc.psum_tensor("gs_u", [P, 2, HALF], F32))

        s_w = [S(f"gs_w{i}") for i in range(WR)]
        items = [(u, name) for u in range(NU) for name, off, _ in proj[u] if off is not None]
        s_done, s_lags = S("gs_done"), S("gs_lags_over")
        s_wa, s_through = S("gs_wa"), S("gs_through")
        s_fm = S("gs_fm")
        s_yo = [S("gs_yo0"), S("gs_yo1")]
        s_lbe, s_lbd = S("gs_lbe"), S("gs_lbd")
        proj_done = Signal(S("gs_proj"), banks)
        read_out = Signal(S("gs_read"), banks)
        gla_log = [(d, f) for d in range(2) for f in range(2)]
        s_gl1, s_gl2, s_gl3, s_gmin, s_gf = S("gs_gl1"), S("gs_gl2"), S("gs_gl3"), S("gs_gmin"), S("gs_gf")
        unit_dir = [(u, d) for u in range(NU) for d in range(2)]
        ready = Signal(S("gs_ready"), range(NU))
        s_chain = S("gs_chain")
        lag_keys = [(u, d, j) for u, d in unit_dir for j in range(LAGS)]
        P_ready = Signal(S("gs_P"), lag_keys)
        R_keys = [k for k in lag_keys if k[2]]
        R_ready = Signal(S("gs_R"), R_keys)
        pieces = []
        for u, d, j in lag_keys:
            for vt_ in range(units[u]["nv"]):
                for hf in (range(2) if j < 8 else range(1)):
                    pieces.append((u, d, j, vt_, hf))
        piece_no = {p: i for i, p in enumerate(pieces)}
        lag_sum = Signal(S("gs_lag"), pieces)
        lag_read = Signal(S("gs_lagr"), pieces)
        suf_ready = Signal(S("gs_suf"), unit_dir)
        qx_keys = [(u, d, vt_) for u, d in unit_dir for vt_ in range(units[u]["nv"])]
        qx_ready = Signal(S("gs_qx"), qx_keys)
        vtr = [(u, t) for u in range(NU) for t in range(TT)]
        v_turned, v_tok = Signal(S("gs_vtr"), vtr), Signal(S("gs_vtk"), vtr)
        kt_keys = [(u, d, f) for u, d in unit_dir for f in range(2)]
        k_turned, k_tok = Signal(S("gs_ktr"), kt_keys), Signal(S("gs_ktk"), kt_keys)
        ut = [(u, d, t) for u, d in unit_dir for t in range(TT)]
        Vx_ready, U_sum, U_ready = Signal(S("gs_vx"), ut), Signal(S("gs_us"), ut), Signal(S("gs_ur"), ut)
        state_ready = Signal(S("gs_st"), unit_dir)
        spread_ready = Signal(S("gs_spr"), unit_dir)
        inter_keys = [(u, d, vt_, f) for u, d in unit_dir for vt_ in range(units[u]["nv"]) for f in range(2)]
        inter_sum, inter_read = Signal(S("gs_is"), inter_keys), Signal(S("gs_ir"), inter_keys)
        fin_keys = [(u, vt_, f) for u in range(NU) for vt_ in range(units[u]["nv"]) for f in range(2)]
        fin_sq, fin_sum, fin_y = (Signal(S("gs_fq"), fin_keys), Signal(S("gs_fs"), fin_keys),
                                  Signal(S("gs_fy"), fin_keys))

        def half(ap, f):
            return ap[:, f * HALF:(f + 1) * HALF]

        with nc.Block() as block:
            @block.sync
            def _(sp):
                sp.dma_start(wa[:], wa2(l)).then_inc(s_wa, 16)
                for i, (u, name) in enumerate(items):
                    if i >= WR:
                        proj_done.wait(sp, (*items[i - WR], 1))
                    off, width = [(o, w) for n, o, w in proj[u] if n == name][0]
                    sp.dma_start(wt[:, i % WR, :, 0:width], w_in(l, off, width)).then_inc(s_w[i % WR], 16)

            def lag_window(ap3, d, j, hf):
                n0, n1 = (32 * hf, 32 * hf + 32) if j < 8 else (0, NCH)
                lo, hi = (j, CHUNK) if d == 0 else (0, CHUNK - j)
                return ap3[:, n0:n1, lo:hi], (n1 - n0) * (CHUNK - j)

            def partner(ap3, d, j, hf):
                n0, n1 = (32 * hf, 32 * hf + 32) if j < 8 else (0, NCH)
                lo, hi = (0, CHUNK - j) if d == 0 else (j, CHUNK)
                return ap3[:, n0:n1, lo:hi]

            def spread_query(dve, c, u, d, vt_):
                i = qx_keys.index((u, d, vt_))
                if i:
                    inter_sum.wait(dve, (*qx_keys[i - 1], 1))
                if u < 2:
                    c.link(nc.vector.memset(qx[:], 0.0))
                dk = units[u]["dk"]
                for h in range(2):
                    rr = slice((2 * vt_ + h) * dk, (2 * vt_ + h + 1) * dk)
                    last = nc.vector.tensor_tensor(qx[rr, h, :], q[rr, :], pre[rr, d, :], ALU.mult)
                last.then_inc(qx_ready.sem, 1)

            def add_between(dve, c, u, d, j):
                vt_, f = divmod(j, 2)
                m = inter_keys.index((u, d, vt_, f))
                inter_sum.wait(dve, (u, d, vt_, f))
                lo, hi = f * HALF, (f + 1) * HALF
                if d == 0 and f == 0:
                    lo += CHUNK
                if d == 1 and f == 1:
                    hi -= CHUNK
                c.wait()
                c.link(nc.vector.tensor_tensor(oacc[:, vt_, lo:hi], oacc[:, vt_, lo:hi],
                                               pu[:, m % 2, lo - f * HALF:hi - f * HALF], ALU.add))
                dve.sem_inc(inter_read.sem, 1)
                if j == 1 and units[u]["nv"] == 2:
                    spread_query(dve, c, u, d, 1)

            def lags(dve, c, u, d):
                un = units[u]
                q3 = by_chunk(q[:])
                k3 = by_chunk(kd[:, d if u else 0])
                R3 = [by_chunk(R[:, i]) for i in range(2)]
                P3 = [by_chunk(Pq[:, i]) for i in range(2)]
                v3 = [by_chunk(v[:, i]) for i in range(2)]
                o3 = [by_chunk(oacc[:, i]) for i in range(2)]
                first = lambda ap, j: ap[:, :, j:] if d == 0 else ap[:, :, :CHUNK - j]
                second = lambda ap, j: ap[:, :, :CHUNK - j] if d == 0 else ap[:, :, j:]

                def decayed(j):
                    if j:
                        R_ready.wait(dve, (u, d, j))
                    if j >= 2:
                        lag_sum.wait(dve, [p for p in pieces if p[:3] == (u, d, j - 2)][-1])
                    elif (u, d) != (0, 0):
                        up, dp = (u, 0) if d else (u - 1, 1)
                        lag_sum.wait(dve, [p for p in pieces if p[:3] == (up, dp, LAGS - 1)][-1])
                    r = k3 if j == 0 else R3[j % 2]
                    nc.vector.tensor_tensor(first(P3[j % 2], j), first(q3, j), first(r, j), ALU.mult).then_inc(P_ready.sem, 1)

                decayed(0)
                for j in range(LAGS):
                    if j + 1 < LAGS:
                        decayed(j + 1)
                    for vt_ in range(un["nv"]):
                        for hf in (range(2) if j < 8 else range(1)):
                            piece = (u, d, j, vt_, hf)
                            n = piece_no[piece]
                            lag_sum.wait(dve, piece)
                            n0, n1 = (32 * hf, 32 * hf + 32) if j < 8 else (0, NCH)
                            cnt = (n1 - n0) * (CHUNK - j)
                            ps3 = plag[n % 4][:, 0:cnt].rearrange("p (n i) -> p n i", i=CHUNK - j)
                            vv = second(v3[vt_], j)[:, n0:n1]
                            oo = first(o3[vt_], j)[:, n0:n1]
                            if d == 0 and j == 0:
                                c.did(nc.vector.tensor_tensor(oo, ps3, vv, ALU.mult))
                                dve.wait_ge(c.sem, c.n)
                                dve.sem_inc(lag_read.sem, 1)
                            else:
                                tt = tmp[:, n % 2, 0:cnt].rearrange("p (n i) -> p n i", i=CHUNK - j)
                                nc.vector.tensor_tensor(tt, ps3, vv, ALU.mult).then_inc(lag_read.sem, 1)
                                lag_read.wait(dve, piece)
                                c.wait()
                                c.did(nc.vector.tensor_tensor(oo, oo, tt, ALU.add))
                    if d and j < 2 * un["nv"]:
                        add_between(dve, c, u, 0, j)
                if d:
                    c.wait()
                    dve.sem_inc(s_lags, 1)

            @block.tensor
            def _(pe):
                ident = K[:, K_ID:K_ID + P]

                def project(u, part):
                    for name, off, width in part:
                        if off is None:
                            read_out.wait(pe, (u, "a", 1))
                            pe.wait_ge(s_wa, 16)
                        else:
                            it = items.index((u, name))
                            pe.wait_ge(s_w[it % WR], 16 * (it // WR + 1))
                        for f in range(2):
                            i = bank_no[(u, name, f)]
                            if i >= 2:
                                read_out.wait(pe, banks[i - 2])
                            if off is None:
                                dd = "fb".index(name[1])
                                last = nc.tensor.matmul(pb[i % 2][:], wa[:, dd * P:(dd + 1) * P], half(ats, f), start=True,
                                                        stop=True)
                            else:
                                for k in range(KT):
                                    last = nc.tensor.matmul(pb[i % 2][0:width, :], wt[:, it % WR, k, 0:width],
                                                            half(hT[:, k], f), start=(k == 0), stop=(k == KT - 1))
                            last.then_inc(proj_done.sem, 1)

                def between(u, d, vt_, f):
                    state_ready.wait(pe, (u, d))
                    qx_ready.wait(pe, (u, d, vt_))
                    m = inter_keys.index((u, d, vt_, f))
                    if m >= 2:
                        inter_read.wait(pe, inter_keys[m - 2])
                    for n in range(32 * f, 32 * f + 32):
                        prev = n - 1 if d == 0 else n + 1
                        if not 0 <= prev < NCH:
                            continue
                        for h in range(2):
                            last = nc.tensor.matmul(
                                pu[64 * h:64 * h + 64, m % 2, (n % 32) * CHUNK:(n % 32 + 1) * CHUNK],
                                U[:, :, prev if d == 0 else NCH - 1 - prev], qx[:, h, n * CHUNK:(n + 1) * CHUNK], start=True, stop=True)
                    last.then_inc(inter_sum.sem, 1)

                def increments(u, d, t):
                    Vx_ready.wait(pe, (u, d, t))
                    if t == 0:
                        k_tok.wait(pe, (u, d, 1))
                        if (u, d) != (0, 0):
                            before = unit_dir[unit_dir.index((u, d)) - 1]
                            inter_read.wait(pe, (*before, units[before[0]]["nv"] - 1, 1))
                    if t >= 2:
                        U_ready.wait(pe, (u, d, t - 2))
                    dk = units[u]["dk"]
                    for h in range(units[u]["heads"]):
                        last = nc.tensor.matmul(pu[h * dk:(h + 1) * dk, t % 2, :], ktok[:, t, h * dk:(h + 1) * dk],
                                                Vx[:, h].rearrange("p j v -> p (j v)"), start=True, stop=True)
                    last.then_inc(U_sum.sem, 1)

                project(0, proj[0][:EARLY[0]])
                for u in range(NU):
                    un = units[u]
                    project(u, proj[u][EARLY[u]:])
                    for t in range(TT):
                        for vt_ in range(un["nv"]):
                            if t >= 2:
                                v_tok.wait(pe, (u, t - 2))
                            read_out.wait(pe, (u, f"v{vt_}", 1))
                            read_out.wait(pe, banks[bank_no[(u, proj[u][-1][0], 1)]])
                            last = nc.tensor.transpose(pb[t % 2][:, vt_ * P:(vt_ + 1) * P], v[:, vt_, t * P:(t + 1) * P], ident)
                        last.then_inc(v_turned.sem, 1)
                    for d in range(2):
                        suf_ready.wait(pe, (u, d))
                        v_tok.wait(pe, (u, TT - 1))
                        for f in range(2):
                            for t in range(4 * f, 4 * f + 4):
                                last = nc.tensor.transpose(pb[f][:, (t % 4) * P:(t % 4 + 1) * P],
                                                           suf[:, d, t * P:(t + 1) * P], ident)
                            last.then_inc(k_turned.sem, 1)
                        if u and d == 0:
                            pe.wait_ge(s_fm, len([k for k in fin_keys if k[0] < u]))
                        for j in range(LAGS):
                            P_ready.wait(pe, (u, d, j))
                            src = by_chunk(Pq[:, j % 2, :])
                            for vt_ in range(un["nv"]):
                                kcol = (K_G0, K_G1)[vt_] if u == 0 else K_H
                                for hf in (range(2) if j < 8 else range(1)):
                                    n = piece_no[(u, d, j, vt_, hf)]
                                    if n >= 4:
                                        lag_read.wait(pe, pieces[n - 4])
                                    rhs, cnt = lag_window(src, d, j, hf)
                                    nc.tensor.matmul(plag[n % 4][:, 0:cnt], K[:, kcol:kcol + P], rhs, start=True,
                                                     stop=True).then_inc(lag_sum.sem, 1)
                            if d and j < 2 * un["nv"]:
                                between(u, 0, j // 2, j % 2)
                            if INC <= j < INC + TT:
                                increments(u, d, j - INC)
                    if u + 1 < NU:
                        k_tok.wait(pe, (u, 1, 1))
                        project(u + 1, proj[u + 1][:1])
                    for j in range(2 * un["nv"]):
                        between(u, 1, j // 2, j % 2)
                        if u + 1 < NU and j % 2:
                            project(u + 1, proj[u + 1][1 + j // 2:2 + j // 2])
                    for vt_ in range(un["nv"]):
                        for f in range(2):
                            fin_sq.wait(pe, (u, vt_, f))
                            m = fin_keys.index((u, vt_, f))
                            if m >= 2:
                                pe.wait_ge(s_fm, m - 1)
                            nc.tensor.matmul(plag[m % 2][:], K[:, K_H:K_H + P], half(Pq[:, m % 2], f), start=True,
                                             stop=True).then_inc(fin_sum.sem, 1)

            @block.scalar
            def _(act):
                act.wait_ge(s_lbd, 1)
                nc.scalar.activation(lb[:, 0:2], lb[:, 4:6], ACT.Sigmoid).then_inc(s_lbe, 1)

                def read_banks(u, part):
                    for name, off, width in part:
                        for f in range(2):
                            proj_done.wait(act, (u, name, f))
                            src = pb[bank_no[(u, name, f)] % 2]
                            d = int(name == "zb")
                            if name == "q":
                                ins = nc.scalar.activation(half(q, f), src[:], ACT.Copy, scale=GLA_DK ** -0.5 if u == 0 else 1.0)
                            elif name == "k":
                                ins = nc.scalar.activation(half(kd[:, 0], f), src[:], ACT.Copy)
                            elif name[0] == "v":
                                ins = nc.scalar.activation(half(v[:, int(name[1])], f), src[:], ACT.Copy)
                            elif name == "a":
                                ins = nc.scalar.activation(half(ats, f), src[0:32, :], ACT.Copy)
                            elif name[0] == "g":
                                ins = nc.scalar.activation(half(gate[:, int(name[1])], f), src[:], ACT.Silu)
                            elif off is None:
                                ins = nc.scalar.activation(half(fd[:, d], f), src[:], ACT.Identity,
                                                           bias=cols[:, C_BA + d:C_BA + d + 1])
                            else:
                                nc.scalar.activation(half(fd[:, d], f), src[:], ACT.Sigmoid)
                                ins = nc.scalar.activation(half(kd[:, d], f), src[:], ACT.Sigmoid, scale=-1.0)
                            ins.then_inc(read_out.sem, 1)
                            if off is None:
                                m = gla_log.index((d, f))
                                read_out.wait(act, (u, name, f))
                                nc.scalar.activation(half(pre[:, d], f), half(fd[:, d], f), ACT.Abs).then_inc(s_gl1, 1)
                                act.wait_ge(s_gl1, m + 1)
                                nc.scalar.activation(half(pre[:, d], f), half(pre[:, d], f), ACT.Exp, scale=-1.0).then_inc(s_gl2, 1)
                                act.wait_ge(s_gl2, m + 1)
                                nc.scalar.activation(half(pre[:, d], f), half(pre[:, d], f), ACT.Ln, bias=1.0).then_inc(s_gl3, 1)
                        if (u, name) == (0, "q"):
                            for m, (d, f) in enumerate(gla_log):
                                act.wait_ge(s_gmin, m + 1)
                                nc.scalar.activation(half(fd[:, d], f), half(fd[:, d], f), ACT.Exp,
                                                     scale=1.0 / GATE_TEMP).then_inc(s_gf, 1)

                read_banks(0, proj[0][:EARLY[0]])
                for u in range(NU):
                    un = units[u]
                    if u:
                        fin_y.wait(act, (u - 1, units[u - 1]["nv"] - 1, 1))
                        act.wait_ge(s_yo[0], 8 * len([k for k in fin_keys if k[0] < u]))
                        act.wait_ge(s_yo[1], 8 * len([k for k in fin_keys if k[0] < u]))
                    read_banks(u, proj[u][EARLY[u]:])
                    for t in range(TT):
                        v_turned.wait(act, (u, t))
                        w = un["nv"] * P
                        nc.scalar.activation(vtok[:, t, 0:w], pb[t % 2][:, 0:w], ACT.Copy).then_inc(v_tok.sem, 1)
                    for d in range(2):
                        for f in range(2):
                            k_turned.wait(act, (u, d, f))
                            if d:
                                U_sum.wait(act, (u, 0, TT - 1))
                            nc.scalar.activation(ktok[:, 4 * f:4 * f + 4, :].rearrange("p t c -> p (t c)"), pb[f][:],
                                                 ACT.Copy).then_inc(k_tok.sem, 1)
                        act.wait_ge(s_through, u + 1)
                        if (u, d) != (0, 0):
                            state_ready.wait(act, unit_dir[unit_dir.index((u, d)) - 1])
                        nc.scalar.activation(factors[:], through[:, d].unsqueeze(1).broadcast_to([P, GLA_DV, NCH]),
                                             ACT.Copy).then_inc(spread_ready.sem, 1)
                        if d:
                            inter_sum.wait(act, (u, 0, un["nv"] - 1, 1))
                        for t in range(TT):
                            U_sum.wait(act, (u, d, t))
                            at = t if d == 0 else TT - 1 - t
                            nc.scalar.activation(U[:, :, at * CPT:(at + 1) * CPT],
                                                 pu[:, t % 2, :].rearrange("p (n v) -> p v n", n=CPT),
                                                 ACT.Copy).then_inc(U_ready.sem, 1)
                    if u + 1 < NU:
                        lag_read.wait(act, [p for p in pieces if p[:2] == (u, 1)][-1])
                        lag_sum.wait(act, [p for p in pieces if p[:2] == (u, 1)][-1])
                        act.wait_ge(s_lags, u + 1)
                        read_banks(u + 1, proj[u + 1][:EARLY[u + 1]])
                    own = [m for m, key in enumerate(fin_keys) if key[0] == u]

                    def root(m):
                        fin_sum.wait(act, fin_keys[m])
                        if m >= own[0] + 2:
                            fin_y.wait(act, fin_keys[m - 2])
                        nc.scalar.activation(tmp[:, m % 2, :], plag[m % 2][:], ACT.Sqrt, scale=1.0 / GLA_DV,
                                             bias=K[:, K_EPS:K_EPS + 1]).then_inc(s_fm, 1)

                    act.wait_ge(s_done, u + 1)
                    for m in own:
                        _, vt_, f = fin_keys[m]
                        if m > own[0]:
                            fin_sum.wait(act, fin_keys[m - 1])
                        nc.scalar.activation(half(Pq[:, m % 2], f), half(oacc[:, vt_], f), ACT.Square).then_inc(fin_sq.sem, 1)
                        if m > own[0]:
                            root(m - 1)
                    root(own[-1])
                    for m, (_, vt_, f) in enumerate(fin_keys):
                        if fin_keys[m][0] == u:
                            fin_y.wait(act, fin_keys[m])
                            act.dma_start(half(y_dram[un["yt"][vt_]], f), ys[:, m % 2, :]).then_inc(s_yo[m % 2], 16)
                for j in range(2):
                    act.wait_ge(s_yo[j], 16 * len(fin_keys) // 2)

            @block.gpsimd
            def _(pool):
                def decayed(u, d, j):
                    f3 = by_chunk(fd[:, d])
                    R3 = [by_chunk(R[:, i]) for i in range(2)]
                    before = by_chunk(kd[:, d if u else 0]) if j == 1 else R3[(j - 1) % 2]
                    here, back = ((slice(j, CHUNK), slice(j - 1, CHUNK - 1)) if d == 0 else
                                  (slice(0, CHUNK - j), slice(1, CHUNK - j + 1)))
                    i = R_keys.index((u, d, j))
                    if i:
                        R_ready.wait(pool, R_keys[i - 1])
                    if j > 2:
                        P_ready.wait(pool, (u, d, j - 2))
                    elif (u, d) != (0, 0):
                        P_ready.wait(pool, (*unit_dir[unit_dir.index((u, d)) - 1], LAGS - 1))
                    nc.gpsimd.tensor_tensor(R3[j % 2][:, :, here], before[:, :, back], f3[:, :, here],
                                            ALU.mult).then_inc(R_ready.sem, 1)

                def masked_values(u, d, t):
                    v_tok.wait(pool, (u, t))
                    i = ut.index((u, d, t))
                    if i:
                        U_sum.wait(pool, ut[i - 1])
                    mask = (K_MASK, K_MASKB)[d]
                    for h in range(units[u]["heads"]):
                        last = nc.gpsimd.tensor_tensor(
                            Vx[:, h], vtok[:, t, h * 64:(h + 1) * 64].unsqueeze(1).broadcast_to([P, CPT, 64]),
                            K[:, mask:mask + CPT].unsqueeze(2).broadcast_to([P, CPT, 64]), ALU.mult)
                    last.then_inc(Vx_ready.sem, 1)

                for u, d in unit_dir:
                    suf_ready.wait(pool, (u, d))
                    for j in range(1, LAGS):
                        decayed(u, d, j)
                        if INC <= j < INC + TT:
                            masked_values(u, d, j - INC)

            @block.vector
            def _(dve):
                c = Chain(dve, s_chain)
                c.link(nc.vector.tensor_tensor(lb[:, 6:8], cols[:, C_LB + 2:C_LB + 4], cols[:, C_LB:C_LB + 2], ALU.subtract))
                nc.vector.tensor_copy(lb[:, 4:6], lb[:, 6:8]).then_inc(s_lbd, 1)
                dve.wait_ge(s_lbe, 1)
                c.link(nc.vector.tensor_scalar(lb[:, 0:2], lb[:, 0:2], cols[:, C_FLAG:C_FLAG + 1], None, ALU.mult))
                c.link(nc.vector.tensor_scalar(lb[:, 2:4], lb[:, 0:2], -1.0, 1.0, ALU.mult, ALU.add))
                for u in range(NU):
                    un = units[u]
                    if u == 0:
                        for m, (d, f) in enumerate(gla_log):
                            dve.wait_ge(s_gl3, m + 1)
                            nc.vector.scalar_tensor_tensor(half(fd[:, d], f), half(fd[:, d], f), 0.0, half(pre[:, d], f),
                                                           ALU.min, ALU.subtract).then_inc(s_gmin, 1)
                        dve.wait_ge(s_gf, 4)
                    else:
                        read_out.wait(dve, (u, "zb", 1))
                        for d in range(2):
                            c.did(nc.vector.tensor_scalar(kd[:, d], kd[:, d], lb[:, 2 + u - 1:3 + u - 1], None, ALU.mult))
                            c.did(nc.vector.tensor_scalar(fd[:, d], fd[:, d], lb[:, 2 + u - 1:3 + u - 1], lb[:, u - 1:u],
                                                          ALU.mult, ALU.add))
                            c.wait()
                            c.link(nc.vector.tensor_scalar(fd[:, d], fd[:, d], F_FLOOR, None, ALU.max))
                    f3 = [by_chunk(fd[:, d]) for d in range(2)]
                    p3 = [by_chunk(pre[:, d]) for d in range(2)]
                    s3 = [by_chunk(suf[:, d]) for d in range(2)]
                    at = lambda d, i: i if d == 0 else CHUNK - 1 - i
                    key = lambda d: kd[:, d if u else 0]
                    for d in range(2):
                        c.did(nc.vector.tensor_copy(p3[d][:, :, at(d, 0)], f3[d][:, :, at(d, 0)]))
                        c.did(nc.vector.memset(s3[d][:, :, at(d, CHUNK - 1)], 1.0))
                    for i in range(1, CHUNK):
                        c.wait()
                        for d in range(2):
                            c.did(nc.vector.tensor_tensor(p3[d][:, :, at(d, i)], p3[d][:, :, at(d, i - 1)],
                                                          f3[d][:, :, at(d, i)], ALU.mult))
                            j = CHUNK - 1 - i
                            c.did(nc.vector.tensor_tensor(s3[d][:, :, at(d, j)], s3[d][:, :, at(d, j + 1)],
                                                          f3[d][:, :, at(d, j + 1)], ALU.mult))
                    c.wait()
                    for d in range(2):
                        nc.vector.tensor_tensor(suf[:, d], suf[:, d], key(d), ALU.mult).then_inc(suf_ready.sem, 1)
                    c.link(nc.vector.tensor_copy(through[:, 0], p3[0][:, :, CHUNK - 1]))
                    turn = through[:, 2:4].rearrange("p x (a b e) -> p x a b e", a=4, b=4)
                    last_first = p3[1][:, :, 0].rearrange("p (a b e) -> p a b e", a=4, b=4)
                    for i in range(4):
                        c.did(nc.vector.tensor_copy(turn[:, 0, 3 - i], last_first[:, i]))
                    c.wait()
                    for i in range(4):
                        c.did(nc.vector.tensor_copy(turn[:, 1, :, 3 - i], turn[:, 0, :, i]))
                    c.wait()
                    by_e = [through[:, i].rearrange("p (a e) -> p a e", e=4) for i in (3, 1)]
                    for i in range(4):
                        c.did(nc.vector.tensor_copy(by_e[1][:, :, 3 - i], by_e[0][:, :, i]))
                    c.wait()
                    nc.vector.memset(through[:, 0:2, 0:1], 0.0).then_inc(s_through, 1)
                    read_out.wait(dve, (u, f"v{un['nv'] - 1}", 1))
                    read_out.wait(dve, (u, "q", 1))
                    for d in range(2):
                        lags(dve, c, u, d)
                        U_ready.wait(dve, (u, d, TT - 1))
                        spread_ready.wait(dve, (u, d))
                        states = U[:].rearrange("p v n -> p (v n)")
                        nc.vector.tensor_tensor_scan(states, factors[:].rearrange("p v n -> p (v n)"), states, 0.0,
                                                     ALU.mult, ALU.add).then_inc(state_ready.sem, 1)
                        spread_query(dve, c, u, d, 0)
                    for j in range(2 * un["nv"]):
                        add_between(dve, c, u, 1, j)
                    dve.sem_inc(s_done, 1)
                    for vt_ in range(un["nv"]):
                        gain = cols[:, C_GLAN:C_GLAN + 1] if u == 0 else cols[:, C_HGRNN:C_HGRNN + 1]
                        for f in range(2):
                            m = fin_keys.index((u, vt_, f))
                            dve.wait_ge(s_fm, m + 1)
                            t0 = tmp[:, m % 2, :]
                            c.link(nc.vector.reciprocal(t0, t0))
                            c.link(nc.vector.tensor_tensor(t0, t0, half(oacc[:, vt_], f), ALU.mult))
                            if m >= 2:
                                dve.wait_ge(s_yo[m % 2], 16 * (m // 2))
                            nc.vector.scalar_tensor_tensor(ys[:, m % 2, :], t0, gain, half(gate[:, vt_], f),
                                                           ALU.mult, ALU.mult).then_inc(fin_y.sem, 1)


def bass_stack(nc, d, out):
    x_all = nc.dram_tensor("x_layers", [DEPTH + 1, SEQ, D], F32, kind="Internal").ap()
    y_dram = nc.dram_tensor("mixed", [KT, P, SEQ], F32, kind="Internal").ap()
    with ExitStack() as ctx:
        sems = []

        def S(name):
            s = ctx.enter_context(nc.semaphore(name))
            sems.append(s)
            return s

        sb = lambda name, shape, dt=F32: ctx.enter_context(nc.sbuf_tensor(name, shape, dt))
        K = sb("consts", [P, K_N])
        s_k = ctx.enter_context(nc.semaphore("consts_in"))
        s_x0 = ctx.enter_context(nc.semaphore("x_copied"))
        with nc.Block() as block:
            @block.sync
            def _(sp):
                sp.dma_start(x_all[0], d["x"].rearrange("b s d -> (b s) d")).then_inc(s_x0, 16)
                sp.dma_start(K[:], d["consts"]).then_inc(s_k, 16)
                sp.wait_ge(s_k, 16)
                sp.wait_ge(s_x0, 16)

        def w_in(l, off, width):
            return d["w_in"][bass.ds(l, 1), :, off:off + width].rearrange("o (k p) n -> p (o k) n", p=P)

        with nc.Fori(0, DEPTH) as l:
            with ExitStack() as lctx:
                hT = lctx.enter_context(nc.sbuf_tensor("hT", [P, KT, SEQ], F32))
                cols = lctx.enter_context(nc.sbuf_tensor("cols", [P, C_N], F32))
                rows = lctx.enter_context(nc.sbuf_tensor("rows", [P, R_N], F32))
                s_par = S("params")
                start = nc.gpsimd
                mark = len(sems)
                clear_at = nc
                with nc.Block() as block:
                    @block.sync
                    def _(sp):
                        sp.dma_start(cols[:], d["cols"][bass.ds(l, 1)].rearrange("o p n -> p (o n)")).then_inc(s_par, 16)
                        sp.dma_start(rows[:], d["rows"][bass.ds(l, 1)].broadcast_to([P, R_N])).then_inc(s_par, 16)
                        sp.wait_ge(s_par, 32)
                norm_transpose(nc, S, lambda t: x_all[bass.ds(l, 1), t * P:(t + 1) * P, :].rearrange("o p n -> p (o n)"),
                               cols[:, C_PRE:C_PRE + 8], hT, K[:, K_ID:K_ID + P], K[:, K_NH:K_NH + 1], "a_")
                diff_attention(nc, S, l, w_in, hT, y_dram, K, rows)
                gated_scans(nc, S, l, w_in, lambda l: d["wa2"][bass.ds(l, 1)].rearrange("o r n -> r (o n)"), hT, y_dram, K, cols)
                out_project(nc, S, y_dram, d["w_out"][bass.ds(l, 1)].rearrange("o (k p) n -> p (o k) n", p=P),
                            lambda t: x_all[bass.ds(l, 1), t * P:(t + 1) * P, :].rearrange("o p n -> p (o n)"),
                            lambda t: x_all[bass.ds(l + 1, 1), t * P:(t + 1) * P, :].rearrange("o p n -> p (o n)"),
                            rows[:, R_POST:R_POST + D], K[:, K_NH:K_NH + 1], "a_")
                nc.all_engine_barrier()
                for s in sems:
                    nc.gpsimd.sem_clear(s)
                nc.all_engine_barrier()
        return x_all




D_CONV = 512
CT = D_CONV // P
CONV_W, LRU_W, LRU_C = 31, 4, 8.0
N_GROUPS, PER_GROUP = 4, 8
N_EXP = N_GROUPS * PER_GROUP
D_EXP = 512
FT = D_EXP // P
PLE = 256
N_OVER = 2 * SEQ // P
N_SLOTS = (N_EXP + N_OVER) * P
BIG = 1e30

(C2_MIX, C2_CW, C2_CB, C2_LG, C2_LB, C2_LW, C2_LCB, C2_BR, C2_BI, C2_LAM, C2_N) = (
    0, 8, 132, 136, 140, 144, 160, 164, 168, 172, 176)
R2_FFN, R2_B, R2_PLE, R2_PROJ, R2_FIN, R2_N = 0, 1024, 1060, 2084, 3108, 4132
K2_ONE, K2_MEAN, K2_TRI, K2_REV, K2_REVG, K2_E, K2_O, K2_TOK, K2_EPS, K2_N = 0, 128, 256, 384, 416, 420, 452, 468, 476, 477


def mixer(nc, S, w_dram, wr_dram, hT, y_dram, K2, cols, clear_extra):
    column = dict(v=0, g=D_CONV, x=2 * D_CONV, l=3 * D_CONV)
    order = [(n, column[n[0]] + P * int(n[1]))
             for n in "g0 v0 g1 v1 x0 l0 x1 g2 v2 g3 v3 l1 x2 l2 x3 l3".split()]
    items = [n for n, _ in order]
    banks = [(n, f) for n in items for f in range(2)]
    PAD = CONV_W - 1
    with ExitStack() as ctx:
        sb = lambda name, shape, dt=F32: ctx.enter_context(nc.sbuf_tensor(name, shape, dt))
        wt = sb("mx_w", [P, 4, KT, P])
        wri = sb("mx_wri", [P, 2, CT, P])
        ub = sb("mx_u", [P, CT, PAD + SEQ])
        sg = sb("mx_sg", [P, 2, HALF])
        cb = sb("mx_c", [P, CT, SEQ])
        yo = sb("mx_y", [P, 2, SEQ])
        xb = sb("mx_x", [P, CT, LRU_W - 1 + SEQ])
        gl = sb("mx_gl", [P, CT, SEQ])
        xr = sb("mx_xr", [P, 2, SEQ])
        mu = sb("mx_mu", [P, SEQ])
        ra = sb("mx_r", [P, 2, SEQ])
        th = sb("mx_t", [P, 2, SEQ])
        ia = sb("mx_i", [P, 2, SEQ])
        sp_ = sb("mx_sp", [P, 6, CT])
        pp = [ctx.enter_context(nc.psum_tensor(f"mx_p{i}", [P, HALF], F32)) for i in range(4)]
        pc = ctx.enter_context(nc.psum_tensor("mx_pc", [P, 2, SEQ], F32))
        s_w = [S(f"mx_w{i}") for i in range(4)]
        s_wri, s_clear, s_c = S("mx_wri"), S("mx_clear"), S("mx_chain")
        proj_done = Signal(S("mx_proj"), banks)
        act_read = Signal(S("mx_ar"), [b for b in banks if b[0][0] != "v"])
        u_ready = Signal(S("mx_ur"), [b for b in banks if b[0][0] == "v"])
        tiles = list(range(CT))
        conv_done = Signal(S("mx_cv"), tiles)
        c_ready = Signal(S("mx_cr"), tiles)
        s_mu, s_cen, s_sq, s_var, s_sd, s_rs, s_nrm = (S("mx_mu"), S("mx_cen"), S("mx_sq"), S("mx_var"), S("mx_sd"),
                                                    S("mx_rs"), S("mx_nrm"))
        s_y = [S("mx_y0"), S("mx_y1")]
        y_ready = Signal(S("mx_yr"), [("c", j) for j in tiles] + [("l", j) for j in tiles])
        lconv, xr_ready = Signal(S("mx_lc"), tiles), Signal(S("mx_xr"), tiles)
        gk = [(j, w, f) for j in tiles for w in range(2) for f in range(2)]
        gate_sum, gate_read = Signal(S("mx_gs"), gk), Signal(S("mx_gr"), gk)
        s_sp, s_nl, s_at, s_m, s_rt, s_ly = S("mx_sp"), S("mx_nl"), S("mx_at"), S("mx_m"), S("mx_rt"), S("mx_ly")
        half = lambda ap, f: ap[:, f * HALF:(f + 1) * HALF]

        def read_bank(eng, b):
            (u_ready if b[0][0] == "v" else act_read).wait(eng, b)

        with nc.Block() as block:
            @block.sync
            def _(sp):
                for i, (name, off) in enumerate(order):
                    if i >= 4:
                        proj_done.wait(sp, (items[i - 4], 1))
                    sp.dma_start(wt[:, i % 4], w_dram(off)).then_inc(s_w[i % 4], 16)
                    if i == 3:
                        sp.dma_start(wri[:], wr_dram).then_inc(s_wri, 16)
                clear_extra(sp, s_clear)
                for n, key in enumerate(y_ready.order):
                    y_ready.wait(sp, key)
                    sp.dma_start(y_dram[n], yo[:, n % 2, :]).then_inc(s_y[n % 2], 16)
                for j in range(2):
                    sp.wait_ge(s_y[j], 16 * CT)
                sp.wait_ge(s_clear, 16)

            @block.tensor
            def _(pe):
                for i, (name, _) in enumerate(order):
                    pe.wait_ge(s_w[i % 4], 16 * (i // 4 + 1))
                    for f in range(2):
                        n = 2 * i + f
                        if n >= 4:
                            read_bank(pe, banks[n - 4])
                        for k in range(KT):
                            last = nc.tensor.matmul(pp[n % 4][:], wt[:, i % 4, k, :], half(hT[:, k], f),
                                                    start=(k == 0), stop=(k == KT - 1))
                        last.then_inc(proj_done.sem, 1)
                act_read.all(pe)
                c_ready.all(pe)
                for f in range(2):
                    for j in range(CT):
                        last = nc.tensor.matmul(pp[f][:], K2[:, K2_MEAN:K2_MEAN + P], half(cb[:, j], f),
                                                start=(j == 0), stop=(j == CT - 1))
                    last.then_inc(s_mu, 1)
                for j in range(CT):
                    for f in range(2):
                        pe.wait_ge(s_sq, 2 * j + f + 1)
                        last = nc.tensor.matmul(pp[2 + f][:], K2[:, K2_MEAN:K2_MEAN + P],
                                                half(th[:, j % 2], f), start=(j == 0), stop=(j == CT - 1))
                    last.then_inc(s_var, 1)
                pe.wait_ge(s_sd, 2)
                pe.wait_ge(s_cen, 1)
                pe.wait_ge(s_wri, 16)
                for n, (j, w, f) in enumerate(gk):
                    xr_ready.wait(pe, j)
                    if n >= 4:
                        gate_read.wait(pe, gk[n - 4])
                    nc.tensor.matmul(pp[n % 4][:], wri[:, w, j, :], half(xr[:, j % 2], f), start=True,
                                     stop=True).then_inc(gate_sum.sem, 1)

            @block.scalar
            def _(act):
                conv_at = {"g2": (0, 1), "l3": (2, 3)}
                for name, _ in order:
                    for f in range(2):
                        n = banks.index((name, f))
                        src = pp[n % 4][:]
                        j = int(name[1])
                        if name[0] == "v":
                            continue
                        proj_done.wait(act, (name, f))
                        if name[0] == "g":
                            if j:
                                u_ready.wait(act, ("v" + str(j - 1), f))
                            ins = nc.scalar.activation(sg[:, f, :], src, ACT.Sigmoid)
                        elif name[0] == "x":
                            ins = nc.scalar.activation(xb[:, j, LRU_W - 1 + f * HALF:LRU_W - 1 + (f + 1) * HALF], src, ACT.Copy)
                        else:
                            ins = nc.scalar.activation(half(gl[:, j], f), src, ACT.Copy)
                        ins.then_inc(act_read.sem, 1)
                    for j in conv_at.get(name, ()):
                        conv_done.wait(act, j)
                        nc.scalar.activation(cb[:, j], pc[:, j % 2], ACT.Identity,
                                             bias=cols[:, C2_CB + j:C2_CB + j + 1]).then_inc(c_ready.sem, 1)
                def short_conv_out(j):
                    lconv.wait(act, j)
                    if j >= 2:
                        gate_sum.wait(act, (j - 2, 1, 1))
                        y_ready.wait(act, ("l", j - 2))
                    nc.scalar.activation(xr[:, j % 2], pc[:, j % 2], ACT.Identity,
                                         bias=cols[:, C2_LCB + j:C2_LCB + j + 1]).then_inc(xr_ready.sem, 1)

                short_conv_out(0)
                short_conv_out(1)
                for j in tiles:
                    act.wait_ge(s_cen, j + 1)
                    if j >= 2:
                        act.wait_ge(s_var, j - 1)
                    for f in range(2):
                        nc.scalar.activation(half(th[:, j % 2], f), half(cb[:, j], f), ACT.Square).then_inc(s_sq, 1)
                act.wait_ge(s_var, CT)
                for f in range(2):
                    nc.scalar.activation(half(mu, f), pp[2 + f][:], ACT.Sqrt, bias=K2[:, K2_EPS:K2_EPS + 1]).then_inc(s_sd, 1)
                for j in tiles:
                    act.wait_ge(s_nrm, j + 1)
                    if j >= 2:
                        act.wait_ge(s_y[j % 2], 16 * (j // 2))
                    nc.scalar.activation(yo[:, j % 2], cb[:, j], ACT.Silu, scale=cols[:, C2_LG + j:C2_LG + j + 1],
                                         bias=cols[:, C2_LB + j:C2_LB + j + 1]).then_inc(y_ready.sem, 1)
                for j in tiles:
                    nc.scalar.activation(gl[:, j], gl[:, j], ACT.Gelu_apprx_tanh).then_inc(s_ly, 1)
                act.wait_ge(s_sp, 1)
                nc.scalar.activation(sp_[:, 1, :], sp_[:, 0, :], ACT.Exp, scale=-1.0).then_inc(s_sp, 1)
                for j in tiles:
                    if j >= 2:
                        short_conv_out(j)
                    for w in range(2):
                        for f in range(2):
                            n = gk.index((j, w, f))
                            gate_sum.wait(act, (j, w, f))
                            col = (C2_BR, C2_BI)[w] + j
                            nc.scalar.activation(half((ra, ia)[w][:, j % 2], f), pp[n % 4][:], ACT.Sigmoid,
                                                 bias=cols[:, col:col + 1]).then_inc(gate_read.sem, 1)
                    act.wait_ge(s_nl, 1)
                    gate_read.wait(act, (j, 0, 1))
                    nc.scalar.activation(th[:, j % 2], ra[:, j % 2], ACT.Tanh, scale=sp_[:, 5, j:j + 1]).then_inc(s_at, 1)
                    nc.scalar.activation(ra[:, j % 2], ra[:, j % 2], ACT.Exp, scale=sp_[:, 5, j:j + 1]).then_inc(s_at, 1)
                    act.wait_ge(s_m, j + 1)
                    nc.scalar.activation(th[:, j % 2], th[:, j % 2], ACT.Sqrt).then_inc(s_rt, 1)

            @block.vector
            def _(dve):
                c = Chain(dve, s_c)
                c.did(nc.vector.memset(ub[:, :, 0:PAD], 0.0))
                c.did(nc.vector.memset(xb[:, :, 0:LRU_W - 1], 0.0))
                for j in tiles:
                    for f in range(2):
                        b = ("v" + str(j), f)
                        proj_done.wait(dve, b)
                        act_read.wait(dve, ("g" + str(j), f))
                        nc.vector.tensor_tensor(ub[:, j, PAD + f * HALF:PAD + (f + 1) * HALF], pp[banks.index(b) % 4][:],
                                                sg[:, f, :], ALU.mult).then_inc(u_ready.sem, 1)
                    if j % 2 == 0:
                        continue
                    u_ready.wait(dve, b)
                    c.wait()
                    if j > 1:
                        c_ready.wait(dve, j - 2)
                    for tap in range(CONV_W):
                        for jj in (j - 1, j):
                            acc = pc[:, jj % 2]
                            wcol = cols[:, C2_CW + tap * CT + jj:C2_CW + tap * CT + jj + 1]
                            src = ub[:, jj, tap:tap + SEQ]
                            if tap:
                                c.wait(c.n if tap == CONV_W - 1 and jj == j else c.n - 1)
                                ins = nc.vector.scalar_tensor_tensor(acc, src, wcol, acc, ALU.mult, ALU.add)
                            else:
                                ins = nc.vector.tensor_scalar(acc, src, wcol, None, ALU.mult)
                            if tap < CONV_W - 1:
                                c.did(ins)
                            else:
                                ins.then_inc(conv_done.sem, 1)
                lam = cols[:, C2_LAM:C2_LAM + CT]
                c.link(nc.vector.tensor_scalar(sp_[:, 4, :], lam, -1.0, None, ALU.mult))
                nc.vector.tensor_tensor(sp_[:, 0, :], lam, sp_[:, 4, :], ALU.max).then_inc(s_sp, 1)
                c.link(nc.vector.tensor_scalar(sp_[:, 4, :], sp_[:, 4, :], 0.0, None, ALU.max))
                def short_conv(j):
                    if j >= 2:
                        xr_ready.wait(dve, j - 2)
                    else:
                        c_ready.wait(dve, CT - 2 + j)
                    acc = pc[:, j % 2]
                    for tap in range(LRU_W):
                        wcol = cols[:, C2_LW + tap * CT + j:C2_LW + tap * CT + j + 1]
                        src = xb[:, j, tap:tap + SEQ]
                        if tap:
                            c.wait()
                            ins = nc.vector.scalar_tensor_tensor(acc, src, wcol, acc, ALU.mult, ALU.add)
                        else:
                            ins = nc.vector.tensor_scalar(acc, src, wcol, None, ALU.mult)
                        if tap < LRU_W - 1:
                            c.did(ins)
                        else:
                            ins.then_inc(lconv.sem, 1)

                act_read.all(dve)
                short_conv(0)
                short_conv(1)
                dve.wait_ge(s_mu, 2)
                for j in tiles:
                    c.did(nc.vector.tensor_tensor(half(cb[:, j], 0), half(cb[:, j], 0), pp[0][:], ALU.subtract))
                    c.did(nc.vector.tensor_tensor(half(cb[:, j], 1), half(cb[:, j], 1), pp[1][:], ALU.subtract))
                    c.wait()
                    dve.sem_inc(s_cen, 1)
                dve.wait_ge(s_sd, 2)
                c.link(nc.vector.reciprocal(mu[:], mu[:]))
                for j in tiles:
                    nc.vector.tensor_tensor(cb[:, j], cb[:, j], mu[:], ALU.mult).then_inc(s_nrm, 1)
                dve.wait_ge(s_sp, 2)
                y1, z, z2, s1 = sp_[:, 1, :], sp_[:, 2, :], sp_[:, 3, :], sp_[:, 5, :]
                c.link(nc.vector.tensor_scalar(z2, y1, 2.0, None, ALU.add))
                c.link(nc.vector.reciprocal(z2, z2))
                c.link(nc.vector.tensor_tensor(z, y1, z2, ALU.mult))
                c.link(nc.vector.tensor_tensor(z2, z, z, ALU.mult))
                c.link(nc.vector.memset(s1, 1.0 / 17))
                for n in range(15, 0, -2):
                    c.link(nc.vector.tensor_tensor(s1, s1, z2, ALU.mult))
                    c.link(nc.vector.tensor_scalar(s1, s1, 1.0 / n, None, ALU.add))
                c.link(nc.vector.tensor_tensor(s1, s1, z, ALU.mult))
                c.link(nc.vector.tensor_scalar(s1, s1, 2.0, None, ALU.mult))
                c.link(nc.vector.tensor_tensor(s1, s1, sp_[:, 4, :], ALU.add))
                nc.vector.tensor_scalar(s1, s1, -LRU_C, None, ALU.mult).then_inc(s_nl, 1)

                for j in tiles:
                    if j + 2 < CT:
                        short_conv(j + 2)
                    dve.wait_ge(s_at, 2 * j + 2)
                    t, i_ = th[:, j % 2], ia[:, j % 2]
                    if j:
                        y_ready.wait(dve, ("l", j - 1))
                    c.link(nc.vector.tensor_scalar(mu[:], t, -1.0, 1.0, ALU.mult, ALU.add))
                    c.link(nc.vector.reciprocal(mu[:], mu[:]))
                    nc.vector.scalar_tensor_tensor(t, t, -2.0, mu[:], ALU.mult, ALU.mult).then_inc(s_m, 1)
                    gate_read.wait(dve, (j, 1, 1))
                    c.link(nc.vector.tensor_tensor(i_, i_, xr[:, j % 2], ALU.mult))
                    dve.wait_ge(s_rt, j + 1)
                    c.link(nc.vector.tensor_tensor(i_, i_, t, ALU.mult))
                    c.link(nc.vector.tensor_tensor_scan(mu[:], ra[:, j % 2], i_, 0.0, ALU.mult, ALU.add))
                    dve.wait_ge(s_ly, j + 1)
                    dve.wait_ge(s_y[j % 2], 16 * (j // 2 + 2))
                    nc.vector.tensor_tensor(yo[:, j % 2], mu[:], gl[:, j], ALU.mult).then_inc(y_ready.sem, 1)


def norm_route(nc, S, x_dram, hf_dram, wr_dram, rows, K, K2, R):
    with ExitStack() as ctx:
        sb = lambda name, shape, dt=F32: ctx.enter_context(nc.sbuf_tensor(name, shape, dt))
        xt = sb("nr_x", [P, 2, D])
        sq = sb("nr_sq", [P, D])
        xn = sb("nr_n", [P, 2, D])
        hT = sb("nr_hT", [P, 2, KT, P])
        ss = sb("nr_ss", [P, TT])
        rstd = sb("nr_r", [P, TT])
        wr = sb("nr_w", [P, KT, N_GROUPS + N_EXP])
        L = sb("nr_L", [P, TT, N_GROUPS + N_EXP])
        ps = ctx.enter_context(nc.psum_tensor("nr_ps", [P, 2, KT, P], F32))
        pl = [ctx.enter_context(nc.psum_tensor(f"nr_pl{i}", [P, HALF], F32)) for i in range(2)]
        pt = [ctx.enter_context(nc.psum_tensor(f"nr_pt{i}", [P, HALF], F32)) for i in range(2)]
        s_x, s_st = [S("nr_x0"), S("nr_x1")], [S("nr_s0"), S("nr_s1")]
        s_w, s_sq, s_rs, s_n, s_t, s_h, s_l, s_L, s_pc, s_c = (S("nr_w"), S("nr_sq"), S("nr_rs"), S("nr_n"), S("nr_t"),
            S("nr_h"), S("nr_l"), S("nr_L"), S("nr_pool"), S("nr_chain"))
        s_a, s_a2, s_M, s_cnt = S("nr_a"), S("nr_a2"), S("nr_M"), S("nr_cnt")
        G = lambda name, *shape: sb("nr_" + name, [P, *shape])
        gm, gs, oh4, em = G("gm", TT), G("gs", TT), G("oh4", TT, 4), G("em", TT, N_EXP)
        oh = G("oh", 2, TT, N_EXP)
        mm, mx, tmp, tmp4, M = G("mm", 2, TT), G("mx", TT), G("tmp", TT, N_EXP), G("tmp4", TT, 4), G("M", TT, N_EXP)
        pos, cum, nb, incl, ex, ob = (G("pos", TT, N_EXP), G("cum", TT + 1, N_EXP), G("nb", N_EXP), G("incl", N_EXP),
                                      G("ex", N_OVER, N_EXP), G("ob", N_OVER + 1))
        one = G("one", N_EXP)
        sl = G("sl", 2, TT)
        gx = G("gx", 4, TT)
        spread = lambda ap, n: ap.unsqueeze(2).broadcast_to([P, TT, n])
        across = lambda ap, n: ap.unsqueeze(1).broadcast_to([P, TT, n])
        with nc.Block() as block:
            @block.sync
            def _(sp):
                sp.dma_start(wr[:], wr_dram).then_inc(s_w, 16)
                for t in range(TT):
                    if t >= 2:
                        sp.wait_ge(s_sq, t - 1)
                        sp.wait_ge(s_n, t - 1)
                    sp.dma_start(xt[:, t % 2, :], x_dram[t * P:(t + 1) * P, :]).then_inc(s_x[t % 2], 16)

            def store(act, t):
                act.wait_ge(s_n, t + 1)
                act.dma_start(hf_dram[t * P:(t + 1) * P, :], xn[:, t % 2, :]).then_inc(s_st[t % 2], 16)

            @block.scalar
            def _(act):
                for t in range(TT):
                    act.wait_ge(s_x[t % 2], 16 * (t // 2 + 1))
                    if t:
                        act.wait_ge(s_sq, t)
                    nc.scalar.activation(sq[:], xt[:, t % 2, :], ACT.Square, accum_out=ss[:, t:t + 1]).then_inc(s_sq, 1)
                    if t:
                        store(act, t - 1)
                store(act, TT - 1)
                act.wait_ge(s_a, 1)
                nc.scalar.activation(tmp4[:], tmp4[:], ACT.Exp).then_inc(s_a2, 1)
                act.wait_ge(s_a, 2)
                nc.scalar.activation(gx[:, 0, :], gx[:, 0, :], ACT.Exp).then_inc(s_a2, 1)
                for j in range(2):
                    act.wait_ge(s_st[j], 16 * TT // 2)

            @block.gpsimd
            def _(pool):
                c = Chain(pool, s_pc)
                for t in range(TT):
                    pool.wait_ge(s_sq, t + 1)
                    rsqrt_of_mean(nc, c, rstd[:, t:t + 1], ss[:, t:t + 1], D, K[:, P:P + 1]).then_inc(s_rs, 1)

            def logits(pe, t):
                if t == 0:
                    pe.wait_ge(s_w, 16)
                pe.wait_ge(s_h, t + 1)
                if t >= 2:
                    pe.wait_ge(s_L, t - 1)
                for k in range(KT):
                    last = nc.tensor.matmul(pl[t % 2][:, 0:36], hT[:, t % 2, k, :], wr[:, k, :], start=(k == 0), stop=(k == KT - 1))
                last.then_inc(s_l, 1)

            @block.tensor
            def _(pe):
                for t in range(TT):
                    pe.wait_ge(s_n, t + 1)
                    if t >= 2:
                        pe.wait_ge(s_h, t - 1)
                    for k in range(KT):
                        last = nc.tensor.transpose(ps[:, t % 2, k, :], xn[:, t % 2, k * P:(k + 1) * P], K[:, K_ID:K_ID + P])
                    last.then_inc(s_t, 1)
                    if t:
                        logits(pe, t - 1)
                logits(pe, TT - 1)
                pe.wait_ge(s_M, 1)
                flat = M[:].rearrange("p t e -> p (t e)")
                nc.tensor.matmul(pt[0][:, 0:TT * N_EXP], K2[:, K2_TRI:K2_TRI + P], flat, start=True, stop=True)
                nc.tensor.matmul(pt[1][:, 0:TT * N_EXP], K2[:, K2_ONE:K2_ONE + P], flat, start=True, stop=True).then_inc(s_cnt, 1)

            def add_bias(dve, t):
                dve.wait_ge(s_l, t + 1)
                nc.vector.tensor_tensor(L[:, t, :], pl[t % 2][:, 0:36], rows[:, R2_B:R2_B + 36], ALU.add).then_inc(s_L, 1)

            @block.vector
            def _(dve):
                c = Chain(dve, s_c)
                for t in range(TT):
                    dve.wait_ge(s_rs, t + 1)
                    dve.wait_ge(s_x[t % 2], 16 * (t // 2 + 1))
                    if t >= 2:
                        dve.wait_ge(s_t, t - 1)
                        dve.wait_ge(s_st[t % 2], 16 * (t // 2))
                    nc.vector.scalar_tensor_tensor(xn[:, t % 2, :], xt[:, t % 2, :], rstd[:, t:t + 1],
                                                   rows[:, R2_FFN:R2_FFN + D], ALU.mult, ALU.mult).then_inc(s_n, 1)
                    dve.wait_ge(s_t, t + 1)
                    if t >= 2:
                        dve.wait_ge(s_l, t - 1)
                    nc.vector.tensor_copy(hT[:, t % 2], ps[:, t % 2]).then_inc(s_h, 1)
                    if t:
                        add_bias(dve, t - 1)
                add_bias(dve, TT - 1)
                dve.wait_ge(s_L, TT)
                V = nc.vector
                gl, el = L[:, :, 0:4], L[:, :, 4:36]
                c.link(V.tensor_reduce(gm[:], gl, AX.X, ALU.max))
                V.tensor_tensor(tmp4[:], gl, spread(gm[:], 4), ALU.subtract).then_inc(s_a, 1)
                c.link(V.tensor_tensor(oh4[:], gl, spread(gm[:], 4), ALU.is_equal))
                c.link(V.tensor_tensor(oh4[:], oh4[:], across(K2[:, K2_REVG:K2_REVG + 4], 4), ALU.mult))
                c.link(V.tensor_reduce(gs[:], oh4[:], AX.X, ALU.max))
                c.link(V.tensor_tensor(oh4[:], across(K2[:, K2_REVG:K2_REVG + 4], 4), spread(gs[:], 4), ALU.is_equal))
                c.link(V.tensor_scalar(oh4[:], oh4[:], BIG, -BIG, ALU.mult, ALU.add))
                for g in range(N_GROUPS):
                    cols8 = slice(g * PER_GROUP, (g + 1) * PER_GROUP)
                    c.did(V.tensor_tensor(em[:, :, cols8], L[:, :, 4 + g * PER_GROUP:4 + (g + 1) * PER_GROUP],
                                          spread(oh4[:, :, g], PER_GROUP), ALU.add))
                c.wait()
                rev = across(K2[:, K2_REV:K2_REV + N_EXP], N_EXP)
                for n in range(2):
                    c.link(V.tensor_reduce(mm[:, n, :], em[:], AX.X, ALU.max))
                    c.link(V.tensor_tensor(tmp[:], em[:], spread(mm[:, n, :], N_EXP), ALU.is_equal))
                    c.link(V.tensor_tensor(tmp[:], tmp[:], rev, ALU.mult))
                    c.link(V.tensor_reduce(mx[:], tmp[:], AX.X, ALU.max))
                    c.link(V.tensor_tensor(oh[:, n], rev, spread(mx[:], N_EXP), ALU.is_equal))
                    if n == 0:
                        c.link(V.tensor_scalar(tmp[:], oh[:, 0], -2 * BIG, None, ALU.mult))
                        c.link(V.tensor_tensor(em[:], em[:], tmp[:], ALU.add))
                V.tensor_tensor(M[:], oh[:, 0], oh[:, 1], ALU.add).then_inc(s_M, 1)
                V.tensor_tensor(gx[:, 0, :], mm[:, 1, :], mm[:, 0, :], ALU.subtract).then_inc(s_a, 1)
                dve.wait_ge(s_a2, 2)
                c.link(V.reduce_sum(gs[:], tmp4[:], AX.X))
                c.link(V.tensor_scalar(gx[:, 1, :], gx[:, 0, :], 1.0, None, ALU.add))
                c.link(V.tensor_tensor(gs[:], gs[:], gx[:, 1, :], ALU.mult))
                c.link(V.reciprocal(R["gates"][:, 0, :], gs[:]))
                c.link(V.tensor_tensor(R["gates"][:, 1, :], R["gates"][:, 0, :], gx[:, 0, :], ALU.mult))
                dve.wait_ge(s_cnt, 1)
                c.link(V.memset(cum[:, 0, :], 0.0))
                for t in range(TT):
                    c.link(V.tensor_tensor(cum[:, t + 1, :], cum[:, t, :], pt[1][:, t * N_EXP:(t + 1) * N_EXP], ALU.add))
                c.link(V.tensor_tensor(pos[:], pt[0][:, 0:TT * N_EXP].rearrange("p (t e) -> p t e", e=N_EXP), cum[:, 0:TT, :],
                                       ALU.add))
                c.did(V.memset(one[:], 1.0))
                c.link(V.tensor_scalar(nb[:], cum[:, TT, :], float(P), None, ALU.is_gt))
                for k in range(2, TT):
                    c.link(V.scalar_tensor_tensor(nb[:], cum[:, TT, :], float(P * k), nb[:], ALU.is_gt, ALU.add))
                c.link(V.tensor_tensor_scan(incl[:], one[:], nb[:], 0.0, ALU.mult, ALU.add))
                c.link(V.tensor_tensor(nb[:], incl[:], nb[:], ALU.subtract))
                c.link(V.tensor_tensor(nb[:], nb[:], K2[:, K2_E:K2_E + N_EXP], ALU.subtract))
                c.link(V.tensor_scalar(nb[:], nb[:], float(N_EXP - 1), float(P), ALU.add, ALU.mult))
                c.link(V.tensor_scalar(tmp[:], pos[:], float(P), None, ALU.is_ge))
                c.link(V.tensor_tensor(tmp[:], tmp[:], across(nb[:], N_EXP), ALU.mult))
                c.link(V.tensor_tensor(pos[:], pos[:], tmp[:], ALU.add))
                c.link(V.tensor_scalar(one[:], K2[:, K2_E:K2_E + N_EXP], float(P), None, ALU.mult))
                c.link(V.tensor_tensor(pos[:], pos[:], across(one[:], N_EXP), ALU.add))
                for n in range(2):
                    c.link(V.tensor_tensor(tmp[:], pos[:], oh[:, n], ALU.mult))
                    c.link(V.reduce_sum(sl[:, n, :], tmp[:], AX.X))
                c.link(V.tensor_copy(R["slots"], sl[:]))
                c.did(V.tensor_copy(ob[:, 0:1], incl[:, N_EXP - 1:N_EXP]))
                c.link(V.tensor_tensor(ex[:], incl[:].unsqueeze(1).broadcast_to([P, N_OVER, N_EXP]),
                                       K2[:, K2_O:K2_O + N_OVER].unsqueeze(2).broadcast_to([P, N_OVER, N_EXP]), ALU.is_le))
                c.link(V.reduce_sum(ob[:, 1:], ex[:], AX.X))
                c.link(V.tensor_scalar(ob[:, 1:], ob[:, 1:], float(N_EXP - 1), None, ALU.min))
                c.link(V.tensor_copy(R["over"], ob[:]))


def token_lists(nc, S, R, tok, idx_dram, idx, K):
    NB = N_SLOTS // P
    with ExitStack() as ctx:
        zero = ctx.enter_context(nc.sbuf_tensor("tl_zero", [NB, P], F32))
        lists = ctx.enter_context(nc.sbuf_tensor("tl_lists", [NB, P], F32))
        ps = ctx.enter_context(nc.psum_tensor("tl_ps", [P, NB], F32))
        s_z, s_zd, s_in, s_t, s_i = S("tl_z"), S("tl_zd"), S("tl_in"), S("tl_t"), S("tl_i")
        s_sc = S("tl_sc")
        by_block = idx_dram.rearrange("(b p) o -> b (p o)", p=P)
        with nc.Block() as block:
            @block.vector
            def _(dve):
                nc.vector.memset(zero[:], 0.0).then_inc(s_z, 1)
                dve.wait_ge(s_t, 1)
                nc.vector.tensor_copy(idx[:], ps[:]).then_inc(s_i, 1)

            @block.sync
            def _(sp):
                sp.wait_ge(s_z, 1)
                sp.dma_start(by_block, zero[:]).then_inc(s_zd, 16)
                sp.wait_ge(s_sc, 16 * 2 * TT)
                sp.dma_start(lists[:], by_block).then_inc(s_in, 16)

            @block.gpsimd
            def _(pool):
                pool.wait_ge(s_zd, 16)
                for n in range(2):
                    for t in range(TT):
                        nc.gpsimd.indirect_dma_start(
                            idx_dram, bass.IndirectOffsetOnAxis(ap=R["slots"][:, n, t:t + 1], axis=0),
                            tok[:, t:t + 1], None).then_inc(s_sc, 16)

            @block.tensor
            def _(pe):
                pe.wait_ge(s_in, 16)
                nc.tensor.transpose(ps[:], lists[:], K[0:NB, K_ID:K_ID + NB]).then_inc(s_t, 1)


def experts(nc, S, w1, w3, w2, hf_dram, y_slots, idx, K):
    with ExitStack() as ctx:
        sb = lambda name, shape, dt=F32: ctx.enter_context(nc.sbuf_tensor(name, shape, dt))
        wa = sb("ex_w13", [P, 2, 2, KT, D_EXP])
        wb = sb("ex_w2", [P, 2, FT, D])
        xe = sb("ex_x", [P, 2, D])
        xT = sb("ex_xT", [P, 2, KT, P])
        sil = sb("ex_s", [P, D_EXP])
        hid = sb("ex_h", [P, D_EXP])
        hidT = sb("ex_hT", [P, 2, FT, P])
        ye = sb("ex_y", [P, 2, D])
        p_x = ctx.enter_context(nc.psum_tensor("ex_px", [P, KT, P], F32))
        p_1 = ctx.enter_context(nc.psum_tensor("ex_p1", [P, D_EXP], F32))
        p_3 = ctx.enter_context(nc.psum_tensor("ex_p3", [P, D_EXP], F32))
        p_t = ctx.enter_context(nc.psum_tensor("ex_pt", [P, FT, P], F32))
        p_y = ctx.enter_context(nc.psum_tensor("ex_py", [P, D], F32))
        s_wa, s_wb = [S("ex_wa0"), S("ex_wa1")], [S("ex_wb0"), S("ex_wb1")]
        s_g, s_o = [S("ex_g0"), S("ex_g1")], [S("ex_o0"), S("ex_o1")]
        x_turned, x_read, h_done, h_act, h_mul, h_turned, h_read, y_done, y_read = (
            S("ex_xt"), S("ex_xr"), S("ex_hd"), S("ex_ha"), S("ex_hm"), S("ex_ht"), S("ex_hr"), S("ex_yd"), S("ex_yr"))
        ident = K[:, K_ID:K_ID + P]
        PAIRS = N_EXP // 2

        with nc.Block() as block:
            @block.sync
            def _(sp):
                def load(e, par, wait):
                    if wait is not None:
                        sp.wait_ge(h_done, wait)
                    for n, w in enumerate((w1, w3)):
                        sp.dma_start(wa[:, par, n], w(e)).then_inc(s_wa[par], 16)
                    if wait is not None:
                        sp.wait_ge(y_done, wait)
                    sp.dma_start(wb[:, par], w2(e)).then_inc(s_wb[par], 16)

                for par in range(2):
                    load(par, par, None)
                with sp.Fori(1, PAIRS) as r:
                    for par in range(2):
                        load(2 * r + par, par, 2 * r + par - 1)

            @block.gpsimd
            def _(pool):
                for e in range(N_EXP):
                    if e >= 2:
                        pool.wait_ge(x_turned, e - 1)
                    nc.gpsimd.indirect_dma_start(xe[:, e % 2, :], None, hf_dram,
                                                 bass.IndirectOffsetOnAxis(ap=idx[:, e:e + 1], axis=0)).then_inc(s_g[e % 2], 16)

            @block.tensor
            def _(pe):
                def turn_x(e, par):
                    pe.wait_ge(s_g[par], 16 * ((e - par) // 2 + 1) if isinstance(e, int) else 8 * (e - par) + 16)
                    if not (isinstance(e, int) and e == 0):
                        pe.wait_ge(x_read, e)
                    for k in range(KT):
                        last = nc.tensor.transpose(p_x[:, k, :], xe[:, par, k * P:(k + 1) * P], ident)
                    last.then_inc(x_turned, 1)

                def first(e, par):
                    pe.wait_ge(s_wa[par], 32 * ((e - par) // 2 + 1) if isinstance(e, int) else 16 * (e - par) + 32)
                    pe.wait_ge(x_read, e + 1)
                    if not (isinstance(e, int) and e == 0):
                        pe.wait_ge(h_mul, e)
                    for n, ps in enumerate((p_1, p_3)):
                        for k in range(KT):
                            last = nc.tensor.matmul(ps[:], xT[:, par, k, :], wa[:, par, n, k, :], start=(k == 0), stop=(k == KT - 1))
                    last.then_inc(h_done, 1)

                def turn_h(e, par):
                    pe.wait_ge(h_mul, e + 1)
                    if not (isinstance(e, int) and e == 0):
                        pe.wait_ge(h_read, e)
                    for k in range(FT):
                        last = nc.tensor.transpose(p_t[:, k, :], hid[:, k * P:(k + 1) * P], ident)
                    last.then_inc(h_turned, 1)

                def second(e, par):
                    pe.wait_ge(s_wb[par], 16 * ((e - par) // 2 + 1) if isinstance(e, int) else 8 * (e - par) + 16)
                    pe.wait_ge(h_read, e + 1)
                    if not (isinstance(e, int) and e == 0):
                        pe.wait_ge(y_read, e)
                    for k in range(FT):
                        for f in range(2):
                            last = nc.tensor.matmul(p_y[:, f * HALF:(f + 1) * HALF], hidT[:, par, k, :],
                                                    wb[:, par, k, f * HALF:(f + 1) * HALF], start=(k == 0), stop=(k == FT - 1))
                    last.then_inc(y_done, 1)

                turn_x(0, 0)
                first(0, 0)
                turn_x(1, 1)
                turn_h(0, 0)

                def middle(e, n):
                    first(e, n % 2)
                    turn_x(e + 1, (n + 1) % 2)
                    second(e - 1, (n + 1) % 2)
                    turn_h(e, n % 2)

                middle(1, 1)
                middle(2, 2)
                with pe.Fori(1, PAIRS - 1) as r:
                    for n in range(1, 3):
                        middle(2 * r + n, n)
                first(N_EXP - 1, 1)
                second(N_EXP - 2, 0)
                turn_h(N_EXP - 1, 1)
                second(N_EXP - 1, 1)

            @block.scalar
            def _(act):
                def copy_x(e, par, later):
                    act.wait_ge(x_turned, e + 1)
                    if later:
                        act.wait_ge(h_done, e - 1)
                    nc.scalar.activation(xT[:, par], p_x[:], ACT.Copy).then_inc(x_read, 1)

                def silu(e, later):
                    act.wait_ge(h_done, e + 1)
                    if later:
                        act.wait_ge(h_mul, e)
                    nc.scalar.activation(sil[:], p_1[:], ACT.Silu).then_inc(h_act, 1)

                def copy_h(e, par, later):
                    act.wait_ge(h_turned, e + 1)
                    if later:
                        act.wait_ge(y_done, e - 1)
                    nc.scalar.activation(hidT[:, par], p_t[:], ACT.Copy).then_inc(h_read, 1)

                def store(e, par):
                    act.wait_ge(y_read, e + 1)
                    act.dma_start(y_slots(e), ye[:, par]).then_inc(s_o[par], 16)

                def middle(e, n):
                    later = not isinstance(e, int) or e >= 2
                    silu(e, True)
                    copy_x(e + 1, (n + 1) % 2, True)
                    copy_h(e, n % 2, later)
                    store(e - 1, (n + 1) % 2)

                copy_x(0, 0, False)
                silu(0, False)
                copy_x(1, 1, False)
                copy_h(0, 0, False)
                middle(1, 1)
                middle(2, 2)
                with act.Fori(1, PAIRS - 1) as r:
                    for n in range(1, 3):
                        middle(2 * r + n, n)
                silu(N_EXP - 1, True)
                copy_h(N_EXP - 1, 1, True)
                store(N_EXP - 2, 0)
                store(N_EXP - 1, 1)
                for j in range(2):
                    act.wait_ge(s_o[j], 16 * PAIRS)

            @block.vector
            def _(dve):
                def steps(e, par, later):
                    dve.wait_ge(h_act, e + 1)
                    if later:
                        dve.wait_ge(h_turned, e)
                    nc.vector.tensor_tensor(hid[:], p_3[:], sil[:], ALU.mult).then_inc(h_mul, 1)

                def result(e, par, later):
                    dve.wait_ge(y_done, e + 1)
                    if later:
                        dve.wait_ge(s_o[par], 8 * (e - par))
                    nc.vector.tensor_copy(ye[:, par], p_y[:]).then_inc(y_read, 1)

                steps(0, 0, False)
                steps(1, 1, True)
                result(0, 0, False)
                steps(2, 0, True)
                result(1, 1, False)
                with dve.Fori(1, PAIRS - 1) as r:
                    for n in range(1, 3):
                        e = 2 * r + n
                        steps(e, n % 2, True)
                        result(e - 1, (n + 1) % 2, True)
                steps(N_EXP - 1, 1, True)
                result(N_EXP - 2, 0, True)
                result(N_EXP - 1, 1, True)


def extra_blocks(nc, S, sems, w1, w3, w2, hf_dram, y_slots, idx, K, over):
    with ExitStack() as ctx:
        sb = lambda name, shape, dt=F32: ctx.enter_context(nc.sbuf_tensor(name, shape, dt))
        wa = sb("xb_w13", [P, 2, KT, D_EXP])
        wb = sb("xb_w2", [P, FT, D])
        xe = sb("xb_x", [P, D])
        xT = sb("xb_xT", [P, KT, P])
        sil = sb("xb_s", [P, D_EXP])
        hidT = sb("xb_hT", [P, FT, P])
        ye = sb("xb_y", [P, D])
        col = sb("xb_i", [P, 1], I32)
        p_x = ctx.enter_context(nc.psum_tensor("xb_px", [P, KT, P], F32))
        p_1 = ctx.enter_context(nc.psum_tensor("xb_p1", [P, D_EXP], F32))
        p_3 = ctx.enter_context(nc.psum_tensor("xb_p3", [P, D_EXP], F32))
        p_t = ctx.enter_context(nc.psum_tensor("xb_pt", [P, FT, P], F32))
        p_y = ctx.enter_context(nc.psum_tensor("xb_py", [P, D], F32))
        first_sem = len(sems)
        s_w = [S("xb_w1"), S("xb_w3"), S("xb_w2")]
        s_i, s_t, s_r, s_h, s_a, s_m, s_y, s_e, s_o = (S("xb_i"), S("xb_t"), S("xb_r"), S("xb_h"),
                                                            S("xb_a"), S("xb_m"), S("xb_y"), S("xb_e"), S("xb_o"))
        s_g = ctx.enter_context(nc.semaphore("xb_gathered"))
        ident = K[:, K_ID:K_ID + P]
        n_over = nc.values_load(over[0:1, 0:1], min_val=0, max_val=N_OVER)
        with nc.If(n_over > 0):
            with nc.Fori(0, N_OVER) as o:
                with nc.If(n_over > o):
                    with nc.Block() as block:
                        @block.sync
                        def _(sp):
                            e = sp.value_load(over[0:1, bass.ds(o + 1, 1)], min_val=0, max_val=N_EXP - 1)
                            for n, w in enumerate((w1, w3)):
                                sp.dma_start(wa[:, n], w(e)).then_inc(s_w[n], 16)
                            sp.dma_start(wb[:], w2(e)).then_inc(s_w[2], 16)
                            sp.wait_ge(s_e, 1)
                            sp.dma_start(y_slots(o + N_EXP), ye[:]).then_inc(s_o, 16)
                            sp.wait_ge(s_o, 16)

                        @block.gpsimd
                        def _(pool):
                            pool.wait_ge(s_i, 1)
                            nc.gpsimd.indirect_dma_start(xe[:], None, hf_dram,
                                                         bass.IndirectOffsetOnAxis(ap=col[:], axis=0)).then_inc(s_g, 16)

                        @block.tensor
                        def _(pe):
                            pe.wait_ge(s_g, 16 * o + 16)
                            for k in range(KT):
                                last = nc.tensor.transpose(p_x[:, k, :], xe[:, k * P:(k + 1) * P], ident)
                            last.then_inc(s_t, 1)
                            pe.wait_ge(s_r, 1)
                            for n, ps in enumerate((p_1, p_3)):
                                pe.wait_ge(s_w[n], 16)
                                for k in range(KT):
                                    last = nc.tensor.matmul(ps[:], xT[:, k, :], wa[:, n, k, :], start=(k == 0), stop=(k == KT - 1))
                            last.then_inc(s_h, 1)
                            pe.wait_ge(s_m, 1)
                            for k in range(FT):
                                last = nc.tensor.transpose(p_t[:, k, :], sil[:, k * P:(k + 1) * P], ident)
                            last.then_inc(s_t, 1)
                            pe.wait_ge(s_r, 2)
                            pe.wait_ge(s_w[2], 16)
                            for k in range(FT):
                                for f in range(2):
                                    last = nc.tensor.matmul(p_y[:, f * HALF:(f + 1) * HALF], hidT[:, k, :],
                                                            wb[:, k, f * HALF:(f + 1) * HALF], start=(k == 0), stop=(k == FT - 1))
                            last.then_inc(s_y, 1)

                        @block.scalar
                        def _(act):
                            act.wait_ge(s_t, 1)
                            nc.scalar.activation(xT[:], p_x[:], ACT.Copy).then_inc(s_r, 1)
                            act.wait_ge(s_h, 1)
                            nc.scalar.activation(sil[:], p_1[:], ACT.Silu).then_inc(s_a, 1)
                            act.wait_ge(s_t, 2)
                            nc.scalar.activation(hidT[:], p_t[:], ACT.Copy).then_inc(s_r, 1)

                        @block.vector
                        def _(dve):
                            nc.vector.tensor_copy(col[:], idx[:, bass.ds(o + N_EXP, 1)]).then_inc(s_i, 1)
                            dve.wait_ge(s_a, 1)
                            nc.vector.tensor_tensor(sil[:], p_3[:], sil[:], ALU.mult).then_inc(s_m, 1)
                            dve.wait_ge(s_y, 1)
                            nc.vector.tensor_copy(ye[:], p_y[:]).then_inc(s_e, 1)
                    nc.all_engine_barrier()
                    for s in sems[first_sem:]:
                        nc.gpsimd.sem_clear(s)
                    nc.all_engine_barrier()


def finish(nc, S, x_dram, p_dram, w_ple, w_gate, y_dram, out_dram, R, rows, K):
    KP = PLE // P
    NB = 3
    with ExitStack() as ctx:
        sb = lambda name, shape, dt=F32: ctx.enter_context(nc.sbuf_tensor(name, shape, dt))
        wg = sb("fn_wg", [P, KT, D])
        wp = sb("fn_wp", [P, KP, D])
        xt = sb("fn_x", [P, NB, D])
        pt_ = sb("fn_p", [P, 2, PLE])
        pT = sb("fn_pT", [P, 2, KP, P])
        y = sb("fn_y", [P, NB, 2, D])
        xn = sb("fn_n", [P, D])
        xT = sb("fn_xT", [P, 2, KT, P])
        em = sb("fn_e", [P, 2, D])
        sg = sb("fn_s", [P, D])
        fo = sb("fn_o", [P, 2, D])
        sq = sb("fn_sq", [P, D])
        ss = sb("fn_ss", [P, 3, TT])
        rs = sb("fn_rs", [P, 3, TT])
        p_t = ctx.enter_context(nc.psum_tensor("fn_pt", [P, KT, P], F32))
        p_g = ctx.enter_context(nc.psum_tensor("fn_pg", [P, D], F32))
        p_e = ctx.enter_context(nc.psum_tensor("fn_pe", [P, D], F32))
        p_p = ctx.enter_context(nc.psum_tensor("fn_pp", [P, HALF], F32))
        s_w, s_wp = S("fn_w"), S("fn_wp")
        two = lambda n: [S(f"fn_{n}0"), S(f"fn_{n}1")]
        s_x, s_p, s_o = [S(f"fn_x{i}") for i in range(NB)], two("p"), two("o")
        s_y = [ctx.enter_context(nc.semaphore(f"fn_y{i}")) for i in range(NB)]
        (s_ad, s_sq, s_rs, s_n, s_t, s_r, s_g, s_sg, s_pt, s_pr, s_e, s_er, s_x5, s_f, s_c, s_pc) = (
            S("fn_" + n) for n in ("ad", "sq", "rs", "n", "t", "r", "g", "sg", "pt", "pr", "e", "er", "x5", "f", "c", "pc"))
        ident = K[:, K_ID:K_ID + P]
        norms = [k for t in range(TT + 1) for k in ([(0, t), (1, t)] if t < TT else []) + ([(2, t - 1)] if t else [])]
        squared, root_ready = Signal(s_sq, norms), Signal(s_rs, norms)
        with nc.Block() as block:
            @block.sync
            def _(sp):
                sp.dma_start(wp[:], w_ple).then_inc(s_wp, 16)
                for t in range(TT):
                    if t >= 2:
                        sp.wait_ge(s_pt, t - 1)
                    sp.dma_start(pt_[:, t % 2], p_dram[t * P:(t + 1) * P, :]).then_inc(s_p[t % 2], 16)
                    if t >= NB:
                        sp.wait_ge(s_f, t - NB + 1)
                    sp.dma_start(xt[:, t % NB], x_dram[t * P:(t + 1) * P, :]).then_inc(s_x[t % NB], 16)
                    if t == 0:
                        sp.dma_start(wg[:], w_gate).then_inc(s_w, 16)

            @block.gpsimd
            def _(pool):
                c = Chain(pool, s_pc)
                half_ = K[:, P:P + 1]

                def gather(t):
                    if t >= NB:
                        pool.wait_ge(s_ad, t - NB + 1)
                    for n in range(2):
                        nc.gpsimd.indirect_dma_start(y[:, t % NB, n, :], None, y_dram, bass.IndirectOffsetOnAxis(
                            ap=R["slots"][:, n, t:t + 1], axis=0)).then_inc(s_y[t % NB], 16)

                for t in range(NB):
                    gather(t)
                for n, t in norms:
                    squared.wait(pool, (n, t))
                    rsqrt_of_mean(nc, c, rs[:, n, t:t + 1], ss[:, n, t:t + 1], D, half_).then_inc(s_rs, 1)
                    if n == 1 and t + NB < TT:
                        gather(t + NB)

            @block.tensor
            def _(pe):
                def embed(t):
                    pe.wait_ge(s_p[t % 2], 16 * (t // 2 + 1))
                    if t:
                        pe.wait_ge(s_pr, t)
                    for k in range(KP):
                        last = nc.tensor.transpose(p_p[:, k * P:(k + 1) * P], pt_[:, t % 2, k * P:(k + 1) * P], ident)
                    last.then_inc(s_pt, 1)
                    pe.wait_ge(s_pr, t + 1)
                    if t == 0:
                        pe.wait_ge(s_wp, 16)
                    if t:
                        pe.wait_ge(s_er, t)
                    for k in range(KP):
                        for f in range(2):
                            last = nc.tensor.matmul(p_e[:, f * HALF:(f + 1) * HALF], pT[:, t % 2, k, :],
                                                    wp[:, k, f * HALF:(f + 1) * HALF], start=(k == 0), stop=(k == KP - 1))
                    last.then_inc(s_e, 1)

                embed(0)
                for t in range(TT):
                    pe.wait_ge(s_n, t + 1)
                    if t:
                        pe.wait_ge(s_r, t)
                    for k in range(KT):
                        last = nc.tensor.transpose(p_t[:, k, :], xn[:, k * P:(k + 1) * P], ident)
                    last.then_inc(s_t, 1)
                    if t + 1 < TT:
                        embed(t + 1)
                    pe.wait_ge(s_r, t + 1)
                    if t == 0:
                        pe.wait_ge(s_w, 16)
                    if t:
                        pe.wait_ge(s_sg, t)
                    for k in range(KT):
                        for f in range(2):
                            last = nc.tensor.matmul(p_g[:, f * HALF:(f + 1) * HALF], xT[:, t % 2, k, :],
                                                    wg[:, k, f * HALF:(f + 1) * HALF], start=(k == 0), stop=(k == KT - 1))
                    last.then_inc(s_g, 1)

            @block.scalar
            def _(act):
                def square(src, n, t):
                    if n + t:
                        act.wait_ge(s_sq, squared.order[n, t] - 1)
                    nc.scalar.activation(sq[:], src, ACT.Square, accum_out=ss[:, n, t:t + 1]).then_inc(s_sq, 1)

                def embed(t):
                    act.wait_ge(s_pt, t + 1)
                    if t >= 2:
                        act.wait_ge(s_e, t - 1)
                    nc.scalar.activation(pT[:, t % 2].rearrange("p k c -> p (k c)"), p_p[:, 0:PLE], ACT.Copy).then_inc(s_pr, 1)
                    act.wait_ge(s_e, t + 1)
                    square(p_e[:], 0, t)
                    act.wait_ge(s_ad, t + 1)
                    square(xt[:, t % NB], 1, t)

                def turned(t):
                    act.wait_ge(s_t, t + 1)
                    if t >= 2:
                        act.wait_ge(s_g, t - 1)
                    nc.scalar.activation(xT[:, t % 2], p_t[:], ACT.Copy).then_inc(s_r, 1)

                embed(0)
                turned(0)
                embed(1)
                for t in range(TT):
                    act.wait_ge(s_g, t + 1)
                    if t:
                        act.wait_ge(s_x5, t)
                    nc.scalar.activation(sg[:], p_g[:], ACT.Sigmoid).then_inc(s_sg, 1)
                    if t + 1 < TT:
                        turned(t + 1)
                    act.wait_ge(s_x5, t + 1)
                    square(xt[:, t % NB], 2, t)
                    act.wait_ge(s_f, t + 1)
                    act.dma_start(out_dram[t * P:(t + 1) * P, :], fo[:, t % 2]).then_inc(s_o[t % 2], 16)
                    if t + 2 < TT:
                        embed(t + 2)
                for j in range(2):
                    act.wait_ge(s_o[j], 16 * TT // 2)

            @block.vector
            def _(dve):
                c = Chain(dve, s_c)
                V = nc.vector

                def front(t):
                    x = xt[:, t % NB]
                    dve.wait_ge(s_x[t % NB], 16 * (t // NB + 1))
                    dve.wait_ge(s_y[t % NB], 32 * (t // NB + 1))
                    c.link(V.scalar_tensor_tensor(x, y[:, t % NB, 0], R["gates"][:, 0, t:t + 1], x, ALU.mult, ALU.add))
                    V.scalar_tensor_tensor(x, y[:, t % NB, 1], R["gates"][:, 1, t:t + 1], x, ALU.mult, ALU.add).then_inc(s_ad, 1)
                    root_ready.wait(dve, (0, t))
                    V.scalar_tensor_tensor(em[:, t % 2], p_e[:], rs[:, 0, t:t + 1], rows[:, R2_PROJ:R2_PROJ + D],
                                           ALU.mult, ALU.mult).then_inc(s_er, 1)
                    dve.wait_ge(s_ad, t + 1)
                    root_ready.wait(dve, (1, t))
                    if t:
                        dve.wait_ge(s_t, t)
                    V.scalar_tensor_tensor(xn[:], x, rs[:, 1, t:t + 1], rows[:, R2_PLE:R2_PLE + D],
                                           ALU.mult, ALU.mult).then_inc(s_n, 1)

                front(0)
                for t in range(TT):
                    if t + 1 < TT:
                        front(t + 1)
                    x = xt[:, t % NB]
                    dve.wait_ge(s_sg, t + 1)
                    dve.wait_ge(s_er, t + 1)
                    c.link(V.tensor_tensor(em[:, t % 2], em[:, t % 2], sg[:], ALU.mult))
                    V.tensor_tensor(x, x, em[:, t % 2], ALU.add).then_inc(s_x5, 1)
                    dve.wait_ge(s_x5, t + 1)
                    root_ready.wait(dve, (2, t))
                    if t >= 2:
                        dve.wait_ge(s_o[t % 2], 16 * (t // 2))
                    V.scalar_tensor_tensor(fo[:, t % 2], x, rs[:, 2, t:t + 1], rows[:, R2_FIN:R2_FIN + D],
                                           ALU.mult, ALU.mult).then_inc(s_f, 1)


def second_block(nc, d, x_dram, out):
    hf = nc.dram_tensor("hf", [SEQ, D], F32, kind="Internal").ap()
    x3 = nc.dram_tensor("x_mixed", [SEQ, D], F32, kind="Internal").ap()
    y_mix = nc.dram_tensor("mixed2", [KT, P, SEQ], F32, kind="Internal").ap()
    idx_dram = nc.dram_tensor("slot_tokens", [N_SLOTS, 1], F32, kind="Internal").ap()
    y_slots = nc.dram_tensor("slot_results", [N_SLOTS, D], F32, kind="Internal").ap()
    tile_of = lambda ap: (lambda t: ap[t * P:(t + 1) * P, :])
    with ExitStack() as ctx:
        sems = []

        def S(name):
            s = ctx.enter_context(nc.semaphore(name))
            sems.append(s)
            return s

        sb = lambda c, name, shape, dt=F32: c.enter_context(nc.sbuf_tensor(name, shape, dt))
        K2 = sb(ctx, "consts2", [P, K2_N])
        K = sb(ctx, "consts_b", [P, P + 1])
        R = {"slots": sb(ctx, "slots", [P, 2, TT], I32)[:], "gates": sb(ctx, "gates", [P, 2, TT])[:],
             "over": sb(ctx, "over", [P, 1 + N_OVER], I32)[:]}
        idx = sb(ctx, "slot_idx", [P, N_SLOTS // P], I32)
        cols = sb(ctx, "cols2", [P, C2_N])
        s_par = S("params2")
        minus_half = K[:, P:P + 1]
        zero = sb(ctx, "zero_row", [P, D])
        s_zero = S("zero_set")
        slot_rows = y_slots.rearrange("(b p) n -> b p n", p=P)

        def clear_extra(sp, sem):
            sp.dma_start(slot_rows[N_EXP:].rearrange("b p n -> p b n"),
                         zero[:].unsqueeze(1).broadcast_to([P, N_OVER, D])).then_inc(sem, 16)

        with nc.Block() as block:
            @block.sync
            def _(sp):
                sp.dma_start(K2[:], d["consts2"]).then_inc(s_par, 16)
                sp.dma_start(K[:], d["consts_b"]).then_inc(s_par, 16)
                sp.dma_start(cols[:], d["cols2"]).then_inc(s_par, 16)
                sp.wait_ge(s_par, 48)
                sp.wait_ge(s_zero, 1)

            @block.gpsimd
            def _(pool):
                nc.gpsimd.memset(zero[:], 0.0).then_inc(s_zero, 1)
        with ExitStack() as m:
            hT = sb(m, "hT2", [P, KT, SEQ])
            norm_transpose(nc, S, tile_of(x_dram), cols[:, C2_MIX:C2_MIX + 8], hT, K[:, K_ID:K_ID + P], minus_half, "b_")
            w = d["w_in_2"]
            mixer(nc, S, lambda off: w[:, off:off + P].rearrange("(k p) n -> p k n", p=P), d["wri"], hT, y_mix, K2, cols,
                  clear_extra)
        out_project(nc, S, y_mix, d["w_out_2"].rearrange("(k p) n -> p k n", p=P), tile_of(x_dram), tile_of(x3), None,
                    minus_half, "b_")
        with ExitStack() as m:
            rows = sb(m, "rows2", [P, R2_N])
            s_r = S("rows2_in")
            with nc.Block() as block:
                @block.sync
                def _(sp):
                    sp.dma_start(rows[:], d["rows2"].broadcast_to([P, R2_N])).then_inc(s_r, 16)
                    sp.wait_ge(s_r, 16)
            norm_route(nc, S, x3, hf, d["w_route"].rearrange("(k p) n -> p k n", p=P), rows, K, K2, R)
            token_lists(nc, S, R, K2[:, K2_TOK:K2_TOK + TT], idx_dram, idx, K)
        one = lambda w, e, split: w[bass.ds(e, 1)].rearrange("o (k p) n -> p (o k) n", p=P)
        w1 = lambda e: one(d["w1"], e, KT)
        w3 = lambda e: one(d["w3"], e, KT)
        w2 = lambda e: one(d["w2"], e, FT)
        slots = lambda b: slot_rows[bass.ds(b, 1)].rearrange("o p n -> p (o n)")
        experts(nc, S, w1, w3, w2, hf, slots, idx, K)
        extra_blocks(nc, S, sems, w1, w3, w2, hf, slots, idx, K, R["over"])
        with ExitStack() as m:
            rows = sb(m, "rows3", [P, R2_N])
            s_r = S("rows3_in")
            with nc.Block() as block:
                @block.sync
                def _(sp):
                    sp.dma_start(rows[:], d["rows2"].broadcast_to([P, R2_N])).then_inc(s_r, 16)
                    sp.wait_ge(s_r, 16)
            finish(nc, S, x3, d["p_2"], d["w_ple"].rearrange("(k p) n -> p k n", p=P),
                   d["w_gate"].rearrange("(k p) n -> p k n", p=P), y_slots, out, R, rows, K)
def constants():
    c = np.zeros((P, K_N), np.float32)
    i = np.arange(P)
    c[i, K_ID + i] = 1
    c[:, K_NH] = -0.5
    c[:, K_EPS] = EPS
    for j in range(P):
        if j % 64 < 32:
            c[j + 32, K_ROT + j] = -1
        else:
            c[j - 32, K_ROT + j] = 1
    for m in range(P):
        c[:, K_G0 + m] = i // 32 == m // 64
        c[:, K_G1 + m] = i // 32 == 2 + m // 64
        c[:, K_H + m] = i // 64 == m // 64
    for j in range(CPT):
        c[:, K_MASK + j] = i // CHUNK == j
        c[:, K_MASKB + j] = i // CHUNK == CPT - 1 - j
    inv = (np.float32(ROPE_THETA) ** (-np.arange(0, DIFF_HD, 2, dtype=np.float32) / np.float32(DIFF_HD))).astype(np.float32)
    ang = np.arange(SEQ, dtype=np.float32)[:, None] * inv[None, :]
    c[:, K_COS:K_COS + SEQ] = np.cos(ang).T[i % 32]
    c[:, K_SIN:K_SIN + SEQ] = np.sin(ang).T[i % 32]
    return c


def constants2():
    c = np.zeros((P, K2_N), np.float32)
    i = np.arange(P)
    c[:, K2_ONE:K2_ONE + P] = 1
    c[:, K2_MEAN:K2_MEAN + P] = 1.0 / D_CONV
    c[:, K2_TRI:K2_TRI + P] = i[:, None] < i[None, :]
    c[:, K2_REV:K2_REV + N_EXP] = N_EXP - np.arange(N_EXP)
    c[:, K2_REVG:K2_REVG + N_GROUPS] = N_GROUPS - np.arange(N_GROUPS)
    c[:, K2_E:K2_E + N_EXP] = np.arange(N_EXP)
    c[:, K2_O:K2_O + N_OVER] = np.arange(N_OVER)
    c[:, K2_TOK:K2_TOK + TT] = np.arange(TT) * P + i[:, None]
    c[:, K2_EPS] = EPS
    return c


def kernel(**inputs):
    import concourse.bacc as bacc
    from concourse.bass_utils import run_bass_kernel_spmd

    a = {k: np.asarray(v) for k, v in inputs.items()}
    wide = lambda v: np.ascontiguousarray(v.reshape(-1, P).T)
    per_layer, rows, wa2 = [], [], []
    for l in range(DEPTH):
        per_layer.append(np.concatenate([
            wide(a["norm_pre"][l]), wide(a["gla_ba_fwd"][l]), wide(a["gla_ba_bwd"][l]),
            wide(np.concatenate([a["gla_norm"][l]] * 2)), wide(np.concatenate([a["hgrn_norm"][l]] * 2)),
            wide(a["hgrn_lb_logits"][0]), wide(a["hgrn_lb_logits"][1]), np.full((P, 1), float(l), np.float32)], axis=1))
        li = 0.8 - 0.6 * math.exp(-0.3 * l)
        rows.append(np.concatenate([a["norm_post"][l], a["diff_norm"][l], a["diff_lq1"][l], a["diff_lk1"][l],
                                    a["diff_lq2"][l], a["diff_lk2"][l], np.array([li, 1.0 - li], np.float32)]))
        z = np.zeros((GLA_RANK, P), np.float32)
        wa2.append(np.concatenate([np.concatenate([a["gla_wa2_fwd"][l], z], 1),
                                   np.concatenate([z, a["gla_wa2_bwd"][l]], 1)], 0))
    given = {"x": a["x"], "w_in": a["w_in"], "w_out": a["w_out"], "cols": np.stack(per_layer), "rows": np.stack(rows),
             "wa2": np.stack(wa2), "consts": constants()}
    by_tap = lambda w: np.concatenate([wide(row) for row in w], axis=1)
    one = {k[:-2]: v[0] for k, v in a.items() if k.endswith("_2") and v.shape[0] == 1}
    given["cols2"] = np.concatenate([
        wide(one["g_mix"]), by_tap(one["conv_dw_w"]), wide(one["conv_dw_b"]), wide(one["conv_ln_g"]), wide(one["conv_ln_b"]),
        by_tap(one["lru_conv_w"]), wide(one["lru_conv_b"]), wide(one["lru_b_r"]), wide(one["lru_b_i"]),
        wide(one["lru_lambda"])], axis=1)
    wri = np.zeros((P, 2, CT, P), np.float32)
    for n, name in enumerate(("lru_w_r", "lru_w_i")):
        for h in range(2 * CT):
            wri[64 * (h % 2):64 * (h % 2) + 64, n, h // 2, 64 * (h % 2):64 * (h % 2) + 64] = one[name][h]
    given["wri"] = wri
    given["rows2"] = np.concatenate([one["g_ffn"], one["b_group"], one["b_expert"], one["g_ple"], one["g_ple_proj"],
                                     a["g_final_2"]])[None, :]
    given["w_route"] = np.concatenate([one["w_group"], one["w_expert"]], axis=1)
    given["consts2"] = constants2()
    given["consts_b"] = np.concatenate([given["consts"][:, :P], np.full((P, 1), -0.5, np.float32)], axis=1)
    given.update(w_in_2=one["w_in"], w_out_2=one["w_out"], w1=one["w1"], w3=one["w3"], w2=one["w2"], w_ple=one["w_ple"],
                 w_gate=one["w_ple_gate"], p_2=one["p"][0])
    given = {k: np.ascontiguousarray(v) for k, v in given.items()}
    nc = bacc.Bacc("TRN2", target_bir_lowering=False, num_devices=1)
    d = {k: nc.dram_tensor(f"in_{k}", v.shape, mybir.dt.from_np(v.dtype), kind="ExternalInput").ap() for k, v in given.items()}
    out = nc.dram_tensor("out_0", (1, SEQ, D), F32, kind="ExternalOutput").ap()
    x_all = bass_stack(nc, d, out)
    second_block(nc, d, x_all[DEPTH], out.rearrange("b s d -> (b s) d"))
    r = run_bass_kernel_spmd(nc, [{f"in_{k}": v for k, v in given.items()}], core_ids=[0])
    return r.results[0]["out_0"]
```
